# Optimizing a Trainium2 kernel written in Bass

```python
import math
import jax, jax.numpy as jnp
from jax import lax
import numpy as np

D_MODEL = 1024
BATCH = 1
SEQ = 1024
DEPTH = 1
DEC_BATCH = 1
DEC_SEQ = 256
PAST_LEN = 128

GRID_W = 64
CHUNK = 128
A_GROUPS = 4
A_WIDTH = 512
A_GC = A_WIDTH // A_GROUPS
POOL_WINDOWS = (2, 4, 8, 16)
B_WIDTH = 512
B_GC = B_WIDTH // len(POOL_WINDOWS)
N_HEADS = 8
N_KV_HEADS = 2
HEAD_DIM = 64
C_WIDTH = N_HEADS * HEAD_DIM
KV_WIDTH = N_KV_HEADS * HEAD_DIM
Q_BLOCK = 128
ROPE_THETA = 10000.0
ROPE_PAIRS_AXIS = HEAD_DIM // 4
D_WIDTH = 512
CONV_W = 3
N_BRANCHES = 4
A_COLS = 2 * A_WIDTH
B_COLS = B_WIDTH
C_COLS = C_WIDTH + 2 * KV_WIDTH
D_COLS = 3 * D_WIDTH
G_COLS = N_BRANCHES * D_MODEL
OFF_A = 0
OFF_B = OFF_A + A_COLS
OFF_C = OFF_B + B_COLS
OFF_D = OFF_C + C_COLS
OFF_G = OFF_D + D_COLS
N_IN = OFF_G + G_COLS
N_EXPERTS = 16
D_FF_EXPERT = 1024
EC_CAPACITY = 2
ALPHA = (2 * DEPTH) ** 0.25
BETA = (8 * DEPTH) ** -0.25
LN_EPS = 1e-5
RMS_EPS = 1e-6

kernel_name = 'hybrid_bidir_encoder_two_groups'

def _ln(x, g=None, b=None):
    x32 = x.astype(jnp.float32)
    xc = x32 - jnp.mean(x32, axis=-1, keepdims=True)
    y = xc * lax.rsqrt(jnp.mean(xc * xc, axis=-1, keepdims=True) + LN_EPS)
    if g is not None:
        y = y * g.astype(jnp.float32) + b.astype(jnp.float32)
    return y.astype(x.dtype)

def _rms(x, g):
    x32 = x.astype(jnp.float32)
    y = x32 * lax.rsqrt(jnp.mean(x32 * x32, axis=-1, keepdims=True) + RMS_EPS) * g.astype(jnp.float32)
    return y.astype(x.dtype)

def _axial_rope(T, dtype):
    n_rows = T // GRID_W
    row = jnp.repeat(jnp.arange(n_rows, dtype=jnp.float32), GRID_W)
    col = jnp.tile(jnp.arange(GRID_W, dtype=jnp.float32), n_rows)
    inv = ROPE_THETA ** (-jnp.arange(ROPE_PAIRS_AXIS, dtype=jnp.float32) / ROPE_PAIRS_AXIS)
    ang = jnp.concatenate([row[:, None] * inv, col[:, None] * inv], axis=-1)
    return jnp.cos(ang).astype(dtype), jnp.sin(ang).astype(dtype)

def _rope(x, cos, sin):
    xr = x.reshape(x.shape[:-1] + (HEAD_DIM // 2, 2))
    x0, x1 = xr[..., 0], xr[..., 1]
    c = cos[None, :, None, :]
    s = sin[None, :, None, :]
    return jnp.stack([x0 * c - x1 * s, x0 * s + x1 * c], axis=-1).reshape(x.shape)

def _spatial_gating(za, ln_g, ln_b, ws, bs):
    B, T, _ = za.shape
    za = jax.nn.gelu(za)
    u, v = za[..., :A_WIDTH], za[..., A_WIDTH:]
    v = _ln(v, ln_g, ln_b).reshape(B, T // CHUNK, CHUNK, A_GROUPS, A_GC)
    sv = jnp.einsum('gpq,bnqgc->bnpgc', ws, v) + bs.T[None, None, :, :, None]
    return u * sv.reshape(B, T, A_WIDTH)

def _multiscale_pool(zb, wg, scale):
    B, T, _ = zb.shape
    z32 = zb.astype(jnp.float32)
    cs = jnp.concatenate([jnp.zeros((B, 1, B_WIDTH), jnp.float32), jnp.cumsum(z32, axis=1)], axis=1)
    t = jnp.arange(T)
    outs = []
    for g, w in enumerate(POOL_WINDOWS):
        lo = jnp.clip(t - w // 2, 0, T)
        hi = jnp.clip(t + w // 2, 0, T)
        csg = cs[..., g * B_GC:(g + 1) * B_GC]
        s = jnp.take(csg, hi, axis=1) - jnp.take(csg, lo, axis=1)
        cnt = (hi - lo).astype(jnp.float32)[None, :, None]
        outs.append(s / cnt - z32[..., g * B_GC:(g + 1) * B_GC])
    pooled = jnp.stack(outs, axis=2).astype(zb.dtype)
    mixed = jnp.einsum('btgc,gcd->btgd', pooled, wg).reshape(B, T, B_WIDTH)
    return mixed * scale

def _attention(zc, q_g, k_g, cos, sin):
    B, T, _ = zc.shape
    q = zc[..., :C_WIDTH].reshape(B, T, N_HEADS, HEAD_DIM)
    k = zc[..., C_WIDTH:C_WIDTH + KV_WIDTH].reshape(B, T, N_KV_HEADS, HEAD_DIM)
    v = zc[..., C_WIDTH + KV_WIDTH:].reshape(B, T, N_KV_HEADS, HEAD_DIM)
    q = _rope(_rms(q, q_g), cos, sin)
    k = _rope(_rms(k, k_g), cos, sin)
    G = N_HEADS // N_KV_HEADS
    nb = T // Q_BLOCK
    qb = jnp.moveaxis(q.reshape(B, nb, Q_BLOCK, N_KV_HEADS, G, HEAD_DIM), 1, 0)
    scale = HEAD_DIM ** -0.5

    def block(qblk):
        s = jnp.einsum('bqkgd,bskd->bkgqs', qblk, k, preferred_element_type=jnp.float32) * scale
        p = jax.nn.softmax(s, axis=-1).astype(v.dtype)
        return jnp.einsum('bkgqs,bskd->bqkgd', p, v)

    o = lax.map(block, qb)
    return jnp.moveaxis(o, 0, 1).reshape(B, T, C_WIDTH)

def _short_conv(zd, conv_w):
    xd = zd[..., :D_WIDTH]
    bg = zd[..., D_WIDTH:2 * D_WIDTH]
    cg = zd[..., 2 * D_WIDTH:]
    z = cg * xd
    T = z.shape[1]
    pad = CONV_W // 2
    zp = jnp.pad(z, ((0, 0), (pad, pad), (0, 0)))
    y = zp[:, 0:T] * conv_w[0]
    for j in range(1, CONV_W):
        y = y + zp[:, j:j + T] * conv_w[j]
    return bg * y

def _expert_choice(h, r_w, r_b, w1, w3, w2):
    B, T, D = h.shape
    n_tok = B * T
    hf = h.reshape(n_tok, D)
    cap = EC_CAPACITY * n_tok // N_EXPERTS
    logits = jnp.dot(hf, r_w, preferred_element_type=jnp.float32) + r_b.astype(jnp.float32)
    aff = jax.nn.softmax(logits, axis=-1)
    gate, idx = lax.top_k(aff.T, cap)
    xg = hf[idx]
    a = jnp.einsum('ecd,edf->ecf', xg, w1)
    b = jnp.einsum('ecd,edf->ecf', xg, w3)
    out = jnp.einsum('ecf,efd->ecd', jax.nn.silu(a) * b, w2) * gate[..., None].astype(h.dtype)
    y = jnp.zeros_like(hf).at[idx.reshape(-1)].add(out.reshape(-1, D))
    return y.reshape(B, T, D)

def _trunk(x, c, w_ada, b_ada, w_in, a_ln_g, a_ln_b, a_ws, a_bs, b_wg, b_scale, c_q_g, c_k_g,
           d_conv, p_a, p_b, p_c, p_d, w_o, ln1_g, ln1_b, r_w, r_b, e_w1, e_w3, e_w2, ln2_g, ln2_b):
    B, T, _ = x.shape
    cos, sin = _axial_rope(T, x.dtype)
    for l in range(DEPTH):
        mod = (jnp.dot(jax.nn.silu(c), w_ada[l]) + b_ada[l])[:, None, :]
        sh1, sc1, g1, sh2, sc2, g2 = jnp.split(mod, 6, axis=-1)
        h = _ln(x) * (1 + sc1) + sh1
        z = jnp.dot(h, w_in[l])
        ya = _spatial_gating(z[..., OFF_A:OFF_B], a_ln_g[l], a_ln_b[l], a_ws[l], a_bs[l])
        yb = _multiscale_pool(z[..., OFF_B:OFF_C], b_wg[l], b_scale[l])
        yc = _attention(z[..., OFF_C:OFF_D], c_q_g[l], c_k_g[l], cos, sin)
        yd = _short_conv(z[..., OFF_D:OFF_G], d_conv[l])
        gates = jax.nn.sigmoid(z[..., OFF_G:].astype(jnp.float32)).astype(x.dtype)
        gates = gates.reshape(B, T, N_BRANCHES, D_MODEL)
        merged = (gates[:, :, 0] * jnp.dot(ya, p_a[l]) + gates[:, :, 1] * jnp.dot(yb, p_b[l])
                  + gates[:, :, 2] * jnp.dot(yc, p_c[l]) + gates[:, :, 3] * jnp.dot(yd, p_d[l]))
        y = jnp.dot(merged, w_o[l])
        x = _ln(ALPHA * x + g1 * y, ln1_g[l], ln1_b[l])
        h = _ln(x) * (1 + sc2) + sh2
        y = _expert_choice(h, r_w[l], r_b[l], e_w1[l], e_w3[l], e_w2[l])
        x = _ln(ALPHA * x + g2 * y, ln2_g[l], ln2_b[l])
    return x

def setup_inputs(seed: int = 0) -> dict:
    key = jax.random.key(seed)
    ks = iter(jax.random.split(key, 40))

    def nrm(shape, scale):
        return jax.random.normal(next(ks), shape, jnp.float32) * scale

    L, D, E, F = DEPTH, D_MODEL, N_EXPERTS, D_FF_EXPERT
    return {
        'x_prompt': nrm((BATCH, SEQ, D), 1.0),
        'x_sample': nrm((DEC_BATCH, DEC_SEQ, D), 1.0),
        'c_prompt': nrm((BATCH, D), 1.0),
        'c_sample': nrm((DEC_BATCH, D), 1.0),
        'w_ada': nrm((L, D, 6 * D), 0.5 * D ** -0.5),
        'b_ada': nrm((L, 6 * D), 0.02),
        'w_in': nrm((L, D, N_IN), D ** -0.5),
        'a_ln_g': 1.0 + nrm((L, A_WIDTH), 0.02),
        'a_ln_b': nrm((L, A_WIDTH), 0.02),
        'a_ws': nrm((L, A_GROUPS, CHUNK, CHUNK), CHUNK ** -0.5),
        'a_bs': 1.0 + nrm((L, A_GROUPS, CHUNK), 0.02),
        'b_wg': nrm((L, len(POOL_WINDOWS), B_GC, B_GC), B_GC ** -0.5),
        'b_scale': 1.0 + nrm((L, B_WIDTH), 0.02),
        'c_q_g': 1.0 + nrm((L, HEAD_DIM), 0.02),
        'c_k_g': 1.0 + nrm((L, HEAD_DIM), 0.02),
        'd_conv': nrm((L, CONV_W, D_WIDTH), CONV_W ** -0.5),
        'p_a': nrm((L, A_WIDTH, D), A_WIDTH ** -0.5),
        'p_b': nrm((L, B_WIDTH, D), B_WIDTH ** -0.5),
        'p_c': nrm((L, C_WIDTH, D), C_WIDTH ** -0.5),
        'p_d': nrm((L, D_WIDTH, D), D_WIDTH ** -0.5),
        'w_o': nrm((L, D, D), BETA * D ** -0.5),
        'ln1_g': 1.0 + nrm((L, D), 0.02),
        'ln1_b': nrm((L, D), 0.02),
        'r_w': nrm((L, D, E), D ** -0.5),
        'r_b': nrm((L, E), 0.01),
        'e_w1': nrm((L, E, D, F), D ** -0.5),
        'e_w3': nrm((L, E, D, F), D ** -0.5),
        'e_w2': nrm((L, E, F, D), BETA * F ** -0.5),
        'ln2_g': 1.0 + nrm((L, D), 0.02),
        'ln2_b': nrm((L, D), 0.02),
    }

def reference(x_prompt, x_sample, c_prompt, c_sample, w_ada, b_ada, w_in, a_ln_g, a_ln_b, a_ws, a_bs,
              b_wg, b_scale, c_q_g, c_k_g, d_conv, p_a, p_b, p_c, p_d, w_o, ln1_g, ln1_b, r_w, r_b,
              e_w1, e_w3, e_w2, ln2_g, ln2_b):
    y_prompt = _trunk(x_prompt, c_prompt, w_ada, b_ada, w_in, a_ln_g, a_ln_b, a_ws, a_bs, b_wg, b_scale,
                      c_q_g, c_k_g, d_conv, p_a, p_b, p_c, p_d, w_o, ln1_g, ln1_b, r_w, r_b,
                      e_w1, e_w3, e_w2, ln2_g, ln2_b)
    y_sample = _trunk(x_sample, c_sample, w_ada, b_ada, w_in, a_ln_g, a_ln_b, a_ws, a_bs, b_wg, b_scale,
                      c_q_g, c_k_g, d_conv, p_a, p_b, p_c, p_d, w_o, ln1_g, ln1_b, r_w, r_b,
                      e_w1, e_w3, e_w2, ln2_g, ln2_b)
    return (y_prompt, y_sample)


_drawn_inputs = setup_inputs


def setup_inputs(seed=0):
    import zlib

    import numpy as np

    out = dict(_drawn_inputs(seed))
    spreads = {}
    factors = {'b_ada': 4.297,
     'a_ln_g': 64.0,
     'a_ln_b': 64.0,
     'a_bs': 60.763,
     'b_scale': 50.0,
     'c_q_g': 48.327,
     'c_k_g': 48.604,
     'ln1_g': 7.636,
     'ln1_b': 7.703,
     'r_b': 64.0,
     'ln2_g': 7.608,
     'ln2_b': 8.024,
     'r_w': 4.212,
     'e_w1': 4.263,
     'e_w3': 3.973,
     'e_w2': 3.961}
    for name, (base, spread) in spreads.items():
        noise = np.random.default_rng([zlib.crc32(name.encode()), seed]).standard_normal(out[name].shape)
        drawn = base * np.exp(spread * noise) if base else spread * noise
        out[name] = __import__('jax').numpy.asarray(drawn.astype(out[name].dtype))
    for name, factor in factors.items():
        out[name] = (out[name] * factor).astype(out[name].dtype)
    return out
```

```python
import itertools
from contextlib import ExitStack

import numpy as np

import concourse.bass as bass
from concourse import mybir

F32 = mybir.dt.float32
U32 = mybir.dt.uint32
ALU = mybir.AluOpType
ACT = mybir.ActivationFunctionType
AX = mybir.AxisListType
ds = bass.ds

P = 128
T_PROMPT, T_SAMPLE = 1024, 256
T = T_PROMPT + T_SAMPLE
TILES = T // P
PAIRS = TILES // 2
PROMPT_PAIRS = T_PROMPT // P // 2
D = 1024
KD = D // P
W_BR = 512
KB = W_BR // P
HD = 64
N_Q, N_KV = 8, 2
N_QK = N_Q + N_KV
COL_U, COL_VG, COL_B = 0, 512, 1024
COL_C = 1536
COL_X, COL_BG, COL_CG = 2304, 2816, 3328
COL_G = 3840
WZ = 3 * 256 + 512
WINDOWS = (2, 4, 8, 16)
NE = 16
CAP_P, CAP_S = 2 * T_PROMPT // NE, 2 * T_SAMPLE // NE
CAP = CAP_P + CAP_S
ALPHA = 2.0 ** 0.25
LN_EPS = 1e-5
RMS_EPS = 1e-6
BLOCKS = ((0, 512), (512, 512), (1024, 256))
NEG = -3.0e38


def wait_apart(eng, sem, value, met, count):
    if not isinstance(value, int):
        value = eng.snap(value)
    eng.wait_ge(met, count)
    eng.wait_ge(sem, value)


class Chain:

    def __init__(self, eng, sem):
        self.eng, self.sem, self.n, self.base = eng, sem, 0, 0

    def did(self, instruction):
        instruction.then_inc(self.sem, 1)
        self.n += 1

    def settle(self):
        self.eng.wait_ge(self.sem, self.base + self.n)


    def enter(self, i, per_turn):
        self.before, self.per = self.n, per_turn
        self.base, self.n = self.before + i * per_turn, 0

    def leave(self, turns):
        assert self.n == self.per, self.n
        self.base, self.n = 0, self.before + turns * self.per


def build(nc, x, c, w_ada, b_ada, w_in, a_ln_g, a_ln_b, a_ws, a_bs, b_wg, b_scale, c_q_g, c_k_g,
          d_conv, p_all, w_o, ln1_g, ln1_b, r_w, r_b, e_w1, e_w3, e_w2, ln2_g, ln2_b,
          rope, inv_count, out):
    with ExitStack() as ctx:
        def sb(name, shape, dt=F32):
            return ctx.enter_context(nc.sbuf_tensor(name, shape, dt))

        def sem(name):
            return ctx.enter_context(nc.semaphore(name))

        h2_rows = nc.dram_tensor("h2_rows", (T, D), F32, kind="Internal").ap()
        x1_rows = nc.dram_tensor("x1_rows", (T, D), F32, kind="Internal").ap()
        mod_rows = nc.dram_tensor("mod_rows", (2, 4 * D), F32, kind="Internal").ap()
        y_rows = nc.dram_tensor("y_rows", (T, D), F32, kind="Internal").ap()

        ident = sb("ident", [P, P])
        rows_in = sb("rows_in", [P, P])
        colT = sb("colT", [P, 80])
        modT = sb("modT", [P, 16, 2])
        aff_t = sb("aff_t", [P, 2, 3, NE])
        rb_b = sb("rb_b", [P, NE])
        small = sb("small", [P, 64])
        half = sb("half", [P, 16])
        aff_t2 = sb("aff_t2", [P, 12])
        zero_col = sb("zero_col", [P, 1])
        carry = sb("carry", [P, 2])
        carried = sb("carried", [P, 16])

        R1 = sb("R1", [P, 20480])
        RQ = sb("RQ", [P, 8960])
        RV = sb("RV", [P, 5120])
        RY = sb("RY", [P, 5120])
        RW = sb("RW", [P, 3072])
        RT = sb("RT", [P, 7040])
        RC = sb("RC", [P, 2048])

        hT = R1[:, 0:10240].rearrange("p (k t) -> p k t", k=KD)
        merged = R1[:, 10240:20480].rearrange("p (k t) -> p k t", k=KD)
        wz = R1[:, 10240:20480].rearrange("p (k n) -> p k n", k=KD)
        w_ada_buf = [RV[:, 0:4096].rearrange("p (k n) -> p k n", k=KD),
                     RY[:, 0:4096].rearrange("p (k n) -> p k n", k=KD)]
        qT = RQ[:, 0:5120].rearrange("p (j t) -> p j t", j=4)
        kT = RQ[:, 5120:7680].rearrange("p (j t) -> p j t", j=2)
        va = RQ[:, 7680:8960].rearrange("p (t n) -> p t n", n=P)
        vln = RV[:, :].rearrange("p (t n) -> p t n", n=W_BR)
        y1 = RV[:, :].rearrange("p (k t) -> p k t", k=KB)
        y0 = RY[:, :].rearrange("p (k t) -> p k t", k=KB)
        w_tile = [RW[:, 1024 * s:1024 * s + 1024].rearrange("p (k n) -> p k n", k=KD) for s in range(2)]
        p_tile = [RW[:, 2048 + 512 * s:2560 + 512 * s].rearrange("p (k n) -> p k n", k=KB) for s in range(2)]
        x_in = [RY[:, 1024 * s:1024 * s + 1024] for s in range(2)]
        xh = [RY[:, 2048 + 1024 * s:3072 + 1024 * s] for s in range(2)]
        h_tile = [RW[:, 1024 * s:1024 * s + 1024].rearrange("p (k n) -> p k n", k=KD) for s in range(2)]
        v_gelu = [RW[:, 2048 + 512 * s:2560 + 512 * s] for s in range(2)]
        z_qkv = [RT[:, 768 * s:768 * s + 768] for s in range(2)]
        qk_out = [RT[:, 1536 + 768 * s:2304 + 768 * s] for s in range(2)]
        r_sq = RT[:, 3072:3712]
        r_n = RT[:, 3712:4352]
        r_a = RT[:, 4352:4672]
        r_b2 = RT[:, 4672:4992]
        gqk = RC[:, 0:640]
        cossin = RC[:, 640:1280].rearrange("p (t a n) -> p t a n", t=TILES, a=2)
        bs_b = RT[:, 6016:6528]
        lng_b = RT[:, 4992:5504]
        lnb_b = RT[:, 5504:6016]
        wsT = RC[:, 1280:1792].rearrange("p (g n) -> p g n", g=4)
        ws_in = RT[:, 6528:7040].rearrange("p (g n) -> p g n", g=4)

        PS = ctx.enter_context(nc.psum_tensor("PS", [P, 8, 512], F32))
        tp = [PS[:, 0:2, :].rearrange("p a (b n) -> p (a b) n", n=P),
              PS[:, 2:4, :].rearrange("p a (b n) -> p (a b) n", n=P)]
        z1, z2, z3 = PS[:, 4, :], PS[:, 5, 0:256], PS[:, 6, :]
        rows_ps = PS[:, 7, 0:80]
        mod_ps = PS[:, 6, 0:32].rearrange("p (m g) -> p m g", g=2)
        ws_ps = PS[:, 4, :].rearrange("p (g n) -> p g n", g=4)

        res = [PS[:, 3 * r:3 * r + 3, :].rearrange("p a n -> p (a n)")[:, 0:T] for r in range(2)]
        sv_ps = [PS[:, 6 + s, :].rearrange("p (g n) -> p g n", g=4) for s in range(2)]
        PADDED = T + 32
        SEGS = ((8, 0, T_PROMPT), (T_PROMPT + 24, T_PROMPT, T_SAMPLE))
        z_pad = [RT[:, PADDED * s:PADDED * (s + 1)] for s in range(2)]
        sum_a, sum_b = (RT[:, PADDED * s:PADDED * (s + 1)] for s in (2, 3))
        gate_sb = RT[:, 5248:5248 + T]
        prod = RT[:, 0:T]
        CSEGS = ((1, 0, T_PROMPT), (T_PROMPT + 3, T_PROMPT, T_SAMPLE))
        cg_sb = RT[:, 1312:1312 + T]
        z_conv = RT[:, 2624:2624 + T + 4]
        taps = RT[:, 3936:3936 + T + 4]
        wg_sb = RC[:, 0:512].rearrange("p (g n) -> p g n", g=4)
        edge = RC[:, 1792:1920].rearrange("p (g e n) -> p g e n", g=4, e=4)
        s_ps = [PS[:, 2 * u:2 * u + 2, :].rearrange("p a n -> p (a n)") for u in range(2)]
        pt_ps = PS[:, 4:6, :].rearrange("p a (b n) -> p (a b) n", n=P)
        o_ps = [PS[:, 6 + u, 0:P] for u in range(2)]
        prob = [RT[:, 1024 * u:1024 * u + 1024] for u in range(2)]
        probT = [RT[:, 2048 + 1024 * u:3072 + 1024 * u].rearrange("p (b n) -> p b n", n=P) for u in range(2)]
        q_tile = RT[:, 4096:4608].rearrange("p (j n) -> p j n", j=4)

        w_mod = [R1[:, 4096 * s:4096 * s + 4096].rearrange("p (k n) -> p k n", k=KD) for s in range(2)]
        c_pad = RT[:, 6528:7040].rearrange("p (k n) -> p k n", k=KD)
        b_row = RT[:, 0:4096]
        m_row = [RT[:, 4096 + 512 * s:4608 + 512 * s] for s in range(2)]
        mod_row_ps = [PS[:, 6 + s, :] for s in range(2)]
        row = lambda region, i: region[:, D * i:D * i + D]
        g1_b, sc2_b, sh2_b = [row(RV, 0), row(RV, 1)], [row(RV, 2), row(RV, 3)], [row(RV, 4), row(RY, 0)]
        ln1g_b, ln1b_b = row(RY, 1), row(RY, 2)
        g2_b = [row(RY, 3), row(RY, 4)]
        x_row = [row(R1, s) for s in range(2)]
        x1_row = [row(R1, 2 + s) for s in range(2)]
        h2_row = [row(R1, 4 + s) for s in range(2)]
        h2T = [row(R1, 6 + s).rearrange("p (k n) -> p k n", k=KD) for s in range(2)]
        m_tile = [row(R1, 8 + s).rearrange("p (k n) -> p k n", k=KD) for s in range(2)]
        wo_sb = RQ[:, 0:8192].rearrange("p (k n) -> p k n", k=KD)
        rw_sb = RQ[:, 8192:8320].rearrange("p (k n) -> p k n", k=KD)
        zeros = RW[:, 0:D]
        affT = RT[0:NE, 0:T]
        y_ps = [PS[:, 2 * s:2 * s + 2, :].rearrange("p a n -> p (a n)") for s in range(2)]
        h2t_ps = PS[:, 4:6, :].rearrange("p a (b n) -> p (a b) n", n=P)
        logit_ps = PS[:, 6, 0:NE]
        affT_ps = PS[0:NE, 7, 0:P]
        top_v, top_f = RT[0:NE, 1280:1440], RT[0:NE, 1440:1600]
        top_i = sb("top_i", [NE, CAP], U32)
        idx_p, idx_s = sb("idx_p", [P, NE], U32), sb("idx_s", [CAP_S, NE], U32)
        gate_p, gate_s = sb("gate_p", [P, NE]), sb("gate_s", [CAP_S, NE])
        g_idx_p, g_idx_s = sb("g_idx_p", [P, 1], U32), sb("g_idx_s", [CAP_S, 1], U32)
        s_idx_p, s_idx_s = sb("s_idx_p", [P, 1], U32), sb("s_idx_s", [CAP_S, 1], U32)
        top_ps = PS[:, 7, 0:4 * NE].rearrange("p (a n) -> p a n", a=4)
        w_half = [R1[:, 4096 * c:4096 * c + 4096].rearrange("p (k n) -> p k n", k=KD) for c in range(5)]
        w_half.append(RV[:, 0:4096].rearrange("p (k n) -> p k n", k=KD))
        xg_p, xg_s = RQ[:, 0:D], RQ[0:CAP_S, D:2 * D]
        xgT, gT, outT = (RQ[:, 2048 + 1280 * i:3328 + 1280 * i].rearrange("p (k n) -> p k n", k=KD) for i in range(3))
        out_p, out_s = RQ[:, 5888:6912], RQ[0:CAP_S, 6912:7936]
        silu = [RQ[:, 7936 + CAP * s:7936 + CAP * (s + 1)] for s in range(2)]
        xt_p = PS[:, 0:2, :].rearrange("p a (b n) -> p (a b) n", n=P)
        xt_s = PS[:, 2, 0:KD * CAP_S].rearrange("p (k n) -> p k n", k=KD)
        ab_ps = [PS[:, 3 + s, 0:2 * CAP].rearrange("p (a n) -> p a n", a=2) for s in range(2)]
        op_ps = PS[:, 5:7, :].rearrange("p a n -> p (a n)")
        os_ps = [PS[0:CAP_S, 7, :], PS[0:CAP_S, 2, :]]
        ln2g_b, ln2b_b = row(RY, 0), row(RY, 1)
        x1_in = [row(RT, s) for s in range(2)]
        y_in = [row(RT, 2 + s) for s in range(2)]

        s_cpad, s_brow, s_modr, s_mrow, s_mout = (sem(n) for n in ("s_cpad", "s_brow", "s_modr", "s_mrow", "s_mout"))
        s_wm = [sem("s_wm0"), sem("s_wm1")]
        s_rows2, s_wo, s_zero, s_y0 = (sem(n) for n in ("s_rows2", "s_wo", "s_zero", "s_y0"))
        s_xr = [sem("s_xr0"), sem("s_xr1")]
        s_x1o, s_h2o = [sem("s_x1o0"), sem("s_x1o1")], [sem("s_h2o0"), sem("s_h2o1")]
        s_mt, s_y, s_yr, s_xa, s_st2, s_rs2, s_ln, s_x1, s_h2 = (
            sem(n) for n in ("s_mt", "s_y", "s_yr", "s_xa", "s_st2", "s_rs2", "s_ln", "s_x1", "s_h2"))
        s_et, s_h2T, s_lg, s_sm, s_se, s_aff, s_at, s_affT = (
            sem(n) for n in ("s_et", "s_h2T", "s_lg", "s_sm", "s_se", "s_aff", "s_at", "s_affT"))
        s_top, s_topT, s_idx = sem("s_top"), sem("s_topT"), sem("s_idx")
        s_wx = [sem(f"s_wx{c}") for c in range(6)]
        s_xg, s_xt, s_xe, s_xes, s_ab, s_si, s_g, s_o, s_oT, s_ot, s_op, s_os, s_sc = (
            sem(n) for n in ("s_xg", "s_xt", "s_xe", "s_xes", "s_ab", "s_si", "s_g", "s_o", "s_oT", "s_ot", "s_op", "s_os", "s_sc"))
        s_fx = [sem("s_fx0"), sem("s_fx1")]
        s_st3, s_rs3, s_fn, s_fo, s_ln2 = sem("s_st3"), sem("s_rs3"), sem("s_fn"), sem("s_fo"), sem("s_ln2")
        s_done = [sem("s_done0"), sem("s_done1")]

        s_w, s_p = [sem("s_w0"), sem("s_w1")], [sem("s_p0"), sem("s_p1")]
        s_f, s_fe = [sem("s_f0"), sem("s_f1")], [sem("s_fe0"), sem("s_fe1")]
        s_sv, s_sve, s_ya = sem("s_sv"), sem("s_sve"), sem("s_ya")
        s_pool, s_mg, s_pads = (sem(n) for n in ("s_pool", "s_mg", "s_pads"))
        s_wg = sem("s_wg")
        s_qb, s_qk, s_mx, s_exp, s_pn, s_pt, s_pte, s_pv, s_oe = (
            sem(n) for n in ("s_qb", "s_qk", "s_mx", "s_exp", "s_pn", "s_pt", "s_pte", "s_pv", "s_oe"))

        N_U, N_B, N_MA, N_D, N_MB, N_MD, N_MC = 0, 4, 8, 16, 28, 36, 44
        R_U, R_B, R_MA, R_MIX, R_D, R_MB, R_MD, R_MC, R_END = 0, 4, 8, 24, 28, 40, 56, 72, 88
        MERGES = {"A": (N_MA, R_MA, 0, 0, y0), "B": (N_MB, R_MB, 1, 8, y1),
                  "D": (N_MD, R_MD, 3, 16, y0), "C": (N_MC, R_MC, 2, 24, y1)}

        s_id0, s_id = sem("s_id0"), sem("s_id")
        s_rows, s_silu, s_rT, s_col = sem("s_rows"), sem("s_silu"), sem("s_rT"), sem("s_col")
        s_wada = [sem("s_wada0"), sem("s_wada1")]
        s_modmm, s_mod = sem("s_modmm"), sem("s_mod")
        s_const = sem("s_const")
        s_wz = sem("s_wz")
        s_gqk = sem("s_gqk")
        s_ws, s_wsT = sem("s_ws"), sem("s_wsT")
        s_x = [sem("s_xin0"), sem("s_xin1")]
        s_stat, s_rs, s_xh, s_tp, s_ht, s_hc = (sem(n) for n in ("s_stat", "s_rs", "s_xh", "s_tp", "s_ht", "s_hc"))
        s_z1, s_z2, s_z3, s_zc, s_vg = (sem(n) for n in ("s_z1", "s_z2", "s_z3", "s_zc", "s_vg"))
        s_qr, s_vn, s_vl, s_qt, s_qe = (sem(n) for n in ("s_qr", "s_vn", "s_vl", "s_qt", "s_qe"))
        own_v, own_p, own_a = sem("own_v"), sem("own_p"), sem("own_a")
        s_out = sem("s_out")
        block = ctx.enter_context(nc.Block())

        def ln_cols(which, s):
            return small[:, 16 * which + 8 * s:16 * which + 8 * s + 8]

        @block.sync
        def _(sp):
            sp.dma_start(rows_in[0:16, :], c.rearrange("g (k n) -> (g k) n", n=P)).then_inc(s_rows, 16)
            sp.dma_start(rows_in[16:64, :], b_ada.rearrange("(k n) -> k n", n=P)).then_inc(s_rows, 16)
            sp.dma_start(rows_in[64:76, :], d_conv.rearrange("j (k n) -> (j k) n", n=P)).then_inc(s_rows, 16)
            sp.dma_start(rows_in[76:80, :], b_scale.rearrange("(k n) -> k n", n=P)).then_inc(s_rows, 16)
            for m in range(4):
                if m >= 2:
                    sp.wait_ge(s_modmm, m - 1)
                sp.dma_start(w_ada_buf[m % 2], w_ada[:, 512 * m:512 * m + 512].rearrange("(k p) n -> p k n", p=P)) \
                  .then_inc(s_wada[m % 2], 16)
            sp.dma_start(wz[:, :, 0:768], w_in[:, COL_C:COL_C + 768].rearrange("(k p) n -> p k n", p=P)).then_inc(s_wz, 16)
            sp.dma_start(wz[:, :, 768:1280], w_in[:, COL_VG:COL_VG + 512].rearrange("(k p) n -> p k n", p=P)).then_inc(s_wz, 16)
            sp.dma_start(ws_in, a_ws.rearrange("g p q -> p g q")).then_inc(s_ws, 16)
            sp.wait_ge(s_modmm, 4)
            for t in range(2):
                sp.dma_start(x_in[t], x[t * P:(t + 1) * P, :]).then_inc(s_x[t], 16)
            with sp.Fori(1, PAIRS) as i:
                for s in range(2):
                    sp.wait_ge(s_xh, 2 * i + s - 1)
                    sp.dma_start(x_in[s], x[ds(i * 256 + s * P, P), :]).then_inc(s_x[s], 16)

            def load_w(slot, cols, r_before, count=None):
                if r_before is not None:
                    sp.wait_ge(s_f[r_before % 2], r_before // 2 + 1 if count is None else count)
                sp.dma_start(w_tile[slot], w_in[:, ds(cols, P)].rearrange("(k p) n -> p k n", p=P)).then_inc(s_w[slot], 16)

            sp.wait_ge(s_z3, TILES)
            sp.wait_ge(s_hc, TILES)
            sp.wait_ge(s_vn, TILES)
            sp.wait_ge(s_qr, TILES)
            sp.dma_start(wg_sb, b_wg.rearrange("g c d -> c g d")).then_inc(s_wg, 16)
            for j in range(4):
                load_w(j % 2, COL_U + P * j, j - 2 if j >= 2 else None)
            for j in range(4):
                load_w(j % 2, COL_B + P * j, R_B + j - 2)

            def load_merge(name, r_last):
                n0, r0, branch, m0, _ = MERGES[name]

                def turn(i, first):
                    for s in range(2):
                        col = COL_G + branch * D + s * P
                        load_w(s, col + i * 256, r_last[s] if first else 0, None if first else r0 // 2 + 2 * i + s - 1)
                        if not first:
                            wait_apart(sp, s_f[1], r0 // 2 + 2 * i + s - 1, s_wg, 16)
                        elif m0:
                            sp.wait_ge(s_f[1], r_proj + s)
                        sp.dma_start(p_tile[s], p_all[branch, :, ds(i * 256 + s * P, P)].rearrange("(k p) n -> p k n", p=P)) \
                          .then_inc(s_p[s], 16)

                r_proj = {"A": 0, "B": R_MA // 2 + 7, "D": R_MB // 2 + 7, "C": R_MD // 2 + 7}[name]
                turn(0, True)
                with sp.Fori(1, 4) as i:
                    turn(i, False)

            load_merge("A", (R_B + 2, R_B + 3))
            for j in range(4):
                for m, col in enumerate((COL_CG, COL_X, COL_BG)):
                    n = 3 * j + m
                    load_w(n % 2, col + P * j, R_MA + 12 + 2 * n if n < 2 else R_D + n - 2)
            load_merge("B", (R_D + 10, R_D + 11))
            load_merge("D", (R_MB + 12, R_MB + 14))
            load_merge("C", (R_MD + 12, R_MD + 14))

            sp.wait_ge(s_f[0], R_END // 2)
            sp.wait_ge(s_f[1], R_END // 2)
            sp.wait_ge(s_mg, 24)
            sp.dma_start(wo_sb, w_o.rearrange("(k p) n -> p k n", p=P)).then_inc(s_wo, 16)

            def store_mod(m):
                sp.wait_ge(s_mrow, 2 * m + 2)
                for g in range(2):
                    sp.dma_start(mod_rows[g:g + 1, 512 * m:512 * m + 512], m_row[m % 2][32 * g:32 * g + 1, :]).then_inc(s_mout, 16)

            for r in (0, 32):
                sp.dma_start(b_row[r:r + 1, :], b_ada[2 * D:6 * D].rearrange("(a n) -> a n", a=1)).then_inc(s_brow, 16)
            for m in range(8):
                if m >= 2:
                    sp.wait_ge(s_modr, m - 1)
                    store_mod(m - 2)
                at = 2 * D + 512 * m
                sp.dma_start(w_mod[m % 2], w_ada[:, at:at + 512].rearrange("(k p) n -> p k n", p=P)).then_inc(s_wm[m % 2], 16)
            sp.dma_start(rw_sb, r_w.rearrange("(k p) n -> p k n", p=P)).then_inc(s_wo, 16)
            sp.wait_ge(s_zero, 1)
            sp.dma_start(y_rows.rearrange("(t p) d -> p t d", p=P), zeros.unsqueeze(1).to_broadcast([P, TILES, D])) \
              .then_inc(s_y0, 16)
            sp.wait_ge(s_modr, 8)
            for s in range(2):
                sp.dma_start(x_row[s], x[s * P:(s + 1) * P, :]).then_inc(s_xr[s], 16)

            for m in (6, 7):
                store_mod(m)
            sp.wait_ge(s_mout, 16 * 16)

            def everywhere(dst, src):
                return sp.dma_start(dst, src.rearrange("(a n) -> a n", a=1).to_broadcast([P, D]))

            for g in range(2):
                for j, dst in enumerate((g1_b, sh2_b, sc2_b, g2_b)):
                    everywhere(dst[g], mod_rows[g, D * j:D * j + D]).then_inc(s_rows2, 16)
            everywhere(ln1g_b, ln1_g).then_inc(s_rows2, 16)
            everywhere(ln1b_b, ln1_b).then_inc(s_rows2, 16)

            def rows_turn(i, more):
                for s in range(2):
                    t = 2 * i + s
                    at = sp.snap(256 * i + P * s) if not isinstance(i, int) else 256 * i + P * s
                    sp.wait_ge(s_x1, t + 1)
                    sp.dma_start(x1_rows[ds(at, P), :], x1_row[s]).then_inc(s_x1o[s], 16)
                    sp.wait_ge(s_h2, t + 1)
                    sp.dma_start(h2_rows[ds(at, P), :], h2_row[s]).then_inc(s_h2o[s], 16)
                    if more:
                        sp.wait_ge(s_xa, t + 1)
                        sp.dma_start(x_row[s], x[ds(at + 256, P), :]).then_inc(s_xr[s], 16)

            with sp.Fori(0, PAIRS - 1) as i:
                rows_turn(i, True)
            rows_turn(PAIRS - 1, False)

            HALVES = ((e_w1, 0), (e_w3, 0), (e_w1, 512), (e_w3, 512), (e_w2, 0), (e_w2, 512))

            def load_expert(e, first):
                for c, (w, lo) in enumerate(HALVES):
                    if not first:
                        done, n = ((s_ab, 4), (s_ab, 4), (s_ab, 8), (s_ab, 8), (s_o, 4), (s_o, 8))[c]
                        sp.wait_ge(done, 8 * e - 8 + n)
                    sp.dma_start(w_half[c], w[ds(e, 1), :, lo:lo + 512].rearrange("a (k p) n -> p (a k) n", p=P)) \
                      .then_inc(s_wx[c], 16)

            sp.wait_ge(s_aff, TILES)
            sp.wait_ge(s_at, TILES)
            for s in range(2):
                sp.wait_ge(s_x1o[s], 16 * PAIRS)
                sp.wait_ge(s_h2o[s], 16 * PAIRS)
            everywhere(ln2g_b, ln2_g).then_inc(s_ln2, 16)
            everywhere(ln2b_b, ln2_b).then_inc(s_ln2, 16)
            load_expert(0, True)
            with sp.Fori(1, NE) as e:
                load_expert(e, False)

            def load_last(i, s, first):
                at = sp.snap(256 * i + P * s) if not isinstance(i, int) else 256 * i + P * s
                if not first:
                    sp.wait_ge(s_done[s], 16 * i)
                sp.dma_start(x1_in[s], x1_rows[ds(at, P), :]).then_inc(s_fx[s], 16)
                sp.dma_start(y_in[s], y_rows[ds(at, P), :]).then_inc(s_fx[s], 16)

            sp.wait_ge(s_sc, 32 * NE)
            for s in range(2):
                load_last(0, s, True)

            def store_last(i, more):
                for s in range(2):
                    t = 2 * i + s
                    at = sp.snap(256 * i + P * s) if not isinstance(i, int) else 256 * i + P * s
                    sp.wait_ge(s_fo, t + 1)
                    sp.dma_start(out[ds(at, P), :], y_in[s]).then_inc(s_done[s], 16)
                    if more:
                        load_last(i + 1, s, False)

            with sp.Fori(0, PAIRS - 1) as i:
                store_last(i, True)
            store_last(PAIRS - 1, False)
            for s in range(2):
                sp.wait_ge(s_done[s], 16 * PAIRS)

        @block.gpsimd
        def _(pool):
            own = Chain(pool, own_p)
            columns = itertools.cycle(range(16))

            def carrier():
                at = next(columns)
                own.did(pool.tensor_tensor(carried[:, at:at + 1], half[:, 0:1], half[:, 1:2], ALU.add))

            pool.memset(ident[:, :], 0.0).then_inc(s_id0, 1)
            own.did(pool.memset(half[:, :], -0.5))
            pool.wait_ge(s_id0, 1)
            pool.affine_select(out=ident[:, :], in_=ident[:, :], compare_op=ALU.not_equal, fill=1.0,
                               base=0, pattern=[[-1, P]], channel_multiplier=1).then_inc(s_id, 1)
            pool.dma_start(cossin, rope).then_inc(s_const, 16)
            pool.dma_start(gqk[:, 0:HD], c_q_g.rearrange("(a n) -> a n", a=1).to_broadcast([P, HD])).then_inc(s_const, 16)
            pool.dma_start(gqk[:, 512:512 + HD], c_k_g.rearrange("(a n) -> a n", a=1).to_broadcast([P, HD])).then_inc(s_const, 16)
            pool.dma_start(lng_b, a_ln_g.rearrange("(a n) -> a n", a=1).to_broadcast([P, W_BR])).then_inc(s_const, 16)
            pool.dma_start(lnb_b, a_ln_b.rearrange("(a n) -> a n", a=1).to_broadcast([P, W_BR])).then_inc(s_const, 16)
            pool.dma_start(bs_b, a_bs.rearrange("g p -> (g p)").rearrange("(a n) -> a n", a=1).to_broadcast([P, W_BR])).then_inc(s_const, 16)
            pool.dma_start(rb_b[:, :], r_b.rearrange("(a n) -> a n", a=1).to_broadcast([P, NE])).then_inc(s_const, 16)
            pool.dma_start(edge, inv_count.rearrange("g e n -> (g e n)").rearrange("(a n) -> a n", a=1).to_broadcast([P, 128])).then_inc(s_const, 16)
            pool.wait_ge(s_const, 8 * 16)
            for h in range(1, N_Q):
                own.did(pool.tensor_copy(gqk[:, h * HD:(h + 1) * HD], gqk[:, 0:HD]))
            pool.tensor_copy(gqk[:, 576:640], gqk[:, 512:576]).then_inc(s_gqk, 1)
            own.settle()

            def power(cols, n, t_sem, count):
                pool.wait_ge(t_sem, count)
                pool.tensor_tensor(cols, cols, half[:, 0:n], ALU.pow).then_inc(s_rs, 1)

            def turn(i, ahead, front=False):
                for s in range(2):
                    t = 2 * i + s
                    n0 = 3 * t + 2
                    power(small[:, 32 + 16 * s:42 + 16 * s], N_QK, s_stat, n0 + 1 if ahead else 3 * t + 3 - s)
                    if ahead:
                        power(ln_cols(0, s)[:, 7:8], 1, s_stat, n0 + 2)
                    pool.wait_ge(s_ht, t + 1)
                    pool.tensor_copy(hT[:, :, ds(i * 256 + s * P, P)], h_tile[s]).then_inc(s_hc, 1)
                    power(ln_cols(1, s)[:, 7:8], 1, s_stat, n0 + 3 if ahead else 3 * t + 4 - s)
                    pool.wait_ge(s_vn, t + 1)
                    carrier()
                    v = vln[:, ds(t, 1), :].rearrange("p a n -> p (a n)")
                    own.did(pool.tensor_tensor(v, v, lng_b, ALU.mult))
                    own.settle()
                    carrier()
                    pool.tensor_tensor(v, v, lnb_b, ALU.add).then_inc(s_vl, 1)

            power(ln_cols(0, 0)[:, 7:8], 1, s_stat, 1)
            power(ln_cols(0, 1)[:, 7:8], 1, s_stat, 2)
            with pool.Fori(0, PAIRS - 1) as i:
                own.enter(i, 6)
                turn(i, True)
                own.leave(PAIRS - 1)
            turn(PAIRS - 1, False)
            pool.wait_ge(s_f[0], R_MC // 2)
            pool.wait_ge(s_f[1], R_MC // 2)
            pool.wait_ge(s_mg, 16)
            pool.tensor_copy(q_tile, qT[:, :, 0:P]).then_inc(s_qb, 1)
            with pool.Fori(1, TILES) as t:
                pool.wait_ge(s_mg, 16)
                pool.wait_ge(s_qk, N_Q * t)
                pool.tensor_copy(q_tile, qT[:, :, ds(t * P, P)]).then_inc(s_qb, 1)
            pool.wait_ge(s_f[0], R_END // 2)
            own.did(pool.memset(zeros, 0.0))
            own.settle()
            pool.tensor_copy(carry[:, 1:2], zeros[:, 0:1]).then_inc(s_zero, 1)

            def power2(s_stat_, s_rs_, cols, count):
                pool.wait_ge(s_stat_, count)
                pool.tensor_tensor(cols[:, 7:8], cols[:, 7:8], half[:, 0:1], ALU.pow).then_inc(s_rs_, 1)

            def take(i, s):
                carrier()
                pool.tensor_copy(m_tile[s], merged[:, :, ds(256 * i + P * s, P)]).then_inc(s_mt, 1)

            pool.wait_ge(s_mg, 24)
            pool.wait_ge(s_f[0], R_END // 2)
            pool.wait_ge(s_modr, 8)
            for s in range(2):
                take(0, s)
            pool.wait_ge(s_rows2, 16 * 10)

            def rows_turn(i, grp, more):
                for s in range(2):
                    t = 2 * i + s
                    power2(s_st2, s_rs2, ln_cols(1, s), 2 * t + 1)
                    for gain, offset, n, done in ((ln1g_b, ln1b_b, 1, s_x1), (sc2_b[grp], sh2_b[grp], 2, s_h2)):
                        r = x1_row[s] if n == 1 else h2_row[s]
                        if n == 2:
                            power2(s_st2, s_rs2, ln_cols(2, s), 2 * t + 2)
                        pool.wait_ge(s_ln, 2 * t + n)
                        own.did(pool.tensor_tensor(r, r, gain, ALU.mult))
                        own.settle()
                        pool.tensor_tensor(r, r, offset, ALU.add).then_inc(done, 1)
                    if more:
                        pool.wait_ge(s_y, t + 1)
                        take(i + 1, s)

            with pool.Fori(0, PROMPT_PAIRS) as i:
                own.enter(i, 6)
                rows_turn(i, 0, True)
                own.leave(PROMPT_PAIRS)
            rows_turn(PROMPT_PAIRS, 1, False)

            def indexed(e, pairs, wait, count):
                pool.wait_ge(wait, count)
                carrier()
                for dst, src in pairs:
                    own.did(pool.tensor_copy(dst, src[:, ds(e, 1)]))
                own.settle()
                carrier()

            def gather(e, wait, count):
                indexed(e, ((g_idx_p[:, :], idx_p), (g_idx_s[:, :], idx_s)), wait, count)
                for dst, idx in ((xg_p, g_idx_p), (xg_s, g_idx_s)):
                    pool.indirect_dma_start(out=dst, out_offset=None, in_=h2_rows,
                                            in_offset=bass.IndirectOffsetOnAxis(ap=idx[:, 0:1], axis=0)).then_inc(s_xg, 16)

            def scatter(e, first=False):
                if not first:
                    pool.wait_ge(s_sc, 32 * e)
                    carrier()
                pool.wait_ge(s_op, e + 1)
                carrier()
                indexed(e, ((s_idx_p[:, :], idx_p), (s_idx_s[:, :], idx_s)), s_os, e + 1)
                for src, idx in ((out_p, s_idx_p), (out_s, s_idx_s)):
                    pool.indirect_dma_start(out=y_rows, out_offset=bass.IndirectOffsetOnAxis(ap=idx[:, 0:1], axis=0),
                                            in_=src, in_offset=None, compute_op=ALU.add).then_inc(s_sc, 16)

            for s in range(2):
                pool.wait_ge(s_h2o[s], 16 * PAIRS)
            pool.wait_ge(s_y0, 16)
            pool.wait_ge(s_topT, 1)
            gather(0, s_idx, 4)
            gather(1, s_xt, 1)
            scatter(0, True)
            n = own.n
            gather(2, s_xt, 2)
            scatter(1)
            per = own.n - n
            with pool.Fori(2, NE - 1) as e:
                own.enter(e - 2, per)
                gather(e + 1, s_xt, e + 1)
                scatter(e)
                own.leave(NE - 3)
            scatter(NE - 1)

            def last_turn(i):
                for s in range(2):
                    t = 2 * i + s
                    power2(s_st3, s_rs3, ln_cols(1, s), t + 1)
                    pool.wait_ge(s_fn, t + 1)
                    own.did(pool.tensor_tensor(y_in[s], y_in[s], ln2g_b, ALU.mult))
                    own.settle()
                    pool.tensor_tensor(y_in[s], y_in[s], ln2b_b, ALU.add).then_inc(s_fo, 1)

            pool.wait_ge(s_ln2, 32)
            with pool.Fori(0, PAIRS) as i:
                own.enter(i, 2)
                last_turn(i)
                own.leave(PAIRS)

        @block.scalar
        def _(act):
            act.wait_ge(s_rows, 64)
            act.activation(rows_in[0:16, :], rows_in[0:16, :], ACT.Silu).then_inc(s_silu, 1)

            def turn(i, group):
                for s in range(2):
                    t = 2 * i + s
                    act.wait_ge(s_tp, t + 1)
                    if group or True:
                        free_at(act, t, i)
                    for k in range(KD):
                        last = act.activation(h_tile[s][:, k, :], tp[s][:, k, :], ACT.Identity,
                                              bias=modT[:, k, group:group + 1],
                                              scale=modT[:, 8 + k, group:group + 1])
                    last.then_inc(s_ht, 1)
                for s in range(2):
                    t = 2 * i + s
                    act.wait_ge(s_z1, t + 1)
                    wait_if(act, s_qr, t - 1, i)
                    act.activation(z_qkv[s][:, 0:512], z1, ACT.Copy).then_inc(s_zc, 1)
                    act.wait_ge(s_z2, t + 1)
                    act.activation(z_qkv[s][:, 512:768], z2, ACT.Copy).then_inc(s_zc, 1)
                    act.wait_ge(s_z3, t + 1)
                    wait_if(act, s_vn, t - 1, i)
                    act.activation(v_gelu[s], z3, ACT.Gelu_apprx_tanh).then_inc(s_vg, 1)
                for s in range(2):
                    t = 2 * i + s
                    act.wait_ge(s_qt, t + 1)
                    act.activation(qT[:, :, ds(i * 256 + s * P, P)], tp[s][:, 0:4, :], ACT.Copy)
                    act.activation(kT[:, :, ds(i * 256 + s * P, P)], tp[s][:, 4:6, :], ACT.Copy).then_inc(s_qe, 1)

            def wait_if(eng, s, value, i):
                if not (isinstance(i, int) and i == 0):
                    eng.wait_ge(s, value)

            def free_at(eng, t, i):
                wait_if(eng, s_z3, t - 1, i)
                wait_if(eng, s_hc, t - 1, i)

            act.wait_ge(s_mod, 1)
            turn(0, 0)
            with act.Fori(1, PROMPT_PAIRS) as i:
                turn(i, 0)
            turn(PROMPT_PAIRS, 1)

            act.wait_ge(s_tp, TILES)
            act.wait_ge(s_xh, TILES)
            for j in range(4):
                act.wait_ge(s_f[j % 2], j // 2 + 1)
                act.activation(y0[:, j, :], res[j % 2], ACT.Gelu_apprx_tanh).then_inc(s_fe[j % 2], 1)
            act.wait_ge(s_pads, 1)
            for g in range(4):
                r = R_B + g
                act.wait_ge(s_f[r % 2], r // 2 + 1)
                if g >= 2:
                    act.wait_ge(s_pool, g - 1)
                for at, lo, n in SEGS:
                    last = act.activation(z_pad[g % 2][:, at:at + n], res[r % 2][:, lo:lo + n], ACT.Copy)
                last.then_inc(s_fe[r % 2], 1)

            def gates(name):
                _, r0, _, m0, _ = MERGES[name]

                def turn(i, first):
                    for s in range(2):
                        act.wait_ge(s_f[0], r0 // 2 + 2 * i + s + 1)
                        act.wait_ge(s_fe[1], r0 // 2 + 2 * i + s)
                        act.activation(gate_sb, res[0], ACT.Sigmoid).then_inc(s_fe[0], 1)

                turn(0, True)
                with act.Fori(1, 4) as i:
                    turn(i, False)

            gates("A")
            for g in range(4):
                r = R_MIX + g
                act.wait_ge(s_f[r % 2], r // 2 + 1)
                act.activation(y1[:, g, :], res[r % 2], ACT.Copy, scale=colT[:, 76 + g:77 + g]).then_inc(s_fe[r % 2], 1)
            for j in range(4):
                r = R_D + 3 * j
                act.wait_ge(s_f[r % 2], r // 2 + 1)
                if j == 0:
                    act.wait_ge(s_pool, 4)
                else:
                    act.wait_ge(s_fe[(r - 2) % 2], (r - 2) // 2 + 1)
                act.activation(cg_sb, res[r % 2], ACT.Copy).then_inc(s_fe[r % 2], 1)
            gates("B")
            gates("D")

            def attend(t, keys):
                n = N_Q * t

                def exp(h):
                    act.wait_ge(s_mx, n + h + 1)
                    if not (isinstance(t, int) and t == 0 and h < 2):
                        act.wait_ge(s_pt, n + h - 1)
                    act.activation(prob[h % 2][:, 0:keys], s_ps[h % 2][:, 0:keys], ACT.Exp,
                                   bias=small[:, 2 * (h % 2):2 * (h % 2) + 1], scale=HD ** -0.5,
                                   accum_out=small[:, 2 * (h % 2) + 1:2 * (h % 2) + 2]).then_inc(s_exp, 1)

                exp(0)
                for h in range(N_Q):
                    if h + 1 < N_Q:
                        exp(h + 1)
                    act.wait_ge(s_pt, n + h + 1)
                    if not (isinstance(t, int) and t == 0 and h < 2):
                        act.wait_ge(s_pv, n + h - 1)
                    act.activation(probT[h % 2][:, 0:keys // P, :], pt_ps[:, 0:keys // P, :], ACT.Copy).then_inc(s_pte, 1)

            attend(0, T_PROMPT)
            with act.Fori(1, T_PROMPT // P) as t:
                attend(t, T_PROMPT)
            with act.Fori(T_PROMPT // P, TILES) as t:
                attend(t, T_SAMPLE)
            gates("C")

            def route(s, t, part):
                if part == "h":
                    act.wait_ge(s_et, t + 1)
                    act.activation(h2T[s], h2t_ps, ACT.Copy).then_inc(s_h2T, 1)
                elif part == "aff":
                    act.wait_ge(s_at, t + 1)
                    act.activation(affT[:, ds(t * P, P)], affT_ps, ACT.Copy).then_inc(s_affT, 1)
                else:
                    act.wait_ge(s_sm, t + 1)
                    act.activation(aff_t[:, s, 1, :], aff_t[:, s, 0, :], ACT.Exp, bias=small[:, 2 * s:2 * s + 1],
                                   accum_out=small[:, 2 * s + 1:2 * s + 2]).then_inc(s_se, 1)

            act.wait_ge(s_f[1], R_END // 2)
            act.wait_ge(s_mg, 24)
            act.wait_ge(s_mout, 16 * 16)
            route(0, 0, "h")
            route(0, 0, "exp")
            route(1, 1, "h")
            route(0, 0, "aff")
            route(1, 1, "exp")
            with act.Fori(1, PAIRS) as i:
                for s in range(2):
                    route(s, 2 * i + s, "h")
                    route(1 - s, 2 * i + s - 1, "aff")
                    route(s, 2 * i + s, "exp")
            route(1, TILES - 1, "aff")

            def expert(e, more):
                for j in range(KD):
                    act.wait_ge(s_ab, 8 * e + j + 1)
                    if not (isinstance(e, int) and e == 0 and j < 2):
                        act.wait_ge(s_g, 8 * e + j - 1)
                    act.activation(silu[j % 2], ab_ps[j % 2][:, 0, :], ACT.Silu).then_inc(s_si, 1)
                if more:
                    act.wait_ge(s_xt, e + 2)
                    act.activation(xgT[:, :, 0:CAP_P], xt_p, ACT.Copy).then_inc(s_xe, 1)
                act.wait_ge(s_ot, e + 1)
                if not (isinstance(e, int) and e == 0):
                    act.wait_ge(s_sc, 32 * e)
                act.activation(out_p, op_ps, ACT.Copy, scale=gate_p[:, ds(e, 1)]).then_inc(s_op, 1)

            act.wait_ge(s_xt, 1)
            act.activation(xgT[:, :, 0:CAP_P], xt_p, ACT.Copy).then_inc(s_xe, 1)
            act.wait_ge(s_idx, 4)
            expert(0, True)
            with act.Fori(1, NE - 1) as e:
                expert(e, True)
            expert(NE - 1, False)

        @block.vector
        def _(dve):
            own = Chain(dve, own_v)

            dve.wait_ge(s_rT, 1)
            dve.wait_ge(own_p, 1)
            dve.tensor_copy(colT[:, :], rows_ps).then_inc(s_col, 1)
            dve.wait_ge(s_modmm, 4)
            dve.wait_ge(s_col, 1)
            own.did(dve.tensor_tensor(modT[:, :, :], mod_ps, colT[:, 16:32].unsqueeze(2).to_broadcast([P, 16, 2]), ALU.add))
            own.settle()
            dve.tensor_scalar(modT[:, 8:16, :], modT[:, 8:16, :], 1.0, None, ALU.add).then_inc(s_mod, 1)
            dve.wait_ge(s_wsT, 1)
            dve.tensor_copy(wsT, ws_ps).then_inc(s_wsT, 1)

            def norm_stats(src, cols, bn, n):
                for j in range(n // 512):
                    own.did(dve.bn_stats(bn[:, 6 * j:6 * j + 6], src[:, 512 * j:512 * j + 512]))
                own.settle()
                own.did(dve.tensor_copy(carry[:, 0:1], half[:, 0:1]))
                own.did(dve.bn_aggr(cols[:, 0:2], bn[:, 0:6 * (n // 512)]))
                own.settle()
                dve.tensor_scalar(cols[:, 7:8], cols[:, 1:2], LN_EPS, None, ALU.add).then_inc(s_stat, 1)

            bn = aff_t[:, 0, 0, 0:12]

            def ln_x_stats(i, s, n_loads):
                dve.wait_ge(s_x[s], n_loads)
                norm_stats(x_in[s], ln_cols(0, s), bn, D)

            def ln_x_apply(s, tile_before, rs_count, first):
                dve.wait_ge(s_rs, rs_count)
                if not first:
                    dve.wait_ge(s_tp, tile_before)
                cols = ln_cols(0, s)
                dve.tensor_scalar(xh[s], x_in[s], cols[:, 0:1], cols[:, 7:8], ALU.subtract, ALU.mult).then_inc(s_xh, 1)

            def turn(i, ahead):
                for s in range(2):
                    t = 2 * i + s
                    n0 = 3 * t + 2
                    z = z_qkv[s]
                    dve.wait_ge(s_zc, 2 * t + 2)
                    own.did(dve.tensor_tensor(r_sq, z[:, 0:640], z[:, 0:640], ALU.mult))
                    own.did(dve.tensor_copy(va[:, ds(t, 1), :].rearrange("p a n -> p (a n)"), z[:, 640:768]))
                    own.settle()
                    rs = small[:, 32 + 16 * s:42 + 16 * s]
                    own.did(dve.tensor_reduce(rs, r_sq.rearrange("p (h n) -> p h n", n=HD), AX.X, ALU.add))
                    own.settle()
                    dve.tensor_scalar(rs, rs, 1.0 / HD, RMS_EPS, ALU.mult, ALU.add).then_inc(s_stat, 1)
                    if ahead:
                        ln_x_stats(i, s, 16 * (i + 2))
                    dve.wait_ge(s_rs, n0 + 1 if ahead else 3 * t + 3 - s)
                    v3 = lambda a: a.rearrange("p (h n) -> p h n", n=HD)
                    own.did(dve.tensor_tensor(v3(r_n), v3(z[:, 0:640]), rs.unsqueeze(2).to_broadcast([P, N_QK, HD]), ALU.mult))
                    own.settle()
                    own.did(dve.tensor_tensor(r_sq, r_n, gqk, ALU.mult))
                    own.settle()
                    pair = r_sq.rearrange("p (h n two) -> p h n two", n=32, two=2)
                    cs = cossin[:, ds(t, 1), :, :].rearrange("p t a n -> p (t a) n")
                    cos = cs[:, 0:1, :].to_broadcast([P, N_QK, 32])
                    sin = cs[:, 1:2, :].to_broadcast([P, N_QK, 32])
                    h3 = lambda a: a.rearrange("p (h n) -> p h n", n=32)
                    if not (isinstance(i, int) and i == 0):
                        dve.wait_ge(s_qt, t - 1)
                    for part, (ca, cb, op) in enumerate(((cos, sin, ALU.subtract), (sin, cos, ALU.add))):
                        if part:
                            own.settle()
                        own.did(dve.tensor_tensor(h3(r_a), pair[:, :, :, 0], ca, ALU.mult))
                        own.did(dve.tensor_tensor(h3(r_b2), pair[:, :, :, 1], cb, ALU.mult))
                        own.settle()
                        oq = qk_out[s][:, 0:512].rearrange("p (h n two) -> p h n two", n=32, two=2)[:, :, :, part]
                        own.did(dve.tensor_tensor(oq, h3(r_a)[:, 0:N_Q, :], h3(r_b2)[:, 0:N_Q, :], op))
                        for copy in range(2):
                            ok = qk_out[s][:, 512:768].rearrange("p (g c n two) -> p g c n two", g=2, c=2, two=2)[:, :, copy, :, part]
                            last = dve.tensor_tensor(ok, h3(r_a)[:, N_Q:N_QK, :], h3(r_b2)[:, N_Q:N_QK, :], op)
                            if part == 0 or copy == 0:
                                own.did(last)
                            else:
                                last.then_inc(s_qr, 1)
                    if ahead:
                        ln_x_apply(s, t + 1, n0 + 2, False)
                    dve.wait_ge(s_vg, t + 1)
                    norm_stats(v_gelu[s], ln_cols(1, s), bn, W_BR)
                    dve.wait_ge(s_rs, n0 + 3 if ahead else 3 * t + 4 - s)
                    cols = ln_cols(1, s)
                    dve.tensor_scalar(vln[:, ds(t, 1), :].rearrange("p a n -> p (a n)"), v_gelu[s],
                                      cols[:, 0:1], cols[:, 7:8], ALU.subtract, ALU.mult).then_inc(s_vn, 1)

            for s in range(2):
                ln_x_stats(0, s, 16)
                ln_x_apply(s, 0, s + 1, True)
            dve.wait_ge(s_gqk, 1)
            n_turn = 2 * (2 + 1 + 3 + 2 + 2 * 3 + 2 + 1 + 2)
            turn_first = own.n
            turn(0, True)
            per = own.n - turn_first
            with dve.Fori(1, PAIRS - 1) as i:
                own.enter(i - 1, per)
                turn(i, True)
                own.leave(PAIRS - 2)
            turn(PAIRS - 1, False)

            own.settle()
            dve.wait_ge(s_qt, TILES)
            dve.wait_ge(s_qr, TILES)
            for s in range(2):
                own.did(dve.memset(z_pad[s], 0.0))
            own.settle()
            dve.tensor_copy(zero_col[:, :], z_pad[0][:, 0:1]).then_inc(s_pads, 1)
            dve.wait_ge(s_fe[0], 2)
            dve.wait_ge(s_fe[1], 2)
            gate3 = gate_sb[:, 0:512].rearrange("p (g n) -> p g n", g=4)
            b3 = bs_b.rearrange("p (g n) -> p g n", g=4)
            for t in range(TILES):
                dve.wait_ge(s_sv, t + 1)
                u = y0[:, :, t * P:(t + 1) * P]
                dve.tensor_tensor(gate3, sv_ps[t % 2], b3, ALU.add).then_inc(s_sve, 1)
                dve.wait_ge(s_sve, t + 1)
                dve.tensor_tensor(u, u, gate3, ALU.mult).then_inc(s_ya, 1)
                dve.wait_ge(s_ya, t + 1)
            for g, w in enumerate(WINDOWS):
                z = z_pad[g % 2]
                dve.wait_ge(s_fe[g % 2], (R_B + g) // 2 + 1)
                n = PADDED
                own.settle()
                own.did(dve.tensor_tensor(sum_a[:, 1:n], z[:, 0:n - 1], z[:, 1:n], ALU.add))
                src, dst, a = sum_a, sum_b, 1
                while 2 * a < w:
                    own.settle()
                    own.did(dve.tensor_tensor(dst[:, 2 * a:n - 2 * a], src[:, a:n - 3 * a], src[:, 3 * a:n - a], ALU.add))
                    src, dst, a = dst, src, 2 * a
                own.settle()
                for at, lo, m in SEGS:
                    own.did(dve.scalar_tensor_tensor(out=y1[:, g, lo:lo + m], in0=src[:, at:at + m], scalar=1.0 / w,
                                                     in1=z[:, at:at + m], op0=ALU.mult, op1=ALU.subtract))
                for e, (at, lo, m) in enumerate(SEGS):
                    for side, (sl, o) in enumerate(((slice(at, at + 8), lo), (slice(at + m - 8, at + m), lo + m - 8))):
                        own.settle()
                        own.did(dve.tensor_tensor(dst[:, 0:8], src[:, sl], edge[:, g, 2 * e + side, :], ALU.mult))
                        own.settle()
                        last = dve.tensor_tensor(y1[:, g, o:o + 8], dst[:, 0:8], z[:, sl], ALU.subtract)
                        if e and side:
                            last.then_inc(s_pool, 1)
                            dve.wait_ge(s_pool, g + 1)
                        else:
                            own.did(last)

            def merge(name):
                _, r0, _, m0, _ = MERGES[name]

                def turn(i, first):
                    for s in range(2):
                        dm = merged[:, ds(2 * i + s, 1), :].rearrange("p a n -> p (a n)")
                        done = r0 // 2 + 2 * i + s + 1
                        dve.wait_ge(s_fe[0], done)
                        dve.wait_ge(s_f[1], done)
                        if name == "A":
                            dve.tensor_tensor(dm, gate_sb, res[1], ALU.mult).then_inc(s_fe[1], 1)
                            continue
                        if not (first and s == 0 and m0 == 8):
                            dve.wait_ge(s_mg, m0 - 8 + 2 * i + s)
                        dve.tensor_tensor(prod, gate_sb, res[1], ALU.mult).then_inc(s_fe[1], 1)
                        dve.wait_ge(s_fe[1], done)
                        dve.tensor_tensor(dm, dm, prod, ALU.add).then_inc(s_mg, 1)

                turn(0, True)
                with dve.Fori(1, 4) as i:
                    turn(i, False)

            merge("A")
            own.did(dve.memset(z_conv, 0.0))
            for j in range(4):
                rc, rx, rb = (R_D + 3 * j + m for m in range(3))
                dve.wait_ge(s_fe[rc % 2], rc // 2 + 1)
                dve.wait_ge(s_f[rx % 2], rx // 2 + 1)
                own.settle()
                for e, (at, lo, m) in enumerate(CSEGS):
                    last = dve.tensor_tensor(z_conv[:, at:at + m], cg_sb[:, lo:lo + m], res[rx % 2][:, lo:lo + m], ALU.mult)
                    if e:
                        last.then_inc(s_fe[rx % 2], 1)
                    else:
                        own.did(last)
                dve.wait_ge(s_fe[rx % 2], rx // 2 + 1)
                own.settle()
                n = T + 4
                tap = [colT[:, 64 + 4 * q + j:65 + 4 * q + j] for q in range(3)]
                own.did(dve.tensor_scalar(taps[:, 1:n - 1], z_conv[:, 0:n - 2], tap[0], None, ALU.mult))
                for q in (1, 2):
                    own.settle()
                    own.did(dve.scalar_tensor_tensor(out=taps[:, 1:n - 1], in0=z_conv[:, q:n - 2 + q], scalar=tap[q],
                                                     in1=taps[:, 1:n - 1], op0=ALU.mult, op1=ALU.add))
                dve.wait_ge(s_f[rb % 2], rb // 2 + 1)
                own.settle()
                for e, (at, lo, m) in enumerate(CSEGS):
                    last = dve.tensor_tensor(y0[:, j, lo:lo + m], taps[:, at:at + m], res[rb % 2][:, lo:lo + m], ALU.mult)
                    if e:
                        last.then_inc(s_fe[rb % 2], 1)
                    else:
                        own.did(last)
                dve.wait_ge(s_fe[rb % 2], rb // 2 + 1)
            merge("B")
            merge("D")

            def attend(t, keys):
                n = N_Q * t

                def row_max(h):
                    u = h % 2
                    dve.wait_ge(s_qk, n + h + 1)
                    own.did(dve.tensor_reduce(small[:, 4 + u:5 + u], s_ps[u][:, 0:keys], AX.X, ALU.max))
                    own.settle()
                    dve.tensor_scalar(small[:, 2 * u:2 * u + 1], small[:, 4 + u:5 + u], -HD ** -0.5, None, ALU.mult).then_inc(s_mx, 1)

                def pair_out(j):
                    dve.wait_ge(s_pv, n + 2 * j + 2)
                    dve.tensor_copy(y1[:, j, ds(t * P, P)], o_ps[j % 2]).then_inc(s_oe, 1)

                row_max(0)
                for h in range(N_Q):
                    u = h % 2
                    if h + 1 < N_Q:
                        row_max(h + 1)
                    dve.wait_ge(s_exp, n + h + 1)
                    own.did(dve.reciprocal(small[:, 6 + u:7 + u], small[:, 2 * u + 1:2 * u + 2]))
                    own.settle()
                    dve.tensor_scalar(prob[u][:, 0:keys], prob[u][:, 0:keys], small[:, 6 + u:7 + u], None, ALU.mult).then_inc(s_pn, 1)
                    if h >= 2 and h % 2 == 0:
                        pair_out(h // 2 - 1)
                pair_out(3)

            dve.wait_ge(s_mg, 16)
            own.enter(0, 0)
            own.base, own.n = own.before, 0
            attend(0, T_PROMPT)
            own.base, own.n = 0, own.before + own.n
            for first, end, keys in ((1, T_PROMPT // P, T_PROMPT), (T_PROMPT // P, TILES, T_SAMPLE)):
                with dve.Fori(first, end) as t:
                    own.enter(t - first, 2 * N_Q)
                    attend(t, keys)
                    own.leave(end - first)
            merge("C")

            dve.wait_ge(s_f[0], R_END // 2)
            dve.wait_ge(s_mg, 24)
            own.did(dve.memset(c_pad, 0.0))
            own.settle()
            dve.tensor_copy(c_pad[:, :, 0:64:32], colT[:, 0:16].rearrange("p (g k) -> p k g", g=2)).then_inc(s_cpad, 1)
            dve.wait_ge(s_brow, 32)
            for m in range(8):
                dve.wait_ge(s_modr, m + 1)
                if m >= 2:
                    dve.wait_ge(s_mout, 32 * m)
                for g in range(2):
                    r = slice(32 * g, 32 * g + 1)
                    one = 1.0 if m in (4, 5) else 0.0
                    dve.scalar_tensor_tensor(out=m_row[m % 2][r, :], in0=mod_row_ps[m % 2][r, :], scalar=one,
                                             in1=b_row[r, 512 * m:512 * m + 512], op0=ALU.add, op1=ALU.add).then_inc(s_mrow, 1)

            bn2 = aff_t2[:, 0:12]

            def stats(src, cols, done):
                for j in range(2):
                    own.did(dve.bn_stats(bn2[:, 6 * j:6 * j + 6], src[:, 512 * j:512 * j + 512]))
                own.settle()
                own.did(dve.tensor_copy(carry[:, 0:1], half[:, 0:1]))
                own.did(dve.bn_aggr(cols[:, 0:2], bn2))
                own.settle()
                dve.tensor_scalar(cols[:, 7:8], cols[:, 1:2], LN_EPS, None, ALU.add).then_inc(done, 1)

            def apply(dst, src, cols, done):
                dve.tensor_scalar(dst, src, cols[:, 0:1], cols[:, 7:8], ALU.subtract, ALU.mult).then_inc(done, 1)

            def soft1(s, t):
                lg = aff_t[:, s, 0, :]
                dve.wait_ge(s_lg, t + 1)
                own.did(dve.tensor_tensor(lg, logit_ps, rb_b[:, :], ALU.add))
                own.settle()
                own.did(dve.tensor_reduce(small[:, 4 + s:5 + s], lg, AX.X, ALU.max))
                own.settle()
                dve.tensor_scalar(small[:, 2 * s:2 * s + 1], small[:, 4 + s:5 + s], -1.0, None, ALU.mult).then_inc(s_sm, 1)

            def soft2(s, t):
                dve.wait_ge(s_se, t + 1)
                own.did(dve.reciprocal(small[:, 6 + s:7 + s], small[:, 2 * s + 1:2 * s + 2]))
                own.settle()
                if not (isinstance(t, int) and t < 2):
                    dve.wait_ge(s_at, t - 1)
                dve.tensor_scalar(aff_t[:, s, 2, :], aff_t[:, s, 1, :], small[:, 6 + s:7 + s], None, ALU.mult).then_inc(s_aff, 1)

            def rows_turn(i, grp, first=False, second=False):
                for s in range(2):
                    t = 2 * i + s
                    c1, c2 = ln_cols(1, s), ln_cols(2, s)
                    dve.wait_ge(s_y, t + 1)
                    if not first:
                        dve.wait_ge(s_x1o[s], 16 * i)
                    dve.tensor_tensor(x1_row[s], y_ps[s], g1_b[grp], ALU.mult).then_inc(s_yr, 1)
                    dve.wait_ge(s_yr, t + 1)
                    dve.wait_ge(s_xr[s], 16 * i + 16)
                    dve.scalar_tensor_tensor(out=x1_row[s], in0=x_row[s], scalar=ALPHA, in1=x1_row[s],
                                             op0=ALU.mult, op1=ALU.add).then_inc(s_xa, 1)
                    dve.wait_ge(s_xa, t + 1)
                    stats(x1_row[s], c1, s_st2)
                    dve.wait_ge(s_rs2, 2 * t + 1)
                    apply(x1_row[s], x1_row[s], c1, s_ln)
                    if not first:
                        soft1(s, t - 2)
                    dve.wait_ge(s_x1, t + 1)
                    stats(x1_row[s], c2, s_st2)
                    if not first:
                        soft2(s, t - 2)
                    dve.wait_ge(s_rs2, 2 * t + 2)
                    if not first:
                        dve.wait_ge(s_h2o[s], 16 * i)
                        dve.wait_ge(s_et, t - 1)
                    apply(h2_row[s], x1_row[s], c2, s_ln)

            dve.wait_ge(s_rows2, 16 * 10)
            rows_turn(0, 0, True)
            n = own.n
            own_before = own.n
            rows_turn(1, 0)
            per = own.n - n
            with dve.Fori(2, PROMPT_PAIRS) as i:
                own.enter(i - 2, per)
                rows_turn(i, 0)
                own.leave(PROMPT_PAIRS - 2)
            rows_turn(PROMPT_PAIRS, 1)
            for s in range(2):
                soft1(s, TILES - 2 + s)
                soft2(s, TILES - 2 + s)

            dve.wait_ge(s_affT, TILES)
            for lo, n, cap, at in ((0, T_PROMPT, CAP_P, 0), (T_PROMPT, T_SAMPLE, CAP_S, CAP_P)):
                left = affT[:, lo:lo + n]
                for r in range(at, at + cap, 8):
                    own.settle()
                    own.did(dve.max(out=top_v[:, r:r + 8], in_=left))
                    own.settle()
                    own.did(dve.max_index(out=top_i[:, r:r + 8], in_max=top_v[:, r:r + 8], in_values=left))
                    own.settle()
                    own.did(dve.match_replace(out=left, in_to_replace=top_v[:, r:r + 8], in_values=left, imm_value=-1.0))
            own.settle()
            own.did(dve.tensor_copy(top_f, top_i[:, :]))
            own.settle()
            dve.tensor_scalar(top_f[:, CAP_P:CAP], top_f[:, CAP_P:CAP], float(T_PROMPT), None, ALU.add).then_inc(s_top, 1)
            dve.wait_ge(s_topT, 1)
            for dst, src in ((gate_p[:, :], top_ps[:, 0, :]), (idx_p[:, :], top_ps[:, 1, :]),
                             (gate_s[:, :], top_ps[0:CAP_S, 2, :]), (idx_s[:, :], top_ps[0:CAP_S, 3, :])):
                dve.tensor_copy(dst, src).then_inc(s_idx, 1)

            def expert(e, more):
                for j in range(KD):
                    dve.wait_ge(s_si, 8 * e + j + 1)
                    dve.tensor_tensor(gT[:, j, :], silu[j % 2], ab_ps[j % 2][:, 1, :], ALU.mult).then_inc(s_g, 1)
                if more:
                    dve.wait_ge(s_xt, e + 2)
                    dve.tensor_copy(xgT[:, :, CAP_P:CAP], xt_s).then_inc(s_xes, 1)
                for j in range(KD):
                    dve.wait_ge(s_o, 8 * e + j + 1)
                    dve.tensor_copy(outT[:, j, :], ab_ps[j % 2][:, 0, :]).then_inc(s_oT, 1)
                dve.wait_ge(s_ot, e + 1)
                if not (isinstance(e, int) and e == 0):
                    dve.wait_ge(s_sc, 32 * e)
                for h in range(2):
                    last = dve.tensor_scalar(out_s[:, 512 * h:512 * h + 512], os_ps[h], gate_s[:, ds(e, 1)], None, ALU.mult)
                last.then_inc(s_os, 1)

            dve.wait_ge(s_idx, 4)
            dve.wait_ge(s_xt, 1)
            dve.tensor_copy(xgT[:, :, CAP_P:CAP], xt_s).then_inc(s_xes, 1)
            expert(0, True)
            with dve.Fori(1, NE - 1) as e:
                expert(e, True)
            expert(NE - 1, False)

            def last_turn(i, grp):
                for s in range(2):
                    t = 2 * i + s
                    c1 = ln_cols(1, s)
                    dve.wait_ge(s_fx[s], 32 * i + 32)
                    own.did(dve.tensor_tensor(y_in[s], y_in[s], g2_b[grp], ALU.mult))
                    own.settle()
                    own.did(dve.scalar_tensor_tensor(out=y_in[s], in0=x1_in[s], scalar=ALPHA, in1=y_in[s],
                                                     op0=ALU.mult, op1=ALU.add))
                    own.settle()
                    stats(y_in[s], c1, s_st3)
                    dve.wait_ge(s_rs3, t + 1)
                    apply(y_in[s], y_in[s], c1, s_fn)

            n = own.n
            last_turn(0, 0)
            per = own.n - n
            with dve.Fori(1, PROMPT_PAIRS) as i:
                own.enter(i - 1, per)
                last_turn(i, 0)
                own.leave(PROMPT_PAIRS - 1)
            last_turn(PROMPT_PAIRS, 1)

        @block.tensor
        def _(pe):
            pe.wait_ge(s_id, 1)
            pe.wait_ge(s_silu, 1)
            pe.wait_ge(s_rows, 64)
            pe.transpose(rows_ps, rows_in[0:80, :], ident[0:80, 0:80]).then_inc(s_rT, 1)
            pe.wait_ge(s_col, 1)
            cT = colT[:, 0:16].rearrange("p (g k) -> p k g", g=2)
            for m in range(4):
                pe.wait_ge(s_wada[m % 2], 16 * (m // 2 + 1))
                for j in range(4):
                    for k in range(KD):
                        last = pe.matmul(mod_ps[:, 4 * m + j, :], w_ada_buf[m % 2][:, k, j * P:(j + 1) * P], cT[:, k, :],
                                         start=k == 0, stop=k == KD - 1)
                last.then_inc(s_modmm, 1)
            pe.wait_ge(s_ws, 16)
            for g in range(4):
                last = pe.transpose(ws_ps[:, g, :], ws_in[:, g, :], ident[:, :])
            last.then_inc(s_wsT, 1)

            def turn(i, first=False):
                for s in range(2):
                    t = 2 * i + s
                    pe.wait_ge(s_xh, t + 1)
                    if not first:
                        pe.wait_ge(s_qe, t - 1)
                    for k in range(KD):
                        last = pe.transpose(tp[s][:, k, :], xh[s][:, k * P:(k + 1) * P], ident[:, :])
                    last.then_inc(s_tp, 1)
                for s in range(2):
                    t = 2 * i + s
                    pe.wait_ge(s_ht, t + 1)
                    zero = first and s == 0
                    for dst, lo, n, done, freed, cnt in ((z1, 0, 512, s_z1, s_zc, 2 * t - 1), (z2, 512, 256, s_z2, s_zc, 2 * t),
                                                         (z3, 768, 512, s_z3, s_vg, t)):
                        if not zero:
                            pe.wait_ge(freed, cnt)
                        for k in range(KD):
                            last = pe.matmul(dst, h_tile[s][:, k, :], wz[:, k, lo:lo + n], start=k == 0, stop=k == KD - 1)
                        last.then_inc(done, 1)
                for s in range(2):
                    t = 2 * i + s
                    pe.wait_ge(s_qr, t + 1)
                    for k in range(6):
                        last = pe.transpose(tp[s][:, k, :], qk_out[s][:, k * P:(k + 1) * P], ident[:, :])
                    last.then_inc(s_qt, 1)

            pe.wait_ge(s_wz, 32)
            pe.wait_ge(s_mod, 1)
            pe.wait_ge(s_wsT, 2)
            turn(0, True)
            with pe.Fori(1, PAIRS) as i:
                turn(i)

            def product(par, freed, w, count, k_tiles, rhs):
                if freed is not None:
                    pe.wait_ge(s_fe[par], freed)
                pe.wait_ge(w[1], count)
                for lo, n in BLOCKS:
                    for k in range(k_tiles):
                        last = pe.matmul(res[par][:, lo:lo + n], w[0][:, k, :], rhs[:, k, lo:lo + n],
                                         start=k == 0, stop=k == k_tiles - 1)
                last.then_inc(s_f[par], 1)

            def wt(s):
                return w_tile[s], s_w[s]

            pe.wait_ge(s_qe, TILES)
            pe.wait_ge(s_zc, 2 * TILES)
            pe.wait_ge(s_vg, TILES)
            pe.wait_ge(s_hc, TILES)
            for s in range(2):
                product(s, None, wt(s), 16, KD, hT)
            with pe.Fori(1, 2) as i:
                for s in range(2):
                    product(s, i, wt(s), 16 * i + 16, KD, hT)
            pe.wait_ge(s_vl, TILES)
            for t in range(TILES):
                if t >= 2:
                    pe.wait_ge(s_sve, t - 1)
                for g in range(4):
                    last = pe.matmul(sv_ps[t % 2][:, g, :], vln[:, t, g * P:(g + 1) * P], wsT[:, g, :], start=True, stop=True)
                last.then_inc(s_sv, 1)
            with pe.Fori(2, 4) as i:
                for s in range(2):
                    product(s, i, wt(s), 16 * i + 16, KD, hT)

            def merge(name):
                n0, r0, _, m0, y = MERGES[name]
                with pe.Fori(0, 4) as i:
                    for s in range(2):
                        product(0, r0 // 2 + 2 * i + s, wt(s), 8 * n0 + 16 * i + 16, KD, hT)
                        product(1, r0 // 2 + 2 * i + s, (p_tile[s], s_p[s]), 8 * m0 + 16 * i + 16, KB, y)

            pe.wait_ge(s_ya, TILES)
            merge("A")
            pe.wait_ge(s_wg, 16)
            pe.wait_ge(s_pool, 4)
            for g in range(4):
                r = R_MIX + g
                pe.wait_ge(s_fe[r % 2], r // 2)
                for lo, n in BLOCKS:
                    last = pe.matmul(res[r % 2][:, lo:lo + n], wg_sb[:, g, :], y1[:, g, lo:lo + n], start=True, stop=True)
                last.then_inc(s_f[r % 2], 1)
            with pe.Fori(0, 2) as i:
                for m in range(6):
                    product(m % 2, R_D // 2 + 3 * i + m // 2, wt(m % 2), 8 * N_D + 48 * i + 16 * (m // 2) + 16, KD, hT)
            pe.wait_ge(s_fe[0], R_D // 2)
            pe.wait_ge(s_fe[1], R_D // 2)
            merge("B")
            pe.wait_ge(s_fe[1], R_MB // 2)
            merge("D")

            def attend(t, keys):
                n = N_Q * t

                def scores(h):
                    lo = HD * (h % 2)
                    if h == 0:
                        pe.wait_ge(s_qb, t + 1)
                    if not (isinstance(t, int) and t == 0 and h < 2):
                        pe.wait_ge(s_exp, n + h - 1)
                    for at in range(0, keys, 512):
                        m = min(512, keys)
                        k0 = 0 if keys == T_PROMPT else T_PROMPT
                        last = pe.matmul(s_ps[h % 2][:, at:at + m], q_tile[lo:lo + HD, h // 2, :],
                                         kT[lo:lo + HD, h // 4, k0 + at:k0 + at + m], start=True, stop=True)
                    last.then_inc(s_qk, 1)

                def weighted(h):
                    lo, j = HD * (h % 2), h // 2
                    pe.wait_ge(s_pte, n + h + 1)
                    if h % 2 == 0 and not (isinstance(t, int) and t == 0 and j < 2):
                        pe.wait_ge(s_oe, 4 * t + j - 1)
                    t0 = 0 if keys == T_PROMPT else T_PROMPT // P
                    for b in range(keys // P):
                        last = pe.matmul(o_ps[j % 2][lo:lo + HD, :], va[:, t0 + b, (h // 4) * HD:(h // 4 + 1) * HD],
                                         probT[h % 2][:, b, :], start=b == 0, stop=b == keys // P - 1)
                    last.then_inc(s_pv, 1)

                scores(0)
                for h in range(N_Q):
                    if h + 1 < N_Q:
                        scores(h + 1)
                    if h:
                        weighted(h - 1)
                    pe.wait_ge(s_pn, n + h + 1)
                    if not (isinstance(t, int) and t == 0 and h == 0):
                        pe.wait_ge(s_pte, n + h)
                    for b in range(keys // P):
                        last = pe.transpose(pt_ps[:, b, :], prob[h % 2][:, b * P:(b + 1) * P], ident[:, :])
                    last.then_inc(s_pt, 1)
                weighted(N_Q - 1)

            for s in range(2):
                pe.wait_ge(s_fe[s], R_MC // 2)
            pe.wait_ge(s_sve, TILES)
            attend(0, T_PROMPT)
            with pe.Fori(1, T_PROMPT // P) as t:
                attend(t, T_PROMPT)
            with pe.Fori(T_PROMPT // P, TILES) as t:
                attend(t, T_SAMPLE)
            pe.wait_ge(s_pte, N_Q * TILES)
            pe.wait_ge(s_exp, N_Q * TILES)
            pe.wait_ge(s_oe, 4 * TILES)
            merge("C")

            pe.wait_ge(s_cpad, 1)
            for s in range(2):
                pe.wait_ge(s_fe[s], R_END // 2)
            for m in range(8):
                pe.wait_ge(s_wm[m % 2], 16 * (m // 2) + 16)
                if m >= 2:
                    pe.wait_ge(s_mrow, 2 * m - 2)
                for k in range(KD):
                    last = pe.matmul(mod_row_ps[m % 2][0:64, :], c_pad[:, k, :], w_mod[m % 2][:, k, :], start=k == 0, stop=k == KD - 1)
                last.then_inc(s_modr, 1)

            def rows_out(i, s):
                t = 2 * i + s
                pe.wait_ge(s_mt, t + 1)
                if not (isinstance(i, int) and i == 0):
                    pe.wait_ge(s_yr, t - 1)
                for h in range(2):
                    for k in range(KD):
                        last = pe.matmul(y_ps[s][:, 512 * h:512 * h + 512], m_tile[s][:, k, :], wo_sb[:, k, 512 * h:512 * h + 512],
                                         start=k == 0, stop=k == KD - 1)
                last.then_inc(s_y, 1)

            def turn_h(s, t):
                pe.wait_ge(s_h2, t + 1)
                if not (isinstance(t, int) and t == 0):
                    pe.wait_ge(s_h2T, t)
                for k in range(KD):
                    last = pe.transpose(h2t_ps[:, k, :], h2_row[s][:, k * P:(k + 1) * P], ident[:, :])
                last.then_inc(s_et, 1)

            def logits(s, t):
                pe.wait_ge(s_h2T, t + 1)
                if not (isinstance(t, int) and t == 0):
                    pe.wait_ge(s_sm, t)
                for k in range(KD):
                    last = pe.matmul(logit_ps, h2T[s][:, k, :], rw_sb[:, k, :], start=k == 0, stop=k == KD - 1)
                last.then_inc(s_lg, 1)

            def turn_aff(s, t):
                pe.wait_ge(s_aff, t + 1)
                if not (isinstance(t, int) and t == 0):
                    pe.wait_ge(s_affT, t)
                pe.transpose(affT_ps, aff_t[:, s, 2, :], ident[:, :]).then_inc(s_at, 1)

            pe.wait_ge(s_wo, 32)
            pe.wait_ge(s_mrow, 16)
            for s in range(2):
                rows_out(0, s)
            for s in range(2):
                turn_h(s, s)
                rows_out(1, s)
                if s:
                    turn_aff(0, 0)
                logits(s, s)
            with pe.Fori(2, PAIRS) as i:
                for s in range(2):
                    turn_h(s, 2 * i + s - 2)
                    rows_out(i, s)
                    turn_aff(1 - s, 2 * i + s - 3)
                    logits(s, 2 * i + s - 2)
            for s in range(2):
                turn_h(s, TILES - 2 + s)
                turn_aff(1 - s, TILES - 3 + s)
                logits(s, TILES - 2 + s)
            turn_aff(1, TILES - 1)

            pe.wait_ge(s_top, 1)
            pe.wait_ge(s_affT, TILES)
            for a, (src, n, at) in enumerate(((top_v, CAP_P, 0), (top_f, CAP_P, 0), (top_v, CAP_S, CAP_P), (top_f, CAP_S, CAP_P))):
                last = pe.transpose(top_ps[0:n, a, :], src[:, at:at + n], ident[0:NE, 0:NE])
            last.then_inc(s_topT, 1)

            def turn_x(e, first=False):
                pe.wait_ge(s_xg, 32 * e + 32)
                if not first:
                    pe.wait_ge(s_os, e - 1)
                for k in range(KD):
                    pe.transpose(xt_p[:, k, :], xg_p[:, k * P:(k + 1) * P], ident[:, :])
                for k in range(KD):
                    last = pe.transpose(xt_s[:, k, :], xg_s[:, k * P:(k + 1) * P], ident[0:CAP_S, 0:CAP_S])
                last.then_inc(s_xt, 1)

            def expert(e, more, first=False):
                pe.wait_ge(s_xe, e + 1)
                pe.wait_ge(s_xes, e + 1)
                for j in range(KD):
                    if not (first and j < 2):
                        if j < 2:
                            pe.wait_ge(s_oT, 8 * e - 1 + j)
                        else:
                            pe.wait_ge(s_g, 8 * e + j - 1)
                    for m in range(2):
                        c = 2 * (j // 4) + m
                        if j % 4 == 0:
                            pe.wait_ge(s_wx[c], 16 * e + 16)
                        for k in range(KD):
                            last = pe.matmul(ab_ps[j % 2][:, m, :], w_half[c][:, k, (j % 4) * P:(j % 4 + 1) * P], xgT[:, k, :],
                                             start=k == 0, stop=k == KD - 1)
                    last.then_inc(s_ab, 1)
                if more:
                    turn_x(e + 1, first)
                for j in range(KD):
                    if j < 2:
                        pe.wait_ge(s_g, 8 * e + 7 + j)
                        if j == 0:
                            pe.wait_ge(s_g, 8 * e + 8)
                    else:
                        pe.wait_ge(s_oT, 8 * e + j - 1)
                    if j % 4 == 0:
                        pe.wait_ge(s_wx[4 + j // 4], 16 * e + 16)
                    for k in range(KD):
                        last = pe.matmul(ab_ps[j % 2][:, 0, :], w_half[4 + j // 4][:, k, (j % 4) * P:(j % 4 + 1) * P], gT[:, k, :],
                                         start=k == 0, stop=k == KD - 1)
                    last.then_inc(s_o, 1)
                pe.wait_ge(s_oT, 8 * e + 8)
                if more:
                    pe.wait_ge(s_xes, e + 2)
                if not first:
                    pe.wait_ge(s_op, e)
                    pe.wait_ge(s_os, e)
                for j in range(KD):
                    pe.transpose(op_ps[:, j * P:(j + 1) * P], outT[:, j, 0:CAP_P], ident[:, :])
                for j in range(KD):
                    last = pe.transpose(os_ps[j // 4][:, (j % 4) * P:(j % 4 + 1) * P], outT[:, j, CAP_P:CAP], ident[:, :])
                last.then_inc(s_ot, 1)

            pe.wait_ge(s_idx, 4)
            turn_x(0, True)
            expert(0, True, True)
            with pe.Fori(1, NE - 1) as e:
                expert(e, True)
            expert(NE - 1, False)


_NAMES = ("w_ada", "b_ada", "w_in", "a_ln_g", "a_ln_b", "a_ws", "a_bs", "b_wg", "b_scale", "c_q_g", "c_k_g", "d_conv")
_NAMES_2 = ("w_o", "ln1_g", "ln1_b", "r_w", "r_b", "e_w1", "e_w3", "e_w2", "ln2_g", "ln2_b")


def rope_table():
    inv = (np.float32(10000.0) ** (-np.arange(16, dtype=np.float32) / np.float32(16))).astype(np.float32)
    tables = []
    for n in (T_PROMPT, T_SAMPLE):
        row = np.repeat(np.arange(n // 64, dtype=np.float32), 64)
        col = np.tile(np.arange(64, dtype=np.float32), n // 64)
        angle = np.concatenate([row[:, None] * inv, col[:, None] * inv], axis=-1)
        tables.append(np.stack([np.cos(angle), np.sin(angle)], axis=1))
    table = np.concatenate(tables).astype(np.float32).reshape(TILES, P, 2, 32)
    return np.ascontiguousarray(table.transpose(1, 0, 2, 3))


def edge_counts():
    rows = []
    for w in WINDOWS:
        for n in (T_PROMPT, T_SAMPLE):
            t = np.arange(n)
            count = np.clip(t + w // 2, 0, n) - np.clip(t - w // 2, 0, n)
            rows += [count[:8], count[-8:]]
    return (np.float32(1) / np.stack(rows).astype(np.float32)).reshape(len(WINDOWS), 4, 8)


def kernel(**inputs):
    import concourse.bacc as _bacc
    from concourse.bass_utils import run_bass_kernel_spmd as _run

    given = {k: np.asarray(v) for k, v in inputs.items()}
    arrays = {
        "x": np.concatenate([given["x_prompt"][0], given["x_sample"][0]]),
        "c": np.concatenate([given["c_prompt"], given["c_sample"]]),
    }
    for name in _NAMES:
        arrays[name] = given[name][0]
    arrays["p_all"] = np.stack([given[f"p_{b}"][0] for b in "abcd"])
    for name in _NAMES_2:
        arrays[name] = given[name][0]
    arrays["rope"] = rope_table()
    arrays["inv_count"] = edge_counts()
    arrays = {f"in_{k}_dram": np.ascontiguousarray(v) for k, v in arrays.items()}

    nc = _bacc.Bacc("TRN2", target_bir_lowering=False, num_devices=1)
    args = [nc.dram_tensor(k, a.shape, mybir.dt.from_np(a.dtype), kind="ExternalInput").ap() for k, a in arrays.items()]
    out = nc.dram_tensor("out_0_dram", (T, D), F32, kind="ExternalOutput").ap()
    build(nc, *args, out)
    rows = _run(nc, [arrays], core_ids=[0]).results[0]["out_0_dram"]
    return rows[:T_PROMPT].reshape(1, T_PROMPT, D), rows[T_PROMPT:].reshape(1, T_SAMPLE, D)
```

```python
import itertools
from contextlib import ExitStack

import numpy as np

import concourse.bass as bass
from concourse import mybir

F32 = mybir.dt.float32
U32 = mybir.dt.uint32
ALU = mybir.AluOpType
ACT = mybir.ActivationFunctionType
AX = mybir.AxisListType
ds = bass.ds

P = 128
T_PROMPT, T_SAMPLE = 1024, 256
T = T_PROMPT + T_SAMPLE
TILES = T // P
PAIRS = TILES // 2
PROMPT_PAIRS = T_PROMPT // P // 2
D = 1024
KD = D // P
W_BR = 512
KB = W_BR // P
HD = 64
N_Q, N_KV = 8, 2
N_QK = N_Q + N_KV
COL_U, COL_VG, COL_B = 0, 512, 1024
COL_C = 1536
COL_X, COL_BG, COL_CG = 2304, 2816, 3328
COL_G = 3840
WZ = 3 * 256 + 512
WINDOWS = (2, 4, 8, 16)
NE = 16
CAP_P, CAP_S = 2 * T_PROMPT // NE, 2 * T_SAMPLE // NE
CAP = CAP_P + CAP_S
ALPHA = 2.0 ** 0.25
LN_EPS = 1e-5
RMS_EPS = 1e-6
LAST = 5
BLOCKS = ((0, 512), (512, 512), (1024, 256))
NEG = -3.0e38


def wait_apart(eng, sem, value, met, count):
    if not isinstance(value, int):
        value = eng.snap(value)
    eng.wait_ge(met, count)
    eng.wait_ge(sem, value)


class Chain:

    def __init__(self, eng, sem):
        self.eng, self.sem, self.n, self.base = eng, sem, 0, 0

    def did(self, instruction):
        instruction.then_inc(self.sem, 1)
        self.n += 1

    def settle(self):
        self.eng.wait_ge(self.sem, self.base + self.n)


    def enter(self, i, per_turn):
        self.before, self.per = self.n, per_turn
        self.base, self.n = self.before + i * per_turn, 0

    def leave(self, turns):
        assert self.n == self.per, self.n
        self.base, self.n = 0, self.before + turns * self.per


def build(nc, x, c, w_ada, b_ada, w_in, a_ln_g, a_ln_b, a_ws, a_bs, b_wg, b_scale, c_q_g, c_k_g,
          d_conv, p_all, w_o, ln1_g, ln1_b, r_w, r_b, e_w1, e_w3, e_w2, ln2_g, ln2_b,
          rope, inv_count, out):
    with ExitStack() as ctx:
        def sb(name, shape, dt=F32):
            return ctx.enter_context(nc.sbuf_tensor(name, shape, dt))

        def sem(name):
            return ctx.enter_context(nc.semaphore(name))

        h2_rows = nc.dram_tensor("h2_rows", (T, D), F32, kind="Internal").ap()
        mod_rows = nc.dram_tensor("mod_rows", (2, 4 * D), F32, kind="Internal").ap()
        y_rows = nc.dram_tensor("y_rows", (T, D), F32, kind="Internal").ap()

        ident = sb("ident", [P, P])
        rows_in = sb("rows_in", [P, P])
        colT = sb("colT", [P, 80])
        modT = sb("modT", [P, 16, 2])
        c_pad = sb("c_pad", [P, KD, 32])
        every32 = sb("every32", [P, NE])
        mod2T = sb("mod2T", [P, 2, 32])
        aff_t = sb("aff_t", [P, 2, 2, NE])
        aff3 = sb("aff3", [P, 2, 96])
        rb_b = sb("rb_b", [P, NE])
        small = sb("small", [P, 64])
        half = sb("half", [P, 16])
        aff_t2 = sb("aff_t2", [P, 12])
        carry = sb("carry", [P, 2])
        carried = sb("carried", [P, 16])

        R1 = sb("R1", [P, 20480])
        RQ = sb("RQ", [P, 8960])
        RV = sb("RV", [P, 5120])
        RY = sb("RY", [P, 5120])
        RW = sb("RW", [P, 3072])
        RT = sb("RT", [P, 7040])
        RC = sb("RC", [P, 2048])

        pads_set = sb("pads_set", [P, 1])
        hT = R1[:, 0:10240].rearrange("p (k t) -> p k t", k=KD)
        merged = R1[:, 10240:20480].rearrange("p (k t) -> p k t", k=KD)
        wz = R1[:, 10240:20480].rearrange("p (k n) -> p k n", k=KD)
        w_ada_buf = [r.rearrange("p (k n) -> p k n", k=KD)
                     for r in (RV[:, 0:4096], RQ[:, 0:4096], R1[:, 0:4096], R1[:, 4096:8192])]
        part_sb = [RQ[:, 4096 + 512 * m:4608 + 512 * m] for m in range(2)]
        qT = RQ[:, 0:5120].rearrange("p (j t) -> p j t", j=4)
        kT = RQ[:, 5120:7680].rearrange("p (j t) -> p j t", j=2)
        va = RQ[:, 7680:8960].rearrange("p (t n) -> p t n", n=P)
        vln = RV[:, :].rearrange("p (t n) -> p t n", n=W_BR)
        y1 = RV[:, :].rearrange("p (k t) -> p k t", k=KB)
        y0 = RY[:, :].rearrange("p (k t) -> p k t", k=KB)
        w_tile = [RW[:, 1024 * s:1024 * s + 1024].rearrange("p (k n) -> p k n", k=KD) for s in range(2)]
        p_tile = [RW[:, 2048 + 512 * s:2560 + 512 * s].rearrange("p (k n) -> p k n", k=KB) for s in range(2)]
        x_in = [RY[:, 1024 * s:1024 * s + 1024] for s in range(2)]
        xh = [RY[:, 2048 + 1024 * s:3072 + 1024 * s] for s in range(2)]
        h_tile = [RW[:, 1024 * s:1024 * s + 1024].rearrange("p (k n) -> p k n", k=KD) for s in range(2)]
        v_gelu = [RW[:, 2048 + 512 * s:2560 + 512 * s] for s in range(2)]
        z_qkv = [RT[:, 768 * s:768 * s + 768] for s in range(2)]
        qk_out = [RT[:, 1536 + 768 * s:2304 + 768 * s] for s in range(2)]
        r_sq = RT[:, 3072:3712]
        r_n = RT[:, 3712:4352]
        r_a = RT[:, 4352:4672]
        r_b2 = RT[:, 4672:4992]
        gqk = RC[:, 0:640]
        cossin = RC[:, 640:1280].rearrange("p (t a n) -> p t a n", t=TILES, a=2)
        bs_b = RT[:, 6016:6528]
        lng_b = RT[:, 4992:5504]
        lnb_b = RT[:, 5504:6016]
        wsT = RC[:, 1280:1792].rearrange("p (g n) -> p g n", g=4)
        ws_in = RT[:, 6528:7040].rearrange("p (g n) -> p g n", g=4)

        PS = ctx.enter_context(nc.psum_tensor("PS", [P, 8, 512], F32))
        tp = [PS[:, 0:2, :].rearrange("p a (b n) -> p (a b) n", n=P),
              PS[:, 2:4, :].rearrange("p a (b n) -> p (a b) n", n=P)]
        z1, z2, z3 = PS[:, 4, :], PS[:, 5, 0:256], PS[:, 6, :]
        rows_ps = PS[:, 7, 0:80]
        part_ps = [PS[:, 5, :], PS[:, 7, :]]
        mod_ps = PS[:, 6, 0:32].rearrange("p (m g) -> p m g", g=2)
        ws_ps = PS[:, 4, :].rearrange("p (g n) -> p g n", g=4)

        res = [PS[:, 3 * r:3 * r + 3, :].rearrange("p a n -> p (a n)")[:, 0:T] for r in range(2)]
        sv_ps = [PS[:, 6 + s, :].rearrange("p (g n) -> p g n", g=4) for s in range(2)]
        PADDED = T + 32
        SEGS = ((8, 0, T_PROMPT), (T_PROMPT + 24, T_PROMPT, T_SAMPLE))
        z_pad = [RT[:, PADDED * s:PADDED * (s + 1)] for s in range(2)]
        sum_a, sum_b = (RT[:, PADDED * s:PADDED * (s + 1)] for s in (2, 3))
        gate_sb = RT[:, 5248:5248 + T]
        prod = RT[:, 0:T]
        CSEGS = ((1, 0, T_PROMPT), (T_PROMPT + 3, T_PROMPT, T_SAMPLE))
        cg_sb = RT[:, 1312:1312 + T]
        z_conv = RT[:, 2624:2624 + T + 4]
        taps = RT[:, 3936:3936 + T + 4]
        wg_sb = RC[:, 0:512].rearrange("p (g n) -> p g n", g=4)
        edge = RC[:, 1792:1920].rearrange("p (g e n) -> p g e n", g=4, e=4)
        s_ps = [PS[:, 2 * u:2 * u + 2, :].rearrange("p a n -> p (a n)") for u in range(2)]
        pt_ps = PS[:, 4:6, :].rearrange("p a (b n) -> p (a b) n", n=P)
        o_ps = [PS[:, 6 + u, 0:HD] for u in range(2)]
        part2_ps, part2_sb = PS[:, 6, 256:512], RT[:, 4608:4864]
        mod2_ps = PS[:, 6, 64:128].rearrange("p (g c) -> p g c", g=2)
        modr_ps = PS[0:64, 6, 128:256]
        oT_ps = PS[:, 7, :].rearrange("p (j n) -> p j n", j=4)
        o_row = RC[:, 0:512]
        w_mod = [RY[:, 2048 * s:2048 * s + 2048].rearrange("p (k n) -> p k n", k=KD) for s in range(2)]
        prob = [RT[:, 1024 * u:1024 * u + 1024] for u in range(2)]
        probT = [RT[:, 2048 + 1024 * u:3072 + 1024 * u].rearrange("p (b n) -> p b n", n=P) for u in range(2)]
        sums = small[:, 32:36]
        q_tile = RT[:, 4096:4608].rearrange("p (j n) -> p j n", j=4)

        row = lambda region, i: region[:, D * i:D * i + D]
        g1_b = [row(RY, 0), row(RY, 1)]
        sh2_b, sc2_b = [row(RY, 2), row(RT, 2)], [row(RY, 3), row(RT, 3)]
        ln1g_b, ln1b_b = row(RY, 4), row(RT, 4)
        x_row = [row(R1, s) for s in range(2)]
        x1_row = [row(R1, 2 + s) for s in range(2)]
        h2_row = [row(R1, 4 + s) for s in range(2)]
        h2T = [row(R1, 6 + s).rearrange("p (k n) -> p k n", k=KD) for s in range(2)]
        m_tile = [row(RC, s).rearrange("p (k n) -> p k n", k=KD) for s in range(2)]
        wo_sb = RQ[:, 0:8192].rearrange("p (k n) -> p k n", k=KD)
        flip = RQ[:, 8448:8576]
        rw_sb = RQ[:, 8192:8448].rearrange("p (k n) -> p k n", k=KD)
        xa_row = [row(RW, s) for s in range(2)]
        HALF = T_PROMPT // 2
        TK = 96
        affT = RT[0:TK, 0:HALF]
        y_ps = [PS[:, 2 * s:2 * s + 2, :].rearrange("p a n -> p (a n)") for s in range(2)]
        h2t_ps = PS[:, 4:6, :].rearrange("p a (b n) -> p (a b) n", n=P)
        logit_ps = PS[:, 6, 0:NE]
        lpart_ps, lpart_sb = PS[:, 6, 128:256], RT[:, 5120:5248]
        affT_ps = PS[0:TK, 7, 0:P]
        top_v, top_f = RT[0:TK, 512:640], RT[0:TK, 640:768]
        top_i = sb("top_i", [TK, CAP_P], U32)
        top_ranks = RT[:, 768:960].rearrange("p (a n) -> p a n", a=2)
        first_wins, index_gap = RT[:, 960:960 + NE], RT[:, 976:976 + NE]
        idx_p, idx_s = sb("idx_p", [P, NE], U32), sb("idx_s", [CAP_S, NE], U32)
        gate_p, gate_s = sb("gate_p", [P, NE]), sb("gate_s", [CAP_S, NE])
        g_idx_p, g_idx_s = sb("g_idx_p", [P, 1], U32), sb("g_idx_s", [CAP_S, 1], U32)
        s_idx_p, s_idx_s = sb("s_idx_p", [P, 1], U32), sb("s_idx_s", [CAP_S, 1], U32)
        top_ps = PS[:, 7, 0:2 * TK].rearrange("p (a n) -> p a n", a=2)
        flip_ps = PS[:, 6, 0:2 * NE].rearrange("p (a n) -> p a n", a=2)
        w_half = [RV[:, 0:4096].rearrange("p (k n) -> p k n", k=KD)]
        w_half += [R1[:, 4096 * c:4096 * c + 4096].rearrange("p (k n) -> p k n", k=KD) for c in (4, 3, 2, 1, 0)]
        xg_p, xg_s = RQ[:, 0:D], RQ[0:CAP_S, D:2 * D]
        xgT, gT, outT = (RQ[:, 2048 + 1280 * i:3328 + 1280 * i].rearrange("p (k n) -> p k n", k=KD) for i in range(3))
        out_p, out_s = RQ[:, 5888:6912], RQ[0:CAP_S, 6912:7936]
        silu = [RQ[:, 7936 + CAP * s:7936 + CAP * (s + 1)] for s in range(2)]
        xt_p = PS[:, 0:2, :].rearrange("p a (b n) -> p (a b) n", n=P)
        xt_s = PS[:, 2, 0:KD * CAP_S].rearrange("p (k n) -> p k n", k=KD)
        ab_ps = [PS[:, 3 + s, 0:2 * CAP].rearrange("p (a n) -> p a n", a=2) for s in range(2)]
        op_ps = PS[:, 5:7, :].rearrange("p a n -> p (a n)")
        os_ps = [PS[0:CAP_S, 7, :], PS[0:CAP_S, 2, :]]
        ln2g_b, ln2b_b = row(RY, 0), row(RY, 1)
        y_in = [row(R1, s) for s in range(LAST)]
        y_out = [row(R1, LAST + s) for s in range(LAST)]

        s_m2, s_m2T, s_m2r, s_m2c, s_mout = (sem(n) for n in ("s_m2", "s_m2T", "s_m2r", "s_m2c", "s_mout"))
        s_wm = [sem("s_wm0"), sem("s_wm1")]
        s_rows2, s_wo, s_xs = sem("s_rows2"), sem("s_wo"), sem("s_xs")
        s_xr = [sem("s_xr0"), sem("s_xr1")]
        s_yo, s_h2o = [sem("s_yo0"), sem("s_yo1")], [sem("s_h2o0"), sem("s_h2o1")]
        s_mt, s_y, s_yr, s_xa, s_st2, s_rs2, s_x1, s_h2 = (
            sem(n) for n in ("s_mt", "s_y", "s_yr", "s_xa", "s_st2", "s_rs2", "s_x1", "s_h2"))
        s_et, s_h2T, s_lg, s_sm, s_se, s_aff, s_at, s_affT = (
            sem(n) for n in ("s_et", "s_h2T", "s_lg", "s_sm", "s_se", "s_aff", "s_at", "s_affT"))
        s_top, s_topT, s_rank, s_flip, s_idx = (sem(n) for n in ("s_top", "s_topT", "s_rank", "s_flip", "s_idx"))
        s_fill, s_rwz, s_lp, s_lpc, s_mt0 = sem("s_fill"), sem("s_rwz"), sem("s_lp"), sem("s_lpc"), sem("s_mt0")
        s_wx = [sem(f"s_wx{c}") for c in range(6)]
        s_xg, s_xt, s_xe, s_xes, s_ab, s_si, s_g, s_o, s_oT, s_ot, s_op, s_os, s_sc = (
            sem(n) for n in ("s_xg", "s_xt", "s_xe", "s_xes", "s_ab", "s_si", "s_g", "s_o", "s_oT", "s_ot", "s_op", "s_os", "s_sc"))
        s_fx, s_done = [sem(f"s_fx{s}") for s in range(LAST)], [sem(f"s_done{s}") for s in range(LAST)]
        s_st3, s_rs3, s_fn, s_fs, s_fo, s_ln2 = (sem(n) for n in ("s_st3", "s_rs3", "s_fn", "s_fs", "s_fo", "s_ln2"))

        s_w, s_p = [sem("s_w0"), sem("s_w1")], [sem("s_p0"), sem("s_p1")]
        s_f, s_fe = [sem("s_f0"), sem("s_f1")], [sem("s_fe0"), sem("s_fe1")]
        s_sv, s_sve, s_ya = sem("s_sv"), sem("s_sve"), sem("s_ya")
        s_pool, s_mg, s_pads = (sem(n) for n in ("s_pool", "s_mg", "s_pads"))
        s_wg = sem("s_wg")
        s_qb, s_qk, s_mx, s_exp, s_pt, s_pte, s_pv, s_oe, s_otp, s_oc = (
            sem(n) for n in ("s_qb", "s_qk", "s_mx", "s_exp", "s_pt", "s_pte", "s_pv", "s_oe", "s_otp", "s_oc"))

        N_U, N_B, N_MA, N_D, N_MB, N_MD, N_MC = 0, 4, 8, 16, 28, 36, 44
        R_U, R_B, R_MA, R_MIX, R_D, R_MB, R_MD, R_MC, R_END = 0, 4, 8, 24, 28, 40, 56, 72, 88
        MERGES = {"A": (N_MA, R_MA, 0, 0, y0), "B": (N_MB, R_MB, 1, 8, y1),
                  "D": (N_MD, R_MD, 3, 16, y0), "C": (N_MC, R_MC, 2, 24, y1)}

        s_id0, s_id = sem("s_id0"), sem("s_id")
        s_rows, s_silu, s_rT, s_col = sem("s_rows"), sem("s_silu"), sem("s_rT"), sem("s_col")
        s_wada = [sem(f"s_wada{m}") for m in range(4)]
        s_cpad, s_modp, s_modc, s_m2p, s_m2s = (sem(n) for n in ("s_cpad", "s_modp", "s_modc", "s_m2p", "s_m2s"))
        s_modmm, s_mod = sem("s_modmm"), sem("s_mod")
        s_const = sem("s_const")
        s_wz = [sem("s_wz0"), sem("s_wz1")]
        s_gqk = sem("s_gqk")
        s_ws, s_wsT = sem("s_ws"), sem("s_wsT")
        s_x = [sem("s_xin0"), sem("s_xin1")]
        s_stat, s_rs, s_xh, s_tp, s_ht, s_hc = (sem(n) for n in ("s_stat", "s_rs", "s_xh", "s_tp", "s_ht", "s_hc"))
        s_z1, s_z2, s_z3, s_zc, s_vg = (sem(n) for n in ("s_z1", "s_z2", "s_z3", "s_zc", "s_vg"))
        s_qr, s_vn, s_vl, s_qt, s_qe = (sem(n) for n in ("s_qr", "s_vn", "s_vl", "s_qt", "s_qe"))
        own_v, own_p, own_a = sem("own_v"), sem("own_p"), sem("own_a")
        s_out = sem("s_out")
        block = ctx.enter_context(nc.Block())

        def ln_cols(which, s):
            return small[:, 16 * which + 8 * s:16 * which + 8 * s + 8]

        def all_tiles(eng, attend, mark=None):
            n_p = T_PROMPT // P
            for keys, t0, t1 in ((T_PROMPT, 0, n_p), (T_SAMPLE, n_p, TILES)):
                attend(t0, keys, first=True)
                if t1 - t0 > 2:
                    with eng.Fori(t0 + 1, t1 - 1) as t:
                        if mark:
                            mark.enter(t - t0 - 1, mark.per_tile)
                        attend(t, keys)
                        if mark:
                            mark.leave(t1 - t0 - 2)
                attend(t1 - 1, keys, last=True)

        @block.sync
        def _(sp):
            sp.dma_start(rows_in[0:16, :], c.rearrange("g (k n) -> (g k) n", n=P)).then_inc(s_rows, 16)
            sp.dma_start(rows_in[16:64, :], b_ada.rearrange("(k n) -> k n", n=P)).then_inc(s_rows, 16)
            sp.dma_start(rows_in[64:76, :], d_conv.rearrange("j (k n) -> (j k) n", n=P)).then_inc(s_rows, 16)
            sp.dma_start(rows_in[76:80, :], b_scale.rearrange("(k n) -> k n", n=P)).then_inc(s_rows, 16)
            for m in range(4):
                sp.dma_start(w_ada_buf[m], w_ada[:, 512 * m:512 * m + 512].rearrange("(k p) n -> p k n", p=P)) \
                  .then_inc(s_wada[m], 16)
                if m < 2:
                    sp.dma_start(x_in[m], x[m * P:(m + 1) * P, :]).then_inc(s_x[m], 16)
            sp.dma_start(wz[:, :, 0:768], w_in[:, COL_C:COL_C + 768].rearrange("(k p) n -> p k n", p=P)).then_inc(s_wz[0], 16)
            sp.dma_start(ws_in, a_ws.rearrange("g p q -> p g q")).then_inc(s_ws, 16)
            sp.dma_start(wz[:, :, 768:1280], w_in[:, COL_VG:COL_VG + 512].rearrange("(k p) n -> p k n", p=P)).then_inc(s_wz[1], 16)
            with sp.Fori(1, PAIRS) as i:
                for s in range(2):
                    sp.wait_ge(s_xh, 2 * i + s - 1)
                    sp.dma_start(x_in[s], x[ds(i * 256 + s * P, P), :]).then_inc(s_x[s], 16)

            def load_w(slot, cols, r_before, count=None):
                if r_before is not None:
                    sp.wait_ge(s_f[r_before % 2], r_before // 2 + 1 if count is None else count)
                sp.dma_start(w_tile[slot], w_in[:, ds(cols, P)].rearrange("(k p) n -> p k n", p=P)).then_inc(s_w[slot], 16)

            sp.wait_ge(s_z3, TILES)
            sp.wait_ge(s_hc, TILES)
            sp.wait_ge(s_vn, TILES)
            sp.wait_ge(s_qr, TILES)
            sp.dma_start(wg_sb, b_wg.rearrange("g c d -> c g d")).then_inc(s_wg, 16)
            for j in range(4):
                load_w(j % 2, COL_U + P * j, j - 2 if j >= 2 else None)
            for j in range(4):
                load_w(j % 2, COL_B + P * j, R_B + j - 2)

            def load_merge(name, r_last, between=None):
                n0, r0, branch, m0, _ = MERGES[name]

                def turn(i, first):
                    for s in range(2):
                        col = COL_G + branch * D + s * P
                        load_w(s, col + i * 256, r_last[s] if first else 0, None if first else r0 // 2 + 2 * i + s - 1)
                        if not first:
                            wait_apart(sp, s_f[1], r0 // 2 + 2 * i + s - 1, s_wg, 16)
                        elif m0:
                            sp.wait_ge(s_f[1], r_proj + s)
                        sp.dma_start(p_tile[s], p_all[branch, :, ds(i * 256 + s * P, P)].rearrange("(k p) n -> p k n", p=P)) \
                          .then_inc(s_p[s], 16)

                r_proj = {"A": 0, "B": R_MA // 2 + 7, "D": R_MB // 2 + 7, "C": R_MD // 2 + 7}[name]
                turn(0, True)
                if between:
                    between()
                with sp.Fori(1, 4) as i:
                    turn(i, False)

            def load_mod(first, end):
                with sp.Fori(first, end) as i:
                    for s in range(2):
                        sp.wait_ge(s_m2, 2 * i + s - 1)
                        sp.dma_start(w_mod[s], w_ada[:, ds(i * 512 + 2 * D + 256 * s, 256)].rearrange("(k p) n -> p k n", p=P)) \
                          .then_inc(s_wm[s], 16)

            load_merge("A", (R_B + 2, R_B + 3))
            for j in range(4):
                for m, col in enumerate((COL_CG, COL_X, COL_BG)):
                    n = 3 * j + m
                    load_w(n % 2, col + P * j, R_MA + 12 + 2 * n if n < 2 else R_D + n - 2)
            load_merge("B", (R_D + 10, R_D + 11))
            load_merge("D", (R_MB + 12, R_MB + 14))
            sp.wait_ge(s_f[1], R_MC // 2)
            for s in range(2):
                sp.dma_start(w_mod[s], w_ada[:, 2 * D + 256 * s:2 * D + 256 * s + 256].rearrange("(k p) n -> p k n", p=P)) \
                  .then_inc(s_wm[s], 16)
            load_mod(1, 8)

            def everywhere(dst, src):
                return sp.dma_start(dst, src.rearrange("(a n) -> a n", a=1).to_broadcast([P, D]))

            def load_rows():
                sp.wait_ge(s_m2c, 1)
                sp.dma_start(mod_rows.rearrange("g (k n) -> (g k) n", n=P), rows_in[0:64, :]).then_inc(s_mout, 16)
                sp.wait_ge(s_pv, N_Q * TILES)
                sp.dma_start(wo_sb, w_o.rearrange("(k p) n -> p k n", p=P)).then_inc(s_wo, 16)
                sp.wait_ge(s_rwz, 1)
                sp.dma_start(rw_sb[:, :, 0:NE], r_w.rearrange("(k p) n -> p k n", p=P)).then_inc(s_wo, 16)
                sp.wait_ge(s_mout, 16)
                for g in range(2):
                    for j, dst in enumerate((g1_b, sh2_b, sc2_b)):
                        everywhere(dst[g], mod_rows[g, D * j:D * j + D]).then_inc(s_rows2, 16)
                everywhere(ln1g_b, ln1_g).then_inc(s_rows2, 16)
                everywhere(ln1b_b, ln1_b).then_inc(s_rows2, 16)

            load_merge("C", (R_MD + 12, R_MD + 14), load_rows)

            sp.wait_ge(s_f[0], R_END // 2)
            for s in range(2):
                sp.dma_start(x_row[s], x[s * P:(s + 1) * P, :]).then_inc(s_xr[s], 16)

            def rows_turn(i, more):
                for s in range(2):
                    t = 2 * i + s
                    at = sp.snap(256 * i + P * s) if not isinstance(i, int) else 256 * i + P * s
                    if more:
                        sp.wait_ge(s_xa, t + 1)
                        sp.dma_start(x_row[s], x[ds(at + 256, P), :]).then_inc(s_xr[s], 16)
                    sp.wait_ge(s_xs, t + 1)
                    sp.dma_start(y_rows[ds(at, P), :], xa_row[s]).then_inc(s_yo[s], 16)
                    sp.wait_ge(s_h2, t + 1)
                    sp.dma_start(h2_rows[ds(at, P), :], h2_row[s]).then_inc(s_h2o[s], 16)

            HALVES = ((e_w1, 0), (e_w3, 0), (e_w1, 512), (e_w3, 512), (e_w2, 0), (e_w2, 512))

            def load_half(e, c):
                w, lo = HALVES[c]
                sp.dma_start(w_half[c], w[ds(e, 1), :, lo:lo + 512].rearrange("a (k p) n -> p (a k) n", p=P)) \
                  .then_inc(s_wx[c], 16)

            sp.wait_ge(s_f[1], R_END // 2)
            load_half(0, 0)
            with sp.Fori(0, PAIRS - 1) as i:
                rows_turn(i, True)
            sp.wait_ge(s_mt, TILES - 1)
            for part in (1, 2):
                load_half(0, part)
            rows_turn(PAIRS - 1, False)
            sp.wait_ge(s_aff, TILES)
            sp.wait_ge(s_at, TILES)
            for s in range(2):
                sp.wait_ge(s_yo[s], 16 * PAIRS)
                sp.wait_ge(s_h2o[s], 16 * PAIRS)
            for part in (3, 4, 5):
                load_half(0, part)
            everywhere(ln2g_b, ln2_g).then_inc(s_ln2, 16)
            everywhere(ln2b_b, ln2_b).then_inc(s_ln2, 16)
            with sp.Fori(1, NE) as e:
                for part, (done, n) in enumerate(((s_ab, 4), (s_ab, 4), (s_ab, 8), (s_ab, 8), (s_o, 4), (s_o, 8))):
                    sp.wait_ge(done, 8 * e - 8 + n)
                    load_half(e, part)

            sp.wait_ge(s_sc, 32 * NE)
            for s in range(LAST):
                sp.dma_start(y_in[s], y_rows[P * s:P * s + P, :]).then_inc(s_fx[s], 16)

            def store_last(i, more):
                for s in range(LAST):
                    t = LAST * i + s
                    if more:
                        sp.wait_ge(s_fn, t + 1)
                        sp.dma_start(y_in[s], y_rows[P * (t + LAST):P * (t + LAST) + P, :]).then_inc(s_fx[s], 16)
                    sp.wait_ge(s_fo, t + 1)
                    sp.dma_start(out[P * t:P * t + P, :], y_out[s]).then_inc(s_done[s], 16)

            store_last(0, True)
            store_last(1, False)
            for s in range(LAST):
                sp.wait_ge(s_done[s], 32)

        @block.gpsimd
        def _(pool):
            own = Chain(pool, own_p)
            columns = itertools.cycle(range(16))

            def carrier():
                at = next(columns)
                own.did(pool.tensor_tensor(carried[:, at:at + 1], half[:, 0:1], half[:, 1:2], ALU.add))

            pool.memset(ident[:, :], 0.0).then_inc(s_id0, 1)
            own.did(pool.memset(half[:, :], -0.5))
            pool.wait_ge(s_id0, 1)
            pool.affine_select(out=ident[:, :], in_=ident[:, :], compare_op=ALU.not_equal, fill=1.0,
                               base=0, pattern=[[-1, P]], channel_multiplier=1).then_inc(s_id, 1)
            pool.dma_start(cossin, rope).then_inc(s_const, 16)
            pool.dma_start(gqk[:, 0:HD], c_q_g.rearrange("(a n) -> a n", a=1).to_broadcast([P, HD])).then_inc(s_const, 16)
            pool.dma_start(gqk[:, 512:512 + HD], c_k_g.rearrange("(a n) -> a n", a=1).to_broadcast([P, HD])).then_inc(s_const, 16)
            pool.dma_start(lng_b, a_ln_g.rearrange("(a n) -> a n", a=1).to_broadcast([P, W_BR])).then_inc(s_const, 16)
            pool.dma_start(lnb_b, a_ln_b.rearrange("(a n) -> a n", a=1).to_broadcast([P, W_BR])).then_inc(s_const, 16)
            pool.dma_start(bs_b, a_bs.rearrange("g p -> (g p)").rearrange("(a n) -> a n", a=1).to_broadcast([P, W_BR])).then_inc(s_const, 16)
            pool.dma_start(rb_b[:, :], r_b.rearrange("(a n) -> a n", a=1).to_broadcast([P, NE])).then_inc(s_const, 16)
            pool.dma_start(edge, inv_count.rearrange("g e n -> (g e n)").rearrange("(a n) -> a n", a=1).to_broadcast([P, 128])).then_inc(s_const, 16)
            def power(cols, n, t_sem, count):
                pool.wait_ge(t_sem, count)
                pool.tensor_tensor(cols, cols, half[:, 0:n], ALU.pow).then_inc(s_rs, 1)

            def turn(i, ahead, front=False):
                for s in range(2):
                    t = 2 * i + s
                    n0 = 3 * t + 2
                    power(small[:, 32 + 16 * s:42 + 16 * s], N_QK, s_stat, n0 + 1 if ahead else 3 * t + 3 - s)
                    if ahead:
                        power(ln_cols(0, s)[:, 7:8], 1, s_stat, n0 + 2)
                    pool.wait_ge(s_ht, t + 1)
                    pool.tensor_copy(hT[:, :, ds(i * 256 + s * P, P)], h_tile[s]).then_inc(s_hc, 1)
                    power(ln_cols(1, s)[:, 7:8], 1, s_stat, n0 + 3 if ahead else 3 * t + 4 - s)
                    pool.wait_ge(s_vn, t + 1)
                    carrier()
                    v = vln[:, ds(t, 1), :].rearrange("p a n -> p (a n)")
                    own.did(pool.tensor_tensor(v, v, lng_b, ALU.mult))
                    own.settle()
                    carrier()
                    pool.tensor_tensor(v, v, lnb_b, ALU.add).then_inc(s_vl, 1)

            own.settle()
            power(ln_cols(0, 0)[:, 7:8], 1, s_stat, 1)
            power(ln_cols(0, 1)[:, 7:8], 1, s_stat, 2)
            pool.wait_ge(s_const, 8 * 16)
            for h in range(1, N_Q):
                own.did(pool.tensor_copy(gqk[:, h * HD:(h + 1) * HD], gqk[:, 0:HD]))
            pool.tensor_copy(gqk[:, 576:640], gqk[:, 512:576]).then_inc(s_gqk, 1)
            own.settle()

            with pool.Fori(0, PAIRS - 1) as i:
                own.enter(i, 6)
                turn(i, True)
                own.leave(PAIRS - 1)
            turn(PAIRS - 1, False)
            pool.wait_ge(s_qe, TILES)
            for s in range(2):
                pool.wait_ge(s_fe[s], R_MB // 2)
            for j in range(4):
                pool.tensor_copy(q_tile[:, j, :], qT[:, j, 0:P]).then_inc(s_qb, 1)
            with pool.Fori(1, TILES) as t:
                for j in range(4):
                    pool.wait_ge(s_mg, 16)
                    pool.wait_ge(s_qk, N_Q * t + 2 * j - 6)
                    pool.tensor_copy(q_tile[:, j:j + 1, :], qT[:, j:j + 1, ds(t * P, P)]).then_inc(s_qb, 1)

            def power2(s_stat_, s_rs_, cols, count):
                pool.wait_ge(s_stat_, count)
                pool.tensor_tensor(cols[:, 7:8], cols[:, 7:8], half[:, 0:1], ALU.pow).then_inc(s_rs_, 1)

            def take(i, s):
                carrier()
                pool.tensor_copy(m_tile[s], merged[:, :, ds(256 * i + P * s, P)]).then_inc(s_mt, 1)

            pool.wait_ge(s_pv, N_Q * TILES)
            pool.memset(rw_sb, 0.0).then_inc(s_rwz, 1)
            own.did(pool.memset(flip, 0.0))
            own.settle()
            pool.affine_select(out=flip, in_=flip, compare_op=ALU.not_equal, fill=1.0,
                               base=1 - P, pattern=[[1, P]], channel_multiplier=1).then_inc(s_id, 1)
            pool.wait_ge(s_mg, 24)
            take(0, 1)

            def rows_turn(i, more):
                for s in range(2):
                    t = 2 * i + s
                    power2(s_st2, s_rs2, ln_cols(1, s), 2 * t + 1)
                    power2(s_st2, s_rs2, ln_cols(2, s), 2 * t + 2)
                    if more:
                        pool.wait_ge(s_y, t + 1)
                        take(i + 1, s)

            with pool.Fori(0, PAIRS - 1) as i:
                own.enter(i, 2)
                rows_turn(i, True)
                own.leave(PAIRS - 1)
            rows_turn(PAIRS - 1, False)

            def indexed(e, pairs, wait, count):
                pool.wait_ge(wait, count)
                carrier()
                for dst, src in pairs:
                    own.did(pool.tensor_copy(dst, src[:, ds(e, 1)]))
                own.settle()
                carrier()

            def gather(e, wait, count):
                indexed(e, ((g_idx_p[:, :], idx_p), (g_idx_s[:, :], idx_s)), wait, count)
                for dst, idx in ((xg_p, g_idx_p), (xg_s, g_idx_s)):
                    pool.indirect_dma_start(out=dst, out_offset=None, in_=h2_rows,
                                            in_offset=bass.IndirectOffsetOnAxis(ap=idx[:, 0:1], axis=0)).then_inc(s_xg, 16)

            def scatter(e, first=False):
                if not first:
                    pool.wait_ge(s_sc, 32 * e)
                    carrier()
                pool.wait_ge(s_op, e + 1)
                carrier()
                indexed(e, ((s_idx_p[:, :], idx_p), (s_idx_s[:, :], idx_s)), s_os, e + 1)
                for src, idx in ((out_p, s_idx_p), (out_s, s_idx_s)):
                    pool.indirect_dma_start(out=y_rows, out_offset=bass.IndirectOffsetOnAxis(ap=idx[:, 0:1], axis=0),
                                            in_=src, in_offset=None, compute_op=ALU.add).then_inc(s_sc, 16)

            for s in range(2):
                pool.wait_ge(s_h2o[s], 16 * PAIRS)
                pool.wait_ge(s_yo[s], 16 * PAIRS)
            pool.wait_ge(s_topT, 1)
            gather(0, s_idx, 4)
            gather(1, s_xt, 1)
            scatter(0, True)
            n = own.n
            gather(2, s_xt, 2)
            scatter(1)
            per = own.n - n
            with pool.Fori(2, NE - 1) as e:
                own.enter(e - 2, per)
                gather(e + 1, s_xt, e + 1)
                scatter(e)
                own.leave(NE - 3)
            scatter(NE - 1)

            pool.wait_ge(s_ln2, 32)
            power2(s_st3, s_rs3, ln_cols(1, 0), 1)
            for t in range(TILES):
                if t + 1 < TILES:
                    power2(s_st3, s_rs3, ln_cols(1, (t + 1) % 2), t + 2)
                pool.wait_ge(s_fs, t + 1)
                pool.tensor_tensor(y_out[t % LAST], y_out[t % LAST], ln2b_b, ALU.add).then_inc(s_fo, 1)

        @block.scalar
        def _(act):
            act.wait_ge(s_rows, 64)
            act.activation(rows_in[0:16, :], rows_in[0:16, :], ACT.Silu).then_inc(s_silu, 1)

            for m in range(4):
                act.wait_ge(s_modp, m + 1)
                if m >= 2:
                    act.wait_ge(s_modmm, m - 1)
                act.activation(part_sb[m % 2], part_ps[m % 2], ACT.Copy).then_inc(s_modc, 1)

            def modulate(i, s, group):
                t = 2 * i + s
                act.wait_ge(s_tp, t + 1)
                if not (isinstance(i, int) and i == 0):
                    act.wait_ge(s_z3, t - 1)
                    act.wait_ge(s_hc, t - 1)
                for k in range(KD):
                    last = act.activation(h_tile[s][:, k, :], tp[s][:, k, :], ACT.Identity,
                                          bias=modT[:, k, group:group + 1],
                                          scale=modT[:, 8 + k, group:group + 1])
                last.then_inc(s_ht, 1)

            def keep_qk(i, s):
                act.wait_ge(s_qt, 2 * i + s + 1)
                act.activation(qT[:, :, ds(i * 256 + s * P, P)], tp[s][:, 0:4, :], ACT.Copy)
                act.activation(kT[:, :, ds(i * 256 + s * P, P)], tp[s][:, 4:6, :], ACT.Copy).then_inc(s_qe, 1)

            def turn(i, group):
                first = isinstance(i, int) and i == 0
                for s in range(2):
                    t = 2 * i + s
                    act.wait_ge(s_z1, t + 1)
                    if not first:
                        act.wait_ge(s_qr, t - 1)
                    act.activation(z_qkv[s][:, 0:512], z1, ACT.Copy).then_inc(s_zc, 1)
                    if s == 0 and not first:
                        keep_qk(i - 1, 0)
                    act.wait_ge(s_z2, t + 1)
                    act.activation(z_qkv[s][:, 512:768], z2, ACT.Copy).then_inc(s_zc, 1)
                    if s == 1 and group is not None:
                        modulate(i + 1, 0, group)
                    act.wait_ge(s_z3, t + 1)
                    if not first:
                        act.wait_ge(s_vn, t - 1)
                    act.activation(v_gelu[s], z3, ACT.Gelu_apprx_tanh).then_inc(s_vg, 1)
                    if s == 0 and not first:
                        keep_qk(i - 1, 1)
                    if s == 1 and group is not None:
                        modulate(i + 1, 1, group)

            act.wait_ge(s_mod, 1)
            for s in range(2):
                modulate(0, s, 0)
            turn(0, 0)
            with act.Fori(1, PROMPT_PAIRS - 1) as i:
                turn(i, 0)
            turn(PROMPT_PAIRS - 1, 1)
            turn(PROMPT_PAIRS, None)
            for s in range(2):
                keep_qk(PAIRS - 1, s)

            act.wait_ge(s_tp, TILES)
            act.wait_ge(s_xh, TILES)
            for j in range(4):
                act.wait_ge(s_f[j % 2], j // 2 + 1)
                act.activation(y0[:, j, :], res[j % 2], ACT.Gelu_apprx_tanh).then_inc(s_fe[j % 2], 1)
            act.wait_ge(s_pads, 1)
            for g in range(4):
                r = R_B + g
                act.wait_ge(s_f[r % 2], r // 2 + 1)
                if g >= 2:
                    act.wait_ge(s_pool, g - 1)
                for at, lo, n in SEGS:
                    last = act.activation(z_pad[g % 2][:, at:at + n], res[r % 2][:, lo:lo + n], ACT.Copy)
                last.then_inc(s_fe[r % 2], 1)

            def gates(name):
                _, r0, _, m0, _ = MERGES[name]

                def turn(i, first):
                    for s in range(2):
                        act.wait_ge(s_f[0], r0 // 2 + 2 * i + s + 1)
                        act.wait_ge(s_fe[1], r0 // 2 + 2 * i + s)
                        act.activation(gate_sb, res[0], ACT.Sigmoid).then_inc(s_fe[0], 1)

                turn(0, True)
                with act.Fori(1, 4) as i:
                    turn(i, False)

            gates("A")
            for g in range(4):
                r = R_MIX + g
                act.wait_ge(s_f[r % 2], r // 2 + 1)
                act.activation(y1[:, g, :], res[r % 2], ACT.Copy, scale=colT[:, 76 + g:77 + g]).then_inc(s_fe[r % 2], 1)
            for j in range(4):
                r = R_D + 3 * j
                act.wait_ge(s_f[r % 2], r // 2 + 1)
                if j == 0:
                    act.wait_ge(s_pool, 4)
                else:
                    act.wait_ge(s_fe[(r - 2) % 2], (r - 2) // 2 + 1)
                act.activation(cg_sb, res[r % 2], ACT.Copy).then_inc(s_fe[r % 2], 1)
            gates("B")
            gates("D")

            def attend(t, keys, first=False, last=False):
                n = N_Q * t

                def exp(h):
                    u = h % 2
                    act.wait_ge(s_mx, n + h + 1)
                    if not (isinstance(t, int) and t == 0 and h < 2):
                        act.wait_ge(s_pt, n + h - 1)
                    act.activation(prob[u][:, 0:keys], s_ps[u][:, 0:keys], ACT.Exp,
                                   bias=small[:, u:u + 1], scale=HD ** -0.5,
                                   accum_out=sums[:, h % 4:h % 4 + 1]).then_inc(s_exp, 1)

                if first:
                    exp(0)
                for h in range(N_Q):
                    if h + 1 < N_Q or not last:
                        exp(h + 1)
                    act.wait_ge(s_pt, n + h + 1)
                    if not (isinstance(t, int) and t == 0 and h < 2):
                        act.wait_ge(s_pv, n + h - 1)
                    act.activation(probT[h % 2][:, 0:keys // P, :], pt_ps[:, 0:keys // P, :], ACT.Copy).then_inc(s_pte, 1)

            all_tiles(act, attend)
            act.wait_ge(s_m2r, 1)
            act.activation(rows_in[0:64, :], modr_ps, ACT.Copy).then_inc(s_m2c, 1)
            gates("C")

            def route(part, t):
                s = t % 2
                if part == "x1":
                    act.wait_ge(s_x1, t + 1)
                    if t >= 2:
                        act.wait_ge(s_yo[s], 8 * (t - s))
                    act.activation(xa_row[s], x1_row[s], ACT.Copy, scale=ALPHA).then_inc(s_xs, 1)
                elif part == "h":
                    act.wait_ge(s_et, t + 1)
                    act.activation(h2T[s], h2t_ps, ACT.Copy).then_inc(s_h2T, 1)
                elif part == "part":
                    act.wait_ge(s_lp, t + 1)
                    act.activation(lpart_sb, lpart_ps, ACT.Copy).then_inc(s_lpc, 1)
                elif part == "aff":
                    act.wait_ge(s_at, t + 1)
                    row, col = t * P // HALF * 32, t * P % HALF
                    act.activation(affT[row:row + NE, col:col + P], affT_ps[row:row + NE, :], ACT.Copy).then_inc(s_affT, 1)
                else:
                    act.wait_ge(s_sm, t + 1)
                    act.activation(aff_t[:, s, 1, :], aff_t[:, s, 0, :], ACT.Exp, bias=small[:, 2 * s:2 * s + 1],
                                   accum_out=small[:, 2 * s + 1:2 * s + 2]).then_inc(s_se, 1)

            act.wait_ge(s_f[1], R_END // 2)
            act.wait_ge(s_mg, 24)
            act.activation(m_tile[0], merged[:, :, 0:P], ACT.Copy).then_inc(s_mt0, 1)
            act.wait_ge(s_fill, 1)
            route("x1", 0)
            for t in range(TILES):
                route("h", t)
                if t:
                    route("exp", t - 1)
                if t + 1 < TILES:
                    route("x1", t + 1)
                route("part", t)
                if t:
                    route("aff", t - 1)
            route("exp", TILES - 1)
            route("aff", TILES - 1)

            def expert(e, more):
                for j in range(KD):
                    act.wait_ge(s_ab, 8 * e + j + 1)
                    if not (isinstance(e, int) and e == 0 and j < 2):
                        act.wait_ge(s_g, 8 * e + j - 1)
                    act.activation(silu[j % 2], ab_ps[j % 2][:, 0, :], ACT.Silu).then_inc(s_si, 1)
                if more:
                    act.wait_ge(s_xt, e + 2)
                    act.activation(xgT[:, :, 0:CAP_P], xt_p, ACT.Copy).then_inc(s_xe, 1)
                act.wait_ge(s_ot, e + 1)
                if not (isinstance(e, int) and e == 0):
                    act.wait_ge(s_sc, 32 * e)
                act.activation(out_p, op_ps, ACT.Copy, scale=gate_p[:, ds(e, 1)]).then_inc(s_op, 1)

            act.wait_ge(s_xt, 1)
            act.activation(xgT[:, :, 0:CAP_P], xt_p, ACT.Copy).then_inc(s_xe, 1)
            act.wait_ge(s_idx, 4)
            expert(0, True)
            with act.Fori(1, NE - 1) as e:
                expert(e, True)
            expert(NE - 1, False)

            for t in range(TILES):
                act.wait_ge(s_rs3, t + 1)
                act.wait_ge(s_fn, t + 1)
                act.activation(y_out[t % LAST], y_out[t % LAST], ACT.Copy, scale=ln_cols(1, t % 2)[:, 7:8]).then_inc(s_fs, 1)

        @block.vector
        def _(dve):
            own = Chain(dve, own_v)

            def norm_stats(src, cols, bn, n):
                for j in range(n // 512):
                    own.did(dve.bn_stats(bn[:, 6 * j:6 * j + 6], src[:, 512 * j:512 * j + 512]))
                own.settle()
                own.did(dve.tensor_copy(carry[:, 0:1], half[:, 0:1]))
                own.did(dve.bn_aggr(cols[:, 0:2], bn[:, 0:6 * (n // 512)]))
                own.settle()
                dve.tensor_scalar(cols[:, 7:8], cols[:, 1:2], LN_EPS, None, ALU.add).then_inc(s_stat, 1)

            bn = aff_t[:, 0, 0, 0:12]

            def ln_x_stats(i, s, n_loads):
                dve.wait_ge(s_x[s], n_loads)
                norm_stats(x_in[s], ln_cols(0, s), bn, D)

            def ln_x_apply(s, tile_before, rs_count, first):
                dve.wait_ge(s_rs, rs_count)
                if not first:
                    dve.wait_ge(s_tp, tile_before)
                cols = ln_cols(0, s)
                dve.tensor_scalar(xh[s], x_in[s], cols[:, 0:1], cols[:, 7:8], ALU.subtract, ALU.mult).then_inc(s_xh, 1)

            dve.wait_ge(s_rT, 1)
            dve.wait_ge(own_p, 1)
            dve.tensor_copy(colT[:, :], rows_ps).then_inc(s_col, 1)
            own.did(dve.memset(c_pad[:, :, :], 0.0))
            own.settle()
            dve.wait_ge(s_col, 1)
            own.did(dve.tensor_copy(c_pad[:, :, 0:2], colT[:, 0:16].rearrange("p (g k) -> p k g", g=2)))
            dve.wait_ge(s_id, 1)
            own.settle()
            dve.tensor_reduce(every32[:, :], ident[:, :].rearrange("p (a n) -> p n a", n=32)[:, 0:NE, :], AX.X, ALU.add).then_inc(s_cpad, 1)
            for s in range(2):
                ln_x_stats(0, s, 16)
                ln_x_apply(s, 0, s + 1, True)
            dve.wait_ge(s_modmm, 4)
            dve.wait_ge(s_col, 1)
            own.did(dve.tensor_tensor(modT[:, :, :], mod_ps, colT[:, 16:32].unsqueeze(2).to_broadcast([P, 16, 2]), ALU.add))
            own.settle()
            dve.tensor_scalar(modT[:, 8:16, :], modT[:, 8:16, :], 1.0, None, ALU.add).then_inc(s_mod, 1)
            dve.wait_ge(s_wsT, 1)
            dve.tensor_copy(wsT, ws_ps).then_inc(s_wsT, 1)

            def turn(i, ahead):
                for s in range(2):
                    t = 2 * i + s
                    n0 = 3 * t + 2
                    z = z_qkv[s]
                    dve.wait_ge(s_zc, 2 * t + 2)
                    own.did(dve.tensor_tensor(r_sq, z[:, 0:640], z[:, 0:640], ALU.mult))
                    own.did(dve.tensor_copy(va[:, ds(t, 1), :].rearrange("p a n -> p (a n)"), z[:, 640:768]))
                    own.settle()
                    rs = small[:, 32 + 16 * s:42 + 16 * s]
                    own.did(dve.tensor_reduce(rs, r_sq.rearrange("p (h n) -> p h n", n=HD), AX.X, ALU.add))
                    own.settle()
                    dve.tensor_scalar(rs, rs, 1.0 / HD, RMS_EPS, ALU.mult, ALU.add).then_inc(s_stat, 1)
                    if ahead:
                        ln_x_stats(i, s, 16 * (i + 2))
                    if ahead:
                        ln_x_apply(s, t + 1, n0 + 2, False)
                    dve.wait_ge(s_rs, n0 + 1 if ahead else 3 * t + 3 - s)
                    v3 = lambda a: a.rearrange("p (h n) -> p h n", n=HD)
                    own.did(dve.tensor_tensor(v3(r_n), v3(z[:, 0:640]), rs.unsqueeze(2).to_broadcast([P, N_QK, HD]), ALU.mult))
                    own.settle()
                    own.did(dve.tensor_tensor(r_sq, r_n, gqk, ALU.mult))
                    own.settle()
                    pair = r_sq.rearrange("p (h n two) -> p h n two", n=32, two=2)
                    cs = cossin[:, ds(t, 1), :, :].rearrange("p t a n -> p (t a) n")
                    cos = cs[:, 0:1, :].to_broadcast([P, N_QK, 32])
                    sin = cs[:, 1:2, :].to_broadcast([P, N_QK, 32])
                    h3 = lambda a: a.rearrange("p (h n) -> p h n", n=32)
                    if not (isinstance(i, int) and i == 0):
                        dve.wait_ge(s_qt, t - 1)
                    for part, (ca, cb, op) in enumerate(((cos, sin, ALU.subtract), (sin, cos, ALU.add))):
                        if part:
                            own.settle()
                        own.did(dve.tensor_tensor(h3(r_a), pair[:, :, :, 0], ca, ALU.mult))
                        own.did(dve.tensor_tensor(h3(r_b2), pair[:, :, :, 1], cb, ALU.mult))
                        own.settle()
                        oq = qk_out[s][:, 0:512].rearrange("p (h n two) -> p h n two", n=32, two=2)[:, :, :, part]
                        own.did(dve.tensor_tensor(oq, h3(r_a)[:, 0:N_Q, :], h3(r_b2)[:, 0:N_Q, :], op))
                        for copy in range(2):
                            ok = qk_out[s][:, 512:768].rearrange("p (g c n two) -> p g c n two", g=2, c=2, two=2)[:, :, copy, :, part]
                            last = dve.tensor_tensor(ok, h3(r_a)[:, N_Q:N_QK, :], h3(r_b2)[:, N_Q:N_QK, :], op)
                            if part == 0 or copy == 0:
                                own.did(last)
                            else:
                                last.then_inc(s_qr, 1)
                    dve.wait_ge(s_vg, t + 1)
                    norm_stats(v_gelu[s], ln_cols(1, s), bn, W_BR)
                    dve.wait_ge(s_rs, n0 + 3 if ahead else 3 * t + 4 - s)
                    cols = ln_cols(1, s)
                    dve.tensor_scalar(vln[:, ds(t, 1), :].rearrange("p a n -> p (a n)"), v_gelu[s],
                                      cols[:, 0:1], cols[:, 7:8], ALU.subtract, ALU.mult).then_inc(s_vn, 1)

            dve.wait_ge(s_gqk, 1)
            turn_first = own.n
            turn(0, True)
            per = own.n - turn_first
            with dve.Fori(1, PAIRS - 1) as i:
                own.enter(i - 1, per)
                turn(i, True)
                own.leave(PAIRS - 2)
            turn(PAIRS - 1, False)

            own.settle()
            dve.wait_ge(s_qt, TILES)
            dve.wait_ge(s_qr, TILES)
            for s in range(2):
                own.did(dve.memset(z_pad[s], 0.0))
            own.settle()
            dve.tensor_copy(pads_set[:, :], z_pad[0][:, 0:1]).then_inc(s_pads, 1)
            dve.wait_ge(s_fe[0], 2)
            dve.wait_ge(s_fe[1], 2)
            gate3 = gate_sb[:, 0:512].rearrange("p (g n) -> p g n", g=4)
            b3 = bs_b.rearrange("p (g n) -> p g n", g=4)
            for t in range(TILES):
                dve.wait_ge(s_sv, t + 1)
                u = y0[:, :, t * P:(t + 1) * P]
                dve.tensor_tensor(gate3, sv_ps[t % 2], b3, ALU.add).then_inc(s_sve, 1)
                dve.wait_ge(s_sve, t + 1)
                dve.tensor_tensor(u, u, gate3, ALU.mult).then_inc(s_ya, 1)
                dve.wait_ge(s_ya, t + 1)
            for g, w in enumerate(WINDOWS):
                z = z_pad[g % 2]
                dve.wait_ge(s_fe[g % 2], (R_B + g) // 2 + 1)
                n = PADDED
                own.settle()
                own.did(dve.tensor_tensor(sum_a[:, 1:n], z[:, 0:n - 1], z[:, 1:n], ALU.add))
                src, dst, a = sum_a, sum_b, 1
                while 2 * a < w:
                    own.settle()
                    own.did(dve.tensor_tensor(dst[:, 2 * a:n - 2 * a], src[:, a:n - 3 * a], src[:, 3 * a:n - a], ALU.add))
                    src, dst, a = dst, src, 2 * a
                own.settle()
                for at, lo, m in SEGS:
                    own.did(dve.scalar_tensor_tensor(out=y1[:, g, lo:lo + m], in0=src[:, at:at + m], scalar=1.0 / w,
                                                     in1=z[:, at:at + m], op0=ALU.mult, op1=ALU.subtract))
                for e, (at, lo, m) in enumerate(SEGS):
                    for side, (sl, o) in enumerate(((slice(at, at + 8), lo), (slice(at + m - 8, at + m), lo + m - 8))):
                        own.settle()
                        own.did(dve.tensor_tensor(dst[:, 0:8], src[:, sl], edge[:, g, 2 * e + side, :], ALU.mult))
                        own.settle()
                        last = dve.tensor_tensor(y1[:, g, o:o + 8], dst[:, 0:8], z[:, sl], ALU.subtract)
                        if e and side:
                            last.then_inc(s_pool, 1)
                            dve.wait_ge(s_pool, g + 1)
                        else:
                            own.did(last)

            def merge(name):
                _, r0, _, m0, _ = MERGES[name]

                def turn(i, first):
                    for s in range(2):
                        dm = merged[:, ds(2 * i + s, 1), :].rearrange("p a n -> p (a n)")
                        done = r0 // 2 + 2 * i + s + 1
                        dve.wait_ge(s_fe[0], done)
                        dve.wait_ge(s_f[1], done)
                        if name == "A":
                            dve.tensor_tensor(dm, gate_sb, res[1], ALU.mult).then_inc(s_fe[1], 1)
                            continue
                        if not (first and s == 0 and m0 == 8):
                            dve.wait_ge(s_mg, m0 - 8 + 2 * i + s)
                        dve.tensor_tensor(prod, gate_sb, res[1], ALU.mult).then_inc(s_fe[1], 1)
                        dve.wait_ge(s_fe[1], done)
                        dve.tensor_tensor(dm, dm, prod, ALU.add).then_inc(s_mg, 1)

                turn(0, True)
                with dve.Fori(1, 4) as i:
                    turn(i, False)

            merge("A")
            own.did(dve.memset(z_conv, 0.0))
            for j in range(4):
                rc, rx, rb = (R_D + 3 * j + m for m in range(3))
                dve.wait_ge(s_fe[rc % 2], rc // 2 + 1)
                dve.wait_ge(s_f[rx % 2], rx // 2 + 1)
                own.settle()
                for e, (at, lo, m) in enumerate(CSEGS):
                    last = dve.tensor_tensor(z_conv[:, at:at + m], cg_sb[:, lo:lo + m], res[rx % 2][:, lo:lo + m], ALU.mult)
                    if e:
                        last.then_inc(s_fe[rx % 2], 1)
                    else:
                        own.did(last)
                dve.wait_ge(s_fe[rx % 2], rx // 2 + 1)
                own.settle()
                n = T + 4
                tap = [colT[:, 64 + 4 * q + j:65 + 4 * q + j] for q in range(3)]
                own.did(dve.tensor_scalar(taps[:, 1:n - 1], z_conv[:, 0:n - 2], tap[0], None, ALU.mult))
                for q in (1, 2):
                    own.settle()
                    own.did(dve.scalar_tensor_tensor(out=taps[:, 1:n - 1], in0=z_conv[:, q:n - 2 + q], scalar=tap[q],
                                                     in1=taps[:, 1:n - 1], op0=ALU.mult, op1=ALU.add))
                dve.wait_ge(s_f[rb % 2], rb // 2 + 1)
                own.settle()
                for e, (at, lo, m) in enumerate(CSEGS):
                    last = dve.tensor_tensor(y0[:, j, lo:lo + m], taps[:, at:at + m], res[rb % 2][:, lo:lo + m], ALU.mult)
                    if e:
                        last.then_inc(s_fe[rb % 2], 1)
                    else:
                        own.did(last)
                dve.wait_ge(s_fe[rb % 2], rb // 2 + 1)
            merge("B")
            merge("D")

            def attend(t, keys, first=False, last=False):
                n = N_Q * t

                def row_max(h):
                    u = h % 2
                    dve.wait_ge(s_qk, n + h + 1)
                    own.did(dve.tensor_reduce(small[:, 4 + u:5 + u], s_ps[u][:, 0:keys], AX.X, ALU.max))
                    own.settle()
                    dve.tensor_scalar(small[:, u:u + 1], small[:, 4 + u:5 + u], -HD ** -0.5, None, ALU.mult).then_inc(s_mx, 1)

                def head_out(h):
                    u, k = h % 4, h % N_Q
                    own.did(dve.reciprocal(small[:, 36 + u:37 + u], sums[:, u:u + 1]))
                    own.settle()
                    dve.wait_ge(s_pv, n + h + 1)
                    if h in (2, 4) and keys == T_PROMPT:
                        dve.wait_ge(s_m2, 2 * t + h // 2)
                        dve.tensor_copy(part2_sb, part2_ps).then_inc(s_m2p, 1)
                    if h == 0 and not (isinstance(t, int) and t == 0):
                        dve.wait_ge(s_otp, t)
                    dve.tensor_scalar(o_row[:, HD * k:HD * k + HD], o_ps[h % 2], small[:, 36 + u:37 + u], None, ALU.mult).then_inc(s_oe, 1)

                def tile_out(i):
                    dve.wait_ge(s_otp, i + 1)
                    dve.tensor_copy(y1[:, :, ds(i * P, P)], oT_ps).then_inc(s_oc, 1)

                if first:
                    row_max(0)
                for h in range(N_Q):
                    if h + 1 < N_Q or not last:
                        row_max(h + 1)
                    if h == 1 and not first:
                        tile_out(t - 1)
                    if h or not first:
                        head_out(h - 1)
                if last:
                    head_out(N_Q - 1)
                    tile_out(t)

            dve.wait_ge(s_mg, 16)
            own.per_tile = 2 * N_Q
            all_tiles(dve, attend, own)
            dve.wait_ge(s_m2s, 16)
            own.did(dve.tensor_tensor(mod2T[:, :, :], mod2_ps, colT[:, 32:64].unsqueeze(1).to_broadcast([P, 2, 32]), ALU.add))
            own.settle()
            dve.tensor_scalar(mod2T[:, :, 16:24], mod2T[:, :, 16:24], 1.0, None, ALU.add).then_inc(s_m2T, 1)
            merge("C")

            bn2 = aff_t2[:, 0:12]

            def stats(src, cols, done):
                for j in range(2):
                    own.did(dve.bn_stats(bn2[:, 6 * j:6 * j + 6], src[:, 512 * j:512 * j + 512]))
                own.settle()
                own.did(dve.tensor_copy(carry[:, 0:1], half[:, 0:1]))
                own.did(dve.bn_aggr(cols[:, 0:2], bn2))
                own.settle()
                dve.tensor_scalar(cols[:, 7:8], cols[:, 1:2], LN_EPS, None, ALU.add).then_inc(done, 1)

            def centre(dst, src, cols, gain):
                own.did(dve.scalar_tensor_tensor(out=dst, in0=src, scalar=cols[:, 0:1], in1=gain,
                                                 op0=ALU.subtract, op1=ALU.mult))
                own.settle()

            def spread(dst, cols, offset, done):
                dve.scalar_tensor_tensor(out=dst, in0=dst, scalar=cols[:, 7:8], in1=offset,
                                         op0=ALU.mult, op1=ALU.add).then_inc(done, 1)

            def soft1(s, t):
                lg = aff_t[:, s, 0, :]
                dve.wait_ge(s_lg, t + 1)
                own.did(dve.tensor_tensor(lg, logit_ps, rb_b[:, :], ALU.add))
                own.settle()
                own.did(dve.tensor_reduce(small[:, 4 + s:5 + s], lg, AX.X, ALU.max))
                own.settle()
                dve.tensor_scalar(small[:, 2 * s:2 * s + 1], small[:, 4 + s:5 + s], -1.0, None, ALU.mult).then_inc(s_sm, 1)

            def soft2(s, t):
                dve.wait_ge(s_se, t + 1)
                own.did(dve.reciprocal(small[:, 6 + s:7 + s], small[:, 2 * s + 1:2 * s + 2]))
                own.settle()
                if not (isinstance(t, int) and t < 2):
                    dve.wait_ge(s_at, t - 1)
                dve.tensor_scalar(aff3[:, s, :].rearrange("p (a n) -> p a n", n=32)[:, :, 0:NE],
                                  aff_t[:, s, 1:2, :].to_broadcast([P, 3, NE]), small[:, 6 + s:7 + s], None, ALU.mult).then_inc(s_aff, 1)

            def rows_turn(i, grp, first=False, second=False):
                for s in range(2):
                    t = 2 * i + s
                    c1, c2 = ln_cols(1, s), ln_cols(2, s)
                    dve.wait_ge(s_y, t + 1)
                    if not first:
                        dve.wait_ge(s_xs, t - 1)
                    dve.tensor_tensor(x1_row[s], y_ps[s], g1_b[grp], ALU.mult).then_inc(s_yr, 1)
                    dve.wait_ge(s_yr, t + 1)
                    dve.wait_ge(s_xr[s], 16 * i + 16)
                    dve.scalar_tensor_tensor(out=x1_row[s], in0=x_row[s], scalar=ALPHA, in1=x1_row[s],
                                             op0=ALU.mult, op1=ALU.add).then_inc(s_xa, 1)
                    dve.wait_ge(s_xa, t + 1)
                    stats(x1_row[s], c1, s_st2)
                    centre(x1_row[s], x1_row[s], c1, ln1g_b)
                    if not first:
                        soft1(s, t - 2)
                    dve.wait_ge(s_rs2, 2 * t + 1)
                    spread(x1_row[s], c1, ln1b_b, s_x1)
                    dve.wait_ge(s_x1, t + 1)
                    stats(x1_row[s], c2, s_st2)
                    if not first:
                        soft2(s, t - 2)
                        dve.wait_ge(s_h2o[s], 16 * i)
                        dve.wait_ge(s_et, t - 1)
                    centre(h2_row[s], x1_row[s], c2, sc2_b[grp])
                    dve.wait_ge(s_rs2, 2 * t + 2)
                    spread(h2_row[s], c2, sh2_b[grp], s_h2)

            own.did(dve.memset(aff3[:, :, :], 0.0))
            dve.wait_ge(s_mg, 24)
            dve.memset(affT, -1.0).then_inc(s_fill, 1)
            own.settle()
            dve.wait_ge(s_rows2, 16 * 8)
            rows_turn(0, 0, True)
            n = own.n
            rows_turn(1, 0)
            per = own.n - n
            with dve.Fori(2, PROMPT_PAIRS) as i:
                own.enter(i - 2, per)
                rows_turn(i, 0)
                own.leave(PROMPT_PAIRS - 2)
            rows_turn(PROMPT_PAIRS, 1)
            for s in range(2):
                soft1(s, TILES - 2 + s)
                soft2(s, TILES - 2 + s)

            dve.wait_ge(s_affT, TILES)
            for r in range(0, CAP_P, 8):
                own.settle()
                own.did(dve.max(out=top_v[:, r:r + 8], in_=affT))
                own.settle()
                own.did(dve.max_index(out=top_i[:, r:r + 8], in_max=top_v[:, r:r + 8], in_values=affT))
                own.settle()
                if r + 8 < CAP_P:
                    own.did(dve.match_replace(out=affT, in_to_replace=top_v[:, r:r + 8], in_values=affT, imm_value=-1.0))
            own.did(dve.tensor_copy(top_f, top_i[:, :]))
            own.settle()
            for g in range(1, 3):
                last = dve.tensor_scalar(top_f[32 * g:32 * g + NE, :], top_f[32 * g:32 * g + NE, :], float(g * HALF), None, ALU.add)
                if g == 1:
                    own.did(last)
            last.then_inc(s_top, 1)
            dve.wait_ge(s_topT, 1)
            dve.tensor_copy(top_ranks, top_ps).then_inc(s_rank, 1)
            dve.wait_ge(s_flip, 1)
            dve.wait_ge(s_rank, 1)
            own.did(dve.tensor_tensor(first_wins, top_ranks[:, 0, 0:NE], flip_ps[:, 0, :], ALU.is_ge))
            own.did(dve.tensor_tensor(index_gap, top_ranks[:, 1, 0:NE], flip_ps[:, 1, :], ALU.subtract))
            dve.tensor_tensor(gate_p[:, :], top_ranks[:, 0, 0:NE], flip_ps[:, 0, :], ALU.max).then_inc(s_idx, 1)
            dve.tensor_copy(gate_s[:, :], top_ranks[0:CAP_S, 0, 64:64 + NE]).then_inc(s_idx, 1)
            dve.tensor_copy(idx_s[:, :], top_ranks[0:CAP_S, 1, 64:64 + NE]).then_inc(s_idx, 1)
            own.settle()
            own.did(dve.tensor_tensor(index_gap, index_gap, first_wins, ALU.mult))
            own.settle()
            dve.tensor_tensor(idx_p[:, :], index_gap, flip_ps[:, 1, :], ALU.add).then_inc(s_idx, 1)

            def expert(e, more):
                for j in range(KD):
                    dve.wait_ge(s_si, 8 * e + j + 1)
                    dve.tensor_tensor(gT[:, j, :], silu[j % 2], ab_ps[j % 2][:, 1, :], ALU.mult).then_inc(s_g, 1)
                if more:
                    dve.wait_ge(s_xt, e + 2)
                    dve.tensor_copy(xgT[:, :, CAP_P:CAP], xt_s).then_inc(s_xes, 1)
                for j in range(KD):
                    dve.wait_ge(s_o, 8 * e + j + 1)
                    own.did(dve.tensor_scalar(outT[:, j, 0:CAP_P], ab_ps[j % 2][:, 0, 0:CAP_P], mod2T[:, 0, 24 + j:25 + j], None, ALU.mult))
                    own.settle()
                    dve.tensor_scalar(outT[:, j, CAP_P:CAP], ab_ps[j % 2][:, 0, CAP_P:CAP], mod2T[:, 1, 24 + j:25 + j], None, ALU.mult).then_inc(s_oT, 1)
                dve.wait_ge(s_ot, e + 1)
                if not (isinstance(e, int) and e == 0):
                    dve.wait_ge(s_sc, 32 * e)
                for h in range(2):
                    last = dve.tensor_scalar(out_s[:, 512 * h:512 * h + 512], os_ps[h], gate_s[:, ds(e, 1)], None, ALU.mult)
                last.then_inc(s_os, 1)

            dve.wait_ge(s_idx, 4)
            dve.wait_ge(s_xt, 1)
            dve.tensor_copy(xgT[:, :, CAP_P:CAP], xt_s).then_inc(s_xes, 1)
            expert(0, True)
            with dve.Fori(1, NE - 1) as e:
                own.enter(e - 1, KD)
                expert(e, True)
                own.leave(NE - 2)
            expert(NE - 1, False)

            dve.wait_ge(s_ln2, 32)
            for t in range(TILES):
                c1 = ln_cols(1, t % 2)
                dve.wait_ge(s_fx[t % LAST], 16 * (t // LAST) + 16)
                if t >= 2:
                    dve.wait_ge(s_fs, t - 1)
                stats(y_in[t % LAST], c1, s_st3)
                if t >= LAST:
                    dve.wait_ge(s_done[t % LAST], 16)
                dve.scalar_tensor_tensor(out=y_out[t % LAST], in0=y_in[t % LAST], scalar=c1[:, 0:1], in1=ln2g_b,
                                         op0=ALU.subtract, op1=ALU.mult).then_inc(s_fn, 1)

        @block.tensor
        def _(pe):
            pe.wait_ge(s_id, 1)
            pe.wait_ge(s_silu, 1)
            pe.wait_ge(s_rows, 64)
            pe.transpose(rows_ps, rows_in[0:80, :], ident[0:80, 0:80]).then_inc(s_rT, 1)
            pe.wait_ge(s_col, 1)
            def partial(dst, w):
                for k in range(KD):
                    g = 32 * (k % 4)
                    last = pe.matmul(dst[g:g + 32, :], c_pad[:, k, :], w[:, k, :], start=k < 4, stop=k >= 4)
                return last

            def summed(dst, part):
                for j in range(part.shape[1] // P):
                    last = pe.matmul(dst(j), part[:, j * P:(j + 1) * P], every32[:, 0:2], start=True, stop=True)
                return last

            pe.wait_ge(s_cpad, 1)
            for m in range(5):
                if m < 4:
                    pe.wait_ge(s_wada[m], 16)
                    if m >= 2:
                        pe.wait_ge(s_modc, m - 1)
                    partial(part_ps[m % 2], w_ada_buf[m]).then_inc(s_modp, 1)
                if m:
                    pe.wait_ge(s_modc, m)
                    summed(lambda j: mod_ps[:, 4 * (m - 1) + j, :], part_sb[(m - 1) % 2]).then_inc(s_modmm, 1)
            pe.wait_ge(s_ws, 16)
            for g in range(4):
                last = pe.transpose(ws_ps[:, g, :], ws_in[:, g, :], ident[:, :])
            last.then_inc(s_wsT, 1)

            def turn_x_rows(i, s):
                t = 2 * i + s
                pe.wait_ge(s_xh, t + 1)
                if not (isinstance(i, int) and i < 2):
                    pe.wait_ge(s_qe, t - 3)
                for k in range(KD):
                    last = pe.transpose(tp[s][:, k, :], xh[s][:, k * P:(k + 1) * P], ident[:, :])
                last.then_inc(s_tp, 1)

            def turn_qk(i, s, more=True):
                t = 2 * i + s
                pe.wait_ge(s_qr, t + 1)
                if more:
                    pe.wait_ge(s_ht, t + 3)
                for k in range(6):
                    last = pe.transpose(tp[s][:, k, :], qk_out[s][:, k * P:(k + 1) * P], ident[:, :])
                last.then_inc(s_qt, 1)

            def turn(i, more=True):
                first = isinstance(i, int) and i == 0
                for s in range(2):
                    t = 2 * i + s
                    zero = first and s == 0
                    pe.wait_ge(s_ht, t + 1)
                    for dst, lo, n, done, freed, cnt in ((z1, 0, 512, s_z1, s_zc, 2 * t - 1), (z2, 512, 256, s_z2, s_zc, 2 * t),
                                                         (z3, 768, 512, s_z3, s_vg, t)):
                        if not zero:
                            pe.wait_ge(freed, cnt)
                        elif dst is z3:
                            pe.wait_ge(s_wz[1], 16)
                        for k in range(KD):
                            last = pe.matmul(dst, h_tile[s][:, k, :], wz[:, k, lo:lo + n], start=k == 0, stop=k == KD - 1)
                        last.then_inc(done, 1)
                        if s == 0 and not first and dst is not z2:
                            turn_qk(i - 1, 0 if dst is z1 else 1)
                        if s == 1 and more and dst is not z1:
                            turn_x_rows(i + 1, 0 if dst is z2 else 1)

            for s in range(2):
                turn_x_rows(0, s)
            pe.wait_ge(s_wz[0], 16)
            pe.wait_ge(s_mod, 1)
            pe.wait_ge(s_wsT, 2)
            turn(0)
            with pe.Fori(1, PAIRS - 1) as i:
                turn(i)
            turn(PAIRS - 1, False)
            for s in range(2):
                turn_qk(PAIRS - 1, s, False)

            def product(par, freed, w, count, k_tiles, rhs):
                if freed is not None:
                    pe.wait_ge(s_fe[par], freed)
                pe.wait_ge(w[1], count)
                for lo, n in BLOCKS:
                    for k in range(k_tiles):
                        last = pe.matmul(res[par][:, lo:lo + n], w[0][:, k, :], rhs[:, k, lo:lo + n],
                                         start=k == 0, stop=k == k_tiles - 1)
                last.then_inc(s_f[par], 1)

            def wt(s):
                return w_tile[s], s_w[s]

            pe.wait_ge(s_qe, TILES)
            pe.wait_ge(s_zc, 2 * TILES)
            pe.wait_ge(s_vg, TILES)
            pe.wait_ge(s_hc, TILES)
            for s in range(2):
                product(s, None, wt(s), 16, KD, hT)
            with pe.Fori(1, 2) as i:
                for s in range(2):
                    product(s, i, wt(s), 16 * i + 16, KD, hT)
            pe.wait_ge(s_vl, TILES)
            for t in range(TILES):
                if t >= 2:
                    pe.wait_ge(s_sve, t - 1)
                for g in range(4):
                    last = pe.matmul(sv_ps[t % 2][:, g, :], vln[:, t, g * P:(g + 1) * P], wsT[:, g, :], start=True, stop=True)
                last.then_inc(s_sv, 1)
            with pe.Fori(2, 4) as i:
                for s in range(2):
                    product(s, i, wt(s), 16 * i + 16, KD, hT)

            def merge(name):
                n0, r0, _, m0, y = MERGES[name]
                with pe.Fori(0, 4) as i:
                    for s in range(2):
                        product(0, r0 // 2 + 2 * i + s, wt(s), 8 * n0 + 16 * i + 16, KD, hT)
                        product(1, r0 // 2 + 2 * i + s, (p_tile[s], s_p[s]), 8 * m0 + 16 * i + 16, KB, y)

            pe.wait_ge(s_ya, TILES)
            merge("A")
            pe.wait_ge(s_wg, 16)
            pe.wait_ge(s_pool, 4)
            for g in range(4):
                r = R_MIX + g
                pe.wait_ge(s_fe[r % 2], r // 2)
                for lo, n in BLOCKS:
                    last = pe.matmul(res[r % 2][:, lo:lo + n], wg_sb[:, g, :], y1[:, g, lo:lo + n], start=True, stop=True)
                last.then_inc(s_f[r % 2], 1)
            with pe.Fori(0, 2) as i:
                for m in range(6):
                    product(m % 2, R_D // 2 + 3 * i + m // 2, wt(m % 2), 8 * N_D + 48 * i + 16 * (m // 2) + 16, KD, hT)
            pe.wait_ge(s_fe[0], R_D // 2)
            pe.wait_ge(s_fe[1], R_D // 2)
            merge("B")
            pe.wait_ge(s_fe[1], R_MB // 2)
            merge("D")

            def modulation(i, h):
                if h >= 4:
                    pe.wait_ge(s_m2p, 2 * i + h // 2 - 1)
                    a = h // 2 - 2
                    summed(lambda j: mod2_ps[:, :, ds(4 * i + 2 * a + j, 1)].rearrange("p g a -> p (g a)"), part2_sb) \
                        .then_inc(s_m2s, 1)
                if h <= 4:
                    a = h // 2 - 1
                    pe.wait_ge(s_wm[a], 16 * i + 16)
                    partial(part2_ps, w_mod[a]).then_inc(s_m2, 1)

            def attend(t, keys, first=False, last=False):
                n = N_Q * t

                def scores(h):
                    k = h % N_Q
                    lo = HD * (k % 2)
                    if k % 2 == 0:
                        pe.wait_ge(s_qb, 4 * t + h // 2 + 1)
                    if not (isinstance(t, int) and t == 0 and h < 2):
                        pe.wait_ge(s_exp, n + h - 1)
                    for at in range(0, keys, 512):
                        m = min(512, keys)
                        k0 = 0 if keys == T_PROMPT else T_PROMPT
                        end = pe.matmul(s_ps[k % 2][:, at:at + m], q_tile[lo:lo + HD, k // 2, :],
                                        kT[lo:lo + HD, k // 4, k0 + at:k0 + at + m], start=True, stop=True)
                    end.then_inc(s_qk, 1)

                def weighted(h):
                    k = h % N_Q
                    pe.wait_ge(s_pte, n + h + 1)
                    if not (isinstance(t, int) and t == 0 and h < 2):
                        pe.wait_ge(s_oe, n + h - 1)
                    if h == 1 and not (isinstance(t, int) and t == 0):
                        pe.wait_ge(s_oc, t)
                    if h in (2, 4, 6) and keys == T_PROMPT:
                        modulation(t, h)
                    t0 = 0 if keys == T_PROMPT else T_PROMPT // P
                    for b in range(keys // P):
                        end = pe.matmul(o_ps[k % 2], probT[k % 2][:, b, :], va[:, t0 + b, (k // 4) * HD:(k // 4 + 1) * HD],
                                        start=b == 0, stop=b == keys // P - 1)
                    end.then_inc(s_pv, 1)

                def turn_out(i):
                    pe.wait_ge(s_oe, N_Q * i + N_Q)
                    if not (isinstance(i, int) and i == 0):
                        pe.wait_ge(s_oc, i)
                    for j in range(4):
                        end = pe.transpose(oT_ps[:, j, :], o_row[:, j * P:(j + 1) * P], ident[:, :])
                    end.then_inc(s_otp, 1)

                if first:
                    scores(0)
                for h in range(N_Q):
                    if h + 1 < N_Q or not last:
                        scores(h + 1)
                    if h == 1 and not first:
                        turn_out(t - 1)
                    pe.wait_ge(s_exp, n + h + 1)
                    if not (isinstance(t, int) and t == 0 and h == 0):
                        pe.wait_ge(s_pte, n + h)
                    for b in range(keys // P):
                        end = pe.transpose(pt_ps[:, b, :], prob[h % 2][:, b * P:(b + 1) * P], ident[:, :])
                    end.then_inc(s_pt, 1)
                    if h or not first:
                        weighted(h - 1)
                if last:
                    weighted(N_Q - 1)
                    turn_out(t)

            for s in range(2):
                pe.wait_ge(s_fe[s], R_MC // 2)
            pe.wait_ge(s_sve, TILES)
            all_tiles(pe, attend)
            pe.wait_ge(s_m2T, 1)
            pe.transpose(modr_ps, mod2T[:, :, :].rearrange("p g c -> p (g c)"), ident[:, :]).then_inc(s_m2r, 1)
            pe.wait_ge(s_exp, N_Q * TILES)
            pe.wait_ge(s_pte, N_Q * TILES)
            pe.wait_ge(s_oc, TILES)
            merge("C")

            for s in range(2):
                pe.wait_ge(s_fe[s], R_END // 2)
            pe.wait_ge(s_m2c, 1)

            def rows_out(i, s, between=None):
                t = 2 * i + s
                if isinstance(i, int) and t == 0:
                    pe.wait_ge(s_mt0, 1)
                else:
                    pe.wait_ge(s_mt, t)
                if not (isinstance(i, int) and i == 0):
                    pe.wait_ge(s_yr, t - 1)
                for h in range(2):
                    for k in range(KD):
                        last = pe.matmul(y_ps[s][:, 512 * h:512 * h + 512], m_tile[s][:, k, :], wo_sb[:, k, 512 * h:512 * h + 512],
                                         start=k == 0, stop=k == KD - 1)
                    if h == 0 and between:
                        between()
                last.then_inc(s_y, 1)

            def turn_h(s, t):
                pe.wait_ge(s_h2, t + 1)
                if not (isinstance(t, int) and t == 0):
                    pe.wait_ge(s_h2T, t)
                for k in range(KD):
                    last = pe.transpose(h2t_ps[:, k, :], h2_row[s][:, k * P:(k + 1) * P], ident[:, :])
                last.then_inc(s_et, 1)

            def logits_part(s, t):
                pe.wait_ge(s_h2T, t + 1)
                if not (isinstance(t, int) and t == 0):
                    pe.wait_ge(s_sm, t)
                for k in range(KD):
                    g = 32 * (k % 4)
                    last = pe.matmul(lpart_ps[g:g + 32, :], rw_sb[:, k, :], h2T[s][:, k, :], start=k < 4, stop=k >= 4)
                last.then_inc(s_lp, 1)

            def logits(t):
                pe.wait_ge(s_lpc, t + 1)
                pe.matmul(logit_ps, lpart_sb, every32[:, :], start=True, stop=True).then_inc(s_lg, 1)

            def turn_aff(s, t):
                pe.wait_ge(s_aff, t + 1)
                if not (isinstance(t, int) and t == 0):
                    pe.wait_ge(s_affT, t)
                pe.transpose(affT_ps, aff3[:, s, :], ident[:, :]).then_inc(s_at, 1)

            pe.wait_ge(s_wo, 32)
            for s in range(2):
                rows_out(0, s)
            for s in range(2):
                turn_h(s, s)
                rows_out(1, s, lambda: logits_part(s, s))
                if s:
                    turn_aff(0, 0)
                logits(s)
            with pe.Fori(2, PAIRS) as i:
                for s in range(2):
                    turn_h(s, 2 * i + s - 2)
                    rows_out(i, s, lambda: logits_part(s, 2 * i + s - 2))
                    turn_aff(1 - s, 2 * i + s - 3)
                    logits(2 * i + s - 2)
            for s in range(2):
                turn_h(s, TILES - 2 + s)
                logits_part(s, TILES - 2 + s)
                turn_aff(1 - s, TILES - 3 + s)
                logits(TILES - 2 + s)
            turn_aff(1, TILES - 1)

            pe.wait_ge(s_top, 1)
            pe.wait_ge(s_affT, TILES)
            pe.transpose(top_ps[:, 0, :], top_v, ident[0:TK, 0:TK])
            pe.transpose(top_ps[:, 1, :], top_f, ident[0:TK, 0:TK]).then_inc(s_topT, 1)
            pe.wait_ge(s_id, 2)
            pe.wait_ge(s_rank, 1)
            pe.matmul(flip_ps, flip, top_ranks[:, :, 32:32 + NE], start=True, stop=True).then_inc(s_flip, 1)

            def turn_x(e, first=False):
                pe.wait_ge(s_xg, 32 * e + 32)
                if not first:
                    pe.wait_ge(s_os, e - 1)
                for k in range(KD):
                    pe.transpose(xt_p[:, k, :], xg_p[:, k * P:(k + 1) * P], ident[:, :])
                for k in range(KD):
                    last = pe.transpose(xt_s[:, k, :], xg_s[:, k * P:(k + 1) * P], ident[0:CAP_S, 0:CAP_S])
                last.then_inc(s_xt, 1)

            def expert(e, more, first=False):
                pe.wait_ge(s_xe, e + 1)
                pe.wait_ge(s_xes, e + 1)
                for j in range(KD):
                    if not (first and j < 2):
                        if j < 2:
                            pe.wait_ge(s_oT, 8 * e - 1 + j)
                        else:
                            pe.wait_ge(s_g, 8 * e + j - 1)
                    for m in range(2):
                        c = 2 * (j // 4) + m
                        if j % 4 == 0:
                            pe.wait_ge(s_wx[c], 16 * e + 16)
                        for k in range(KD):
                            last = pe.matmul(ab_ps[j % 2][:, m, :], w_half[c][:, k, (j % 4) * P:(j % 4 + 1) * P], xgT[:, k, :],
                                             start=k == 0, stop=k == KD - 1)
                    last.then_inc(s_ab, 1)
                if more:
                    turn_x(e + 1, first)
                for j in range(KD):
                    if j < 2:
                        pe.wait_ge(s_g, 8 * e + 7 + j)
                        if j == 0:
                            pe.wait_ge(s_g, 8 * e + 8)
                    else:
                        pe.wait_ge(s_oT, 8 * e + j - 1)
                    if j % 4 == 0:
                        pe.wait_ge(s_wx[4 + j // 4], 16 * e + 16)
                    for k in range(KD):
                        last = pe.matmul(ab_ps[j % 2][:, 0, :], w_half[4 + j // 4][:, k, (j % 4) * P:(j % 4 + 1) * P], gT[:, k, :],
                                         start=k == 0, stop=k == KD - 1)
                    last.then_inc(s_o, 1)
                pe.wait_ge(s_oT, 8 * e + 8)
                if more:
                    pe.wait_ge(s_xes, e + 2)
                if not first:
                    pe.wait_ge(s_op, e)
                    pe.wait_ge(s_os, e)
                for j in range(KD):
                    pe.transpose(op_ps[:, j * P:(j + 1) * P], outT[:, j, 0:CAP_P], ident[:, :])
                for j in range(KD):
                    last = pe.transpose(os_ps[j // 4][:, (j % 4) * P:(j % 4 + 1) * P], outT[:, j, CAP_P:CAP], ident[:, :])
                last.then_inc(s_ot, 1)

            pe.wait_ge(s_idx, 4)
            turn_x(0, True)
            expert(0, True, True)
            with pe.Fori(1, NE - 1) as e:
                expert(e, True)
            expert(NE - 1, False)


_NAMES = ("w_ada", "b_ada", "w_in", "a_ln_g", "a_ln_b", "a_ws", "a_bs", "b_wg", "b_scale", "c_q_g", "c_k_g", "d_conv")
_NAMES_2 = ("w_o", "ln1_g", "ln1_b", "r_w", "r_b", "e_w1", "e_w3", "e_w2", "ln2_g", "ln2_b")


def rope_table():
    inv = (np.float32(10000.0) ** (-np.arange(16, dtype=np.float32) / np.float32(16))).astype(np.float32)
    tables = []
    for n in (T_PROMPT, T_SAMPLE):
        row = np.repeat(np.arange(n // 64, dtype=np.float32), 64)
        col = np.tile(np.arange(64, dtype=np.float32), n // 64)
        angle = np.concatenate([row[:, None] * inv, col[:, None] * inv], axis=-1)
        tables.append(np.stack([np.cos(angle), np.sin(angle)], axis=1))
    table = np.concatenate(tables).astype(np.float32).reshape(TILES, P, 2, 32)
    return np.ascontiguousarray(table.transpose(1, 0, 2, 3))


def edge_counts():
    rows = []
    for w in WINDOWS:
        for n in (T_PROMPT, T_SAMPLE):
            t = np.arange(n)
            count = np.clip(t + w // 2, 0, n) - np.clip(t - w // 2, 0, n)
            rows += [count[:8], count[-8:]]
    return (np.float32(1) / np.stack(rows).astype(np.float32)).reshape(len(WINDOWS), 4, 8)


def kernel(**inputs):
    import concourse.bacc as _bacc
    from concourse.bass_utils import run_bass_kernel_spmd as _run

    given = {k: np.asarray(v) for k, v in inputs.items()}
    arrays = {
        "x": np.concatenate([given["x_prompt"][0], given["x_sample"][0]]),
        "c": np.concatenate([given["c_prompt"], given["c_sample"]]),
    }
    for name in _NAMES:
        arrays[name] = given[name][0]
    arrays["p_all"] = np.stack([given[f"p_{b}"][0] for b in "abcd"])
    for name in _NAMES_2:
        arrays[name] = given[name][0]
    arrays["rope"] = rope_table()
    arrays["inv_count"] = edge_counts()
    arrays = {f"in_{k}_dram": np.ascontiguousarray(v) for k, v in arrays.items()}

    nc = _bacc.Bacc("TRN2", target_bir_lowering=False, num_devices=1)
    args = [nc.dram_tensor(k, a.shape, mybir.dt.from_np(a.dtype), kind="ExternalInput").ap() for k, a in arrays.items()]
    out = nc.dram_tensor("out_0_dram", (T, D), F32, kind="ExternalOutput").ap()
    build(nc, *args, out)
    rows = _run(nc, [arrays], core_ids=[0]).results[0]["out_0_dram"]
    return rows[:T_PROMPT].reshape(1, T_PROMPT, D), rows[T_PROMPT:].reshape(1, T_SAMPLE, D)
```

```python
import itertools
from contextlib import ExitStack

import numpy as np

import concourse.bass as bass
from concourse import mybir

F32 = mybir.dt.float32
U32 = mybir.dt.uint32
ALU = mybir.AluOpType
ACT = mybir.ActivationFunctionType
AX = mybir.AxisListType
ds = bass.ds

P = 128
T_PROMPT, T_SAMPLE = 1024, 256
T = T_PROMPT + T_SAMPLE
TILES = T // P
PAIRS = TILES // 2
PROMPT_PAIRS = T_PROMPT // P // 2
D = 1024
KD = D // P
W_BR = 512
KB = W_BR // P
HD = 64
N_Q, N_KV = 8, 2
N_QK = N_Q + N_KV
COL_U, COL_VG, COL_B = 0, 512, 1024
COL_C = 1536
COL_X, COL_BG, COL_CG = 2304, 2816, 3328
COL_G = 3840
WINDOWS = (2, 4, 8, 16)
NE = 16
CAP_P, CAP_S = 2 * T_PROMPT // NE, 2 * T_SAMPLE // NE
CAP = CAP_P + CAP_S
ALPHA = 2.0 ** 0.25
LN_EPS = 1e-5
RMS_EPS = 1e-6
LAST = 5
BLOCKS = ((0, 512), (512, 512), (1024, 256))


def wait_apart(eng, sem, value, met, count):
    if not isinstance(value, int):
        value = eng.snap(value)
    eng.wait_ge(met, count)
    eng.wait_ge(sem, value)


class Chain:

    def __init__(self, eng, sem):
        self.eng, self.sem, self.n, self.base = eng, sem, 0, 0

    def did(self, instruction):
        instruction.then_inc(self.sem, 1)
        self.n += 1

    def settle(self):
        self.eng.wait_ge(self.sem, self.base + self.n)

    def enter(self, i, per_turn):
        self.before, self.per = self.n, per_turn
        self.base, self.n = self.before + i * per_turn, 0

    def leave(self, turns):
        assert self.n == self.per, self.n
        self.base, self.n = 0, self.before + turns * self.per


def build(nc, x, c, w_ada, b_ada, w_in, a_ln_g, a_ln_b, a_ws, a_bs, b_wg, b_scale, c_q_g, c_k_g,
          d_conv, p_all, w_o, ln1_g, ln1_b, r_w, r_b, e_w1, e_w3, e_w2, ln2_g, ln2_b,
          rope, inv_count, out):
    with ExitStack() as ctx:
        def sb(name, shape, dt=F32):
            return ctx.enter_context(nc.sbuf_tensor(name, shape, dt))

        def sem(name):
            return ctx.enter_context(nc.semaphore(name))

        def sems(names):
            return [sem(name) for name in names.split()]

        h2_rows = nc.dram_tensor("h2_rows", (T, D), F32, kind="Internal").ap()
        mod_rows = nc.dram_tensor("mod_rows", (2, 4 * D), F32, kind="Internal").ap()
        y_rows = nc.dram_tensor("y_rows", (T, D), F32, kind="Internal").ap()

        ident = sb("ident", [P, P])
        rows_in = sb("rows_in", [P, P])
        colT = sb("colT", [P, 80])
        modT = sb("modT", [P, 16, 2])
        c_pad = sb("c_pad", [P, KD, 32])
        every32 = sb("every32", [P, NE])
        mod2T = sb("mod2T", [P, 2, 32])
        aff_t = sb("aff_t", [P, 2, 2, NE])
        aff3 = sb("aff3", [P, 2, 96])
        rb_b = sb("rb_b", [P, NE])
        small = sb("small", [P, 64])
        half = sb("half", [P, 16])
        aff_t2 = sb("aff_t2", [P, 12])
        carry = sb("carry", [P, 1])
        carried = sb("carried", [P, 16])

        R1 = sb("R1", [P, 20480])
        RQ = sb("RQ", [P, 8960])
        RV = sb("RV", [P, 5120])
        RY = sb("RY", [P, 5120])
        RW = sb("RW", [P, 3072])
        RT = sb("RT", [P, 7040])
        RC = sb("RC", [P, 2048])

        pads_set = sb("pads_set", [P, 1])
        hT = R1[:, 0:10240].rearrange("p (k t) -> p k t", k=KD)
        merged = R1[:, 10240:20480].rearrange("p (k t) -> p k t", k=KD)
        wz = R1[:, 10240:20480].rearrange("p (k n) -> p k n", k=KD)
        w_ada_buf = [r.rearrange("p (k n) -> p k n", k=KD)
                     for r in (RV[:, 0:4096], RQ[:, 0:4096], R1[:, 0:4096], R1[:, 4096:8192])]
        part_sb = [RQ[:, 4096 + 512 * m:4608 + 512 * m] for m in range(2)]
        qT = RQ[:, 0:5120].rearrange("p (j t) -> p j t", j=4)
        kT = RQ[:, 5120:7680].rearrange("p (j t) -> p j t", j=2)
        va = RQ[:, 7680:8960].rearrange("p (t n) -> p t n", n=P)
        vln = RV[:, :].rearrange("p (t n) -> p t n", n=W_BR)
        y1 = RV[:, :].rearrange("p (k t) -> p k t", k=KB)
        y0 = RY[:, :].rearrange("p (k t) -> p k t", k=KB)
        w_tile = [RW[:, 1024 * s:1024 * s + 1024].rearrange("p (k n) -> p k n", k=KD) for s in range(2)]
        p_tile = [RW[:, 2048 + 512 * s:2560 + 512 * s].rearrange("p (k n) -> p k n", k=KB) for s in range(2)]
        x_in = [RY[:, 1024 * s:1024 * s + 1024] for s in range(2)]
        xh = [RY[:, 2048 + 1024 * s:3072 + 1024 * s] for s in range(2)]
        h_tile = [RW[:, 1024 * s:1024 * s + 1024].rearrange("p (k n) -> p k n", k=KD) for s in range(2)]
        v_gelu = [RW[:, 2048 + 512 * s:2560 + 512 * s] for s in range(2)]
        z_qkv = [RT[:, 768 * s:768 * s + 768] for s in range(2)]
        qk_out = [RT[:, 1536 + 768 * s:2304 + 768 * s] for s in range(2)]
        r_sq = RT[:, 3072:3712]
        r_n = RT[:, 3712:4352]
        r_a = RT[:, 4352:4672]
        r_b2 = RT[:, 4672:4992]
        gqk = RC[:, 0:640]
        cossin = RC[:, 640:1280].rearrange("p (t a n) -> p t a n", t=TILES, a=2)
        bs_b = RT[:, 6016:6528]
        lng_b = RT[:, 4992:5504]
        lnb_b = RT[:, 5504:6016]
        wsT = RC[:, 1280:1792].rearrange("p (g n) -> p g n", g=4)
        ws_in = RT[:, 6528:7040].rearrange("p (g n) -> p g n", g=4)

        PS = ctx.enter_context(nc.psum_tensor("PS", [P, 8, 512], F32))
        tp = [PS[:, 0:2, :].rearrange("p a (b n) -> p (a b) n", n=P),
              PS[:, 2:4, :].rearrange("p a (b n) -> p (a b) n", n=P)]
        z1, z2, z3 = PS[:, 4, :], PS[:, 5, 0:256], PS[:, 6, :]
        rows_ps = PS[:, 7, 0:80]
        part_ps = [PS[:, 5, :], PS[:, 7, :]]
        mod_ps = PS[:, 6, 0:32].rearrange("p (m g) -> p m g", g=2)
        ws_ps = PS[:, 4, :].rearrange("p (g n) -> p g n", g=4)

        res = [PS[:, 3 * r:3 * r + 3, :].rearrange("p a n -> p (a n)")[:, 0:T] for r in range(2)]
        sv_ps = [PS[:, 6 + s, :].rearrange("p (g n) -> p g n", g=4) for s in range(2)]
        PADDED = T + 32
        SEGS = ((8, 0, T_PROMPT), (T_PROMPT + 24, T_PROMPT, T_SAMPLE))
        z_pad = [RT[:, PADDED * s:PADDED * (s + 1)] for s in range(2)]
        sum_a, sum_b = (RT[:, PADDED * s:PADDED * (s + 1)] for s in (2, 3))
        gate_sb = RT[:, 5248:5248 + T]
        prod = RT[:, 0:T]
        CSEGS = ((1, 0, T_PROMPT), (T_PROMPT + 3, T_PROMPT, T_SAMPLE))
        cg_sb = RT[:, 1312:1312 + T]
        z_conv = RT[:, 2624:2624 + T + 4]
        taps = RT[:, 3936:3936 + T + 4]
        wg_sb = RC[:, 0:512].rearrange("p (g n) -> p g n", g=4)
        edge = RC[:, 1792:1920].rearrange("p (g e n) -> p g e n", g=4, e=4)
        score_ps = [PS[:, 2 * u:2 * u + 2, :].rearrange("p a n -> p (a n)") for u in range(2)]
        pt_ps = PS[:, 4:6, :].rearrange("p a (b n) -> p (a b) n", n=P)
        o_ps = [PS[:, 6 + u, 0:HD] for u in range(2)]
        part2_ps, part2_sb = PS[:, 6, 256:512], RT[:, 4608:4864]
        mod2_ps = PS[:, 6, 64:128].rearrange("p (g c) -> p g c", g=2)
        modr_ps = PS[0:64, 6, 128:256]
        oT_ps = PS[:, 7, :].rearrange("p (j n) -> p j n", j=4)
        o_row = RC[:, 0:512]
        w_mod = [RY[:, 2048 * s:2048 * s + 2048].rearrange("p (k n) -> p k n", k=KD) for s in range(2)]
        prob = [RT[:, 1024 * u:1024 * u + 1024] for u in range(2)]
        probT = [RT[:, 2048 + 1024 * u:3072 + 1024 * u].rearrange("p (b n) -> p b n", n=P) for u in range(2)]
        sums = small[:, 32:36]
        q_tile = RT[:, 4096:4608].rearrange("p (j n) -> p j n", j=4)

        row = lambda region, i: region[:, D * i:D * i + D]
        g1_b = [row(RY, 0), row(RY, 1)]
        sh2_b, sc2_b = [row(RY, 2), row(RT, 2)], [row(RY, 3), row(RT, 3)]
        ln1g_b, ln1b_b = row(RY, 4), row(RT, 4)
        x_row = [row(R1, s) for s in range(2)]
        x1_row = [row(R1, 2 + s) for s in range(2)]
        h2_row = [row(R1, 4 + s) for s in range(2)]
        h2T = [row(R1, 6 + s).rearrange("p (k n) -> p k n", k=KD) for s in range(2)]
        m_tile = [row(RC, s).rearrange("p (k n) -> p k n", k=KD) for s in range(2)]
        wo_sb = RQ[:, 0:8192].rearrange("p (k n) -> p k n", k=KD)
        flip = RQ[:, 8448:8576]
        rw_sb = RQ[:, 8192:8448].rearrange("p (k n) -> p k n", k=KD)
        xa_row = [row(RW, s) for s in range(2)]
        HALF = T_PROMPT // 2
        TK = 96
        affT = RT[0:TK, 0:HALF]
        y_ps = [PS[:, 2 * s:2 * s + 2, :].rearrange("p a n -> p (a n)") for s in range(2)]
        h2t_ps = PS[:, 4:6, :].rearrange("p a (b n) -> p (a b) n", n=P)
        logit_ps = PS[:, 6, 0:NE]
        lpart_ps, lpart_sb = PS[:, 6, 128:256], RT[:, 5120:5248]
        affT_ps = PS[0:TK, 7, 0:P]
        top_v, top_f = RT[0:TK, 512:640], RT[0:TK, 640:768]
        top_i = sb("top_i", [TK, CAP_P], U32)
        top_ranks = RT[:, 768:960].rearrange("p (a n) -> p a n", a=2)
        first_wins, index_gap = RT[:, 960:960 + NE], RT[:, 976:976 + NE]
        idx_p, idx_s = sb("idx_p", [P, NE], U32), sb("idx_s", [CAP_S, NE], U32)
        gate_p, gate_s = sb("gate_p", [P, NE]), sb("gate_s", [CAP_S, NE])
        get_idx_p, get_idx_s = sb("get_idx_p", [P, 1], U32), sb("get_idx_s", [CAP_S, 1], U32)
        add_idx_p, add_idx_s = sb("add_idx_p", [P, 1], U32), sb("add_idx_s", [CAP_S, 1], U32)
        top_ps = PS[:, 7, 0:2 * TK].rearrange("p (a n) -> p a n", a=2)
        flip_ps = PS[:, 6, 0:2 * NE].rearrange("p (a n) -> p a n", a=2)
        w_half = [RV[:, 0:4096].rearrange("p (k n) -> p k n", k=KD)]
        w_half += [R1[:, 4096 * c:4096 * c + 4096].rearrange("p (k n) -> p k n", k=KD) for c in (4, 3, 2, 1, 0)]
        xg_p, xg_s = RQ[:, 0:D], RQ[0:CAP_S, D:2 * D]
        xgT, gT, outT = (RQ[:, 2048 + 1280 * i:3328 + 1280 * i].rearrange("p (k n) -> p k n", k=KD) for i in range(3))
        out_p, out_s = RQ[:, 5888:6912], RQ[0:CAP_S, 6912:7936]
        silu = [RQ[:, 7936 + CAP * s:7936 + CAP * (s + 1)] for s in range(2)]
        xt_p = PS[:, 0:2, :].rearrange("p a (b n) -> p (a b) n", n=P)
        xt_s = PS[:, 2, 0:KD * CAP_S].rearrange("p (k n) -> p k n", k=KD)
        ab_ps = [PS[:, 3 + s, 0:2 * CAP].rearrange("p (a n) -> p a n", a=2) for s in range(2)]
        op_ps = PS[:, 5:7, :].rearrange("p a n -> p (a n)")
        os_ps = [PS[0:CAP_S, 7, :], PS[0:CAP_S, 2, :]]
        ln2g_b, ln2b_b = row(RY, 0), row(RY, 1)
        y_in = [row(R1, s) for s in range(LAST)]
        y_out = [row(R1, LAST + s) for s in range(LAST)]

        mod2_parts_done, mod2_by_feature, mod2_rows_turned = sems("mod2_parts_done mod2_by_feature mod2_rows_turned")
        mod2_rows_copied, mod2_rows_stored = sems("mod2_rows_copied mod2_rows_stored")
        mod2_weights_in = [sem("mod2_weights_in0"), sem("mod2_weights_in1")]
        row_constants_in, w_o_in, x1_scaled = sems("row_constants_in w_o_in x1_scaled")
        x_row_in = [sem("x_row_in0"), sem("x_row_in1")]
        y_row_stored, h2_row_stored = [sem("y_row_stored0"), sem("y_row_stored1")], [sem("h2_row_stored0"), sem("h2_row_stored1")]
        merged_tile_taken, w_o_product_done, y_gated, x_added = sems("merged_tile_taken w_o_product_done y_gated x_added")
        var2_ready, rstd2_ready, x1_ready, h2_ready = sems("var2_ready rstd2_ready x1_ready h2_ready")
        h2_turned, h2T_copied, logits_done, logit_max_ready = sems("h2_turned h2T_copied logits_done logit_max_ready")
        route_exp_done, affinity_ready, affinity_turned = sems("route_exp_done affinity_ready affinity_turned")
        affinity_copied = sem("affinity_copied")
        top_found, top_turned, top_copied, half2_reversed = sems("top_found top_turned top_copied half2_reversed")
        choice_ready = sem("choice_ready")
        affT_filled, router_zeroed, logit_parts_done = sems("affT_filled router_zeroed logit_parts_done")
        logit_parts_copied, first_merged_tile_taken = sems("logit_parts_copied first_merged_tile_taken")
        expert_half_in = [sem(f"expert_half_in{c}") for c in range(6)]
        rows_gathered, xg_p_turned, xgT_p_copied, xgT_s_copied = sems("rows_gathered xg_p_turned xgT_p_copied xgT_s_copied")
        ab_done, silu_done, gT_ready, w2_product_done = sems("ab_done silu_done gT_ready w2_product_done")
        outT_copied, out_turned, out_p_ready, out_s_ready = sems("outT_copied out_turned out_p_ready out_s_ready")
        out_added = sem("out_added")
        xg_s_turned = sem("xg_s_turned")
        y_tile_in, out_stored = [sem(f"y_tile_in{s}") for s in range(LAST)], [sem(f"out_stored{s}") for s in range(LAST)]
        var3_ready, rstd3_ready, y_centred, y_spread = sems("var3_ready rstd3_ready y_centred y_spread")
        last_ready, ln2_in = sems("last_ready ln2_in")

        w_tile_in, p_tile_in = [sem("w_tile_in0"), sem("w_tile_in1")], [sem("p_tile_in0"), sem("p_tile_in1")]
        result_done, result_used = [sem("result_done0"), sem("result_done1")], [sem("result_used0"), sem("result_used1")]
        spatial_done, spatial_used, ya_ready = sems("spatial_done spatial_used ya_ready")
        pooled_ready, merge_added, pads_ready = sems("pooled_ready merge_added pads_ready")
        wg_in = sem("wg_in")
        q_tile_copied, scores_done, score_max_ready, exp_done = sems("q_tile_copied scores_done score_max_ready exp_done")
        prob_turned, probT_copied, weighted_done = sems("prob_turned probT_copied weighted_done")
        head_out_ready, heads_turned, heads_copied = sems("head_out_ready heads_turned heads_copied")

        N_U, N_B, N_MA, N_D, N_MB, N_MD, N_MC = 0, 4, 8, 16, 28, 36, 44
        R_U, R_B, R_MA, R_MIX, R_D, R_MB, R_MD, R_MC, R_END = 0, 4, 8, 24, 28, 40, 56, 72, 88
        MERGES = {"A": (N_MA, R_MA, 0, 0, y0), "B": (N_MB, R_MB, 1, 8, y1),
                  "D": (N_MD, R_MD, 3, 16, y0), "C": (N_MC, R_MC, 2, 24, y1)}

        zeros_for_ident, ident_ready = sems("zeros_for_ident ident_ready")
        setup_rows_in, silu_c_done, setup_rows_turned = sems("setup_rows_in silu_c_done setup_rows_turned")
        columns_ready = sem("columns_ready")
        w_ada_in = [sem(f"w_ada_in{m}") for m in range(4)]
        mod_ready_to_multiply, mod_parts_done = sems("mod_ready_to_multiply mod_parts_done")
        mod_parts_copied, mod2_parts_copied, mod2_summed = sems("mod_parts_copied mod2_parts_copied mod2_summed")
        mod_summed, mod_ready = sems("mod_summed mod_ready")
        constants_in = sem("constants_in")
        wz_in = [sem("wz_in0"), sem("wz_in1")]
        gains_spread = sem("gains_spread")
        ws_in_sem, ws_turned = sems("ws_in_sem ws_turned")
        x_tile_in = [sem("x_tile_in0"), sem("x_tile_in1")]
        var_ready, rstd_ready, xh_ready, xh_turned = sems("var_ready rstd_ready xh_ready xh_turned")
        h_tile_ready, h_joined = sems("h_tile_ready h_joined")
        z1_done, z2_done, z3_done, z_copied, v_gelu_ready = sems("z1_done z2_done z3_done z_copied v_gelu_ready")
        qk_rotated, v_normed, v_ready, qk_turned, qk_copied = sems("qk_rotated v_normed v_ready qk_turned qk_copied")
        vector_own, pool_own = sems("vector_own pool_own")
        block = ctx.enter_context(nc.Block())

        def ln_cols(which, s):
            return small[:, 16 * which + 8 * s:16 * which + 8 * s + 8]

        def all_tiles(eng, attend, mark=None):
            n_p = T_PROMPT // P
            for keys, t0, t1 in ((T_PROMPT, 0, n_p), (T_SAMPLE, n_p, TILES)):
                attend(t0, keys, first=True)
                if t1 - t0 > 2:
                    with eng.Fori(t0 + 1, t1 - 1) as t:
                        if mark:
                            mark.enter(t - t0 - 1, mark.per_tile)
                        attend(t, keys)
                        if mark:
                            mark.leave(t1 - t0 - 2)
                attend(t1 - 1, keys, last=True)

        @block.sync
        def _(sp):
            sp.dma_start(rows_in[0:16, :], c.rearrange("g (k n) -> (g k) n", n=P)).then_inc(setup_rows_in, 16)
            sp.dma_start(rows_in[16:64, :], b_ada.rearrange("(k n) -> k n", n=P)).then_inc(setup_rows_in, 16)
            sp.dma_start(rows_in[64:76, :], d_conv.rearrange("j (k n) -> (j k) n", n=P)).then_inc(setup_rows_in, 16)
            sp.dma_start(rows_in[76:80, :], b_scale.rearrange("(k n) -> k n", n=P)).then_inc(setup_rows_in, 16)
            for m in range(4):
                sp.dma_start(w_ada_buf[m], w_ada[:, 512 * m:512 * m + 512].rearrange("(k p) n -> p k n", p=P)) \
                  .then_inc(w_ada_in[m], 16)
                if m < 2:
                    sp.dma_start(x_in[m], x[m * P:(m + 1) * P, :]).then_inc(x_tile_in[m], 16)
            sp.dma_start(wz[:, :, 0:768], w_in[:, COL_C:COL_C + 768].rearrange("(k p) n -> p k n", p=P)).then_inc(wz_in[0], 16)
            sp.dma_start(ws_in, a_ws.rearrange("g p q -> p g q")).then_inc(ws_in_sem, 16)
            sp.dma_start(wz[:, :, 768:1280], w_in[:, COL_VG:COL_VG + 512].rearrange("(k p) n -> p k n", p=P)).then_inc(wz_in[1], 16)
            with sp.Fori(1, PAIRS) as i:
                for s in range(2):
                    sp.wait_ge(xh_ready, 2 * i + s - 1)
                    sp.dma_start(x_in[s], x[ds(i * 256 + s * P, P), :]).then_inc(x_tile_in[s], 16)

            def load_w(slot, cols, r_before, count=None):
                if r_before is not None:
                    sp.wait_ge(result_done[r_before % 2], r_before // 2 + 1 if count is None else count)
                sp.dma_start(w_tile[slot], w_in[:, ds(cols, P)].rearrange("(k p) n -> p k n", p=P)).then_inc(w_tile_in[slot], 16)

            for j in range(2):
                sp.wait_ge(z3_done, TILES - 1 + j)
                sp.wait_ge(h_joined, TILES - 1 + j)
                load_w(j, COL_U + P * j, None)
            sp.wait_ge(v_normed, TILES)
            sp.wait_ge(qk_rotated, TILES)
            sp.dma_start(wg_sb, b_wg.rearrange("g c d -> c g d")).then_inc(wg_in, 16)
            for j in range(2, 4):
                load_w(j % 2, COL_U + P * j, j - 2)
            for j in range(4):
                load_w(j % 2, COL_B + P * j, R_B + j - 2)

            def load_merge(name, r_last, between=None):
                n0, r0, branch, m0, _ = MERGES[name]

                def turn(i, first):
                    for s in range(2):
                        col = COL_G + branch * D + s * P
                        load_w(s, col + i * 256, r_last[s] if first else 0, None if first else r0 // 2 + 2 * i + s - 1)
                        if not first:
                            wait_apart(sp, result_done[1], r0 // 2 + 2 * i + s - 1, wg_in, 16)
                        elif m0:
                            sp.wait_ge(result_done[1], r_proj + s)
                        sp.dma_start(p_tile[s], p_all[branch, :, ds(i * 256 + s * P, P)].rearrange("(k p) n -> p k n", p=P)) \
                          .then_inc(p_tile_in[s], 16)

                r_proj = {"A": 0, "B": R_MA // 2 + 7, "D": R_MB // 2 + 7, "C": R_MD // 2 + 7}[name]
                turn(0, True)
                if between:
                    between()
                with sp.Fori(1, 4) as i:
                    turn(i, False)

            def load_mod(first, end):
                with sp.Fori(first, end) as i:
                    for s in range(2):
                        sp.wait_ge(mod2_parts_done, 2 * i + s - 1)
                        sp.dma_start(w_mod[s], w_ada[:, ds(i * 512 + 2 * D + 256 * s, 256)].rearrange("(k p) n -> p k n", p=P)) \
                          .then_inc(mod2_weights_in[s], 16)

            load_merge("A", (R_B + 2, R_B + 3))
            for j in range(4):
                for m, col in enumerate((COL_CG, COL_X, COL_BG)):
                    n = 3 * j + m
                    load_w(n % 2, col + P * j, R_MA + 12 + 2 * n if n < 2 else R_D + n - 2)
            load_merge("B", (R_D + 10, R_D + 11))
            load_merge("D", (R_MB + 12, R_MB + 14))
            sp.wait_ge(result_done[1], R_MC // 2)
            for s in range(2):
                sp.dma_start(w_mod[s], w_ada[:, 2 * D + 256 * s:2 * D + 256 * s + 256].rearrange("(k p) n -> p k n", p=P)) \
                  .then_inc(mod2_weights_in[s], 16)
            load_mod(1, 8)

            def everywhere(dst, src):
                return sp.dma_start(dst, src.rearrange("(a n) -> a n", a=1).to_broadcast([P, D]))

            def load_rows():
                sp.wait_ge(mod2_rows_copied, 1)
                sp.dma_start(mod_rows.rearrange("g (k n) -> (g k) n", n=P), rows_in[0:64, :]).then_inc(mod2_rows_stored, 16)
                sp.wait_ge(weighted_done, N_Q * TILES)
                sp.dma_start(wo_sb, w_o.rearrange("(k p) n -> p k n", p=P)).then_inc(w_o_in, 16)
                sp.wait_ge(router_zeroed, 1)
                sp.dma_start(rw_sb[:, :, 0:NE], r_w.rearrange("(k p) n -> p k n", p=P)).then_inc(w_o_in, 16)
                sp.wait_ge(mod2_rows_stored, 16)
                for g in range(2):
                    for j, dst in enumerate((g1_b, sh2_b, sc2_b)):
                        everywhere(dst[g], mod_rows[g, D * j:D * j + D]).then_inc(row_constants_in, 16)
                everywhere(ln1g_b, ln1_g).then_inc(row_constants_in, 16)
                everywhere(ln1b_b, ln1_b).then_inc(row_constants_in, 16)

            load_merge("C", (R_MD + 12, R_MD + 14), load_rows)

            sp.wait_ge(result_done[0], R_END // 2)
            for s in range(2):
                sp.dma_start(x_row[s], x[s * P:(s + 1) * P, :]).then_inc(x_row_in[s], 16)

            def rows_turn(i, more):
                for s in range(2):
                    t = 2 * i + s
                    at = sp.snap(256 * i + P * s) if not isinstance(i, int) else 256 * i + P * s
                    if more:
                        sp.wait_ge(x_added, t + 1)
                        sp.dma_start(x_row[s], x[ds(at + 256, P), :]).then_inc(x_row_in[s], 16)
                    sp.wait_ge(x1_scaled, t + 1)
                    sp.dma_start(y_rows[ds(at, P), :], xa_row[s]).then_inc(y_row_stored[s], 16)
                    sp.wait_ge(h2_ready, t + 1)
                    sp.dma_start(h2_rows[ds(at, P), :], h2_row[s]).then_inc(h2_row_stored[s], 16)

            HALVES = ((e_w1, 0), (e_w3, 0), (e_w1, 512), (e_w3, 512), (e_w2, 0), (e_w2, 512))

            def load_half(e, c):
                w, lo = HALVES[c]
                sp.dma_start(w_half[c], w[ds(e, 1), :, lo:lo + 512].rearrange("a (k p) n -> p (a k) n", p=P)) \
                  .then_inc(expert_half_in[c], 16)

            sp.wait_ge(result_done[1], R_END // 2)
            load_half(0, 0)
            with sp.Fori(0, PAIRS - 1) as i:
                rows_turn(i, True)
            sp.wait_ge(merged_tile_taken, TILES - 1)
            for part in (1, 2):
                load_half(0, part)
            rows_turn(PAIRS - 1, False)
            sp.wait_ge(affinity_ready, TILES)
            sp.wait_ge(affinity_turned, TILES)
            for s in range(2):
                sp.wait_ge(y_row_stored[s], 16 * PAIRS)
                sp.wait_ge(h2_row_stored[s], 16 * PAIRS)
            for part in (3, 4, 5):
                load_half(0, part)
            everywhere(ln2g_b, ln2_g).then_inc(ln2_in, 16)
            everywhere(ln2b_b, ln2_b).then_inc(ln2_in, 16)
            with sp.Fori(1, NE) as e:
                for part, (done, n) in enumerate(((ab_done, 4), (ab_done, 4), (ab_done, 8), (ab_done, 8), (w2_product_done, 4), (w2_product_done, 8))):
                    sp.wait_ge(done, 8 * e - 8 + n)
                    load_half(e, part)

            sp.wait_ge(out_added, 32 * NE)
            for s in range(LAST):
                sp.dma_start(y_in[s], y_rows[P * s:P * s + P, :]).then_inc(y_tile_in[s], 16)

            def store_last(i, more):
                for s in range(LAST):
                    t = LAST * i + s
                    if more:
                        sp.wait_ge(y_centred, t + 1)
                        sp.dma_start(y_in[s], y_rows[P * (t + LAST):P * (t + LAST) + P, :]).then_inc(y_tile_in[s], 16)
                    sp.wait_ge(last_ready, t + 1)
                    sp.dma_start(out[P * t:P * t + P, :], y_out[s]).then_inc(out_stored[s], 16)

            store_last(0, True)
            store_last(1, False)
            for s in range(LAST):
                sp.wait_ge(out_stored[s], 32)

        @block.gpsimd
        def _(pool):
            own = Chain(pool, pool_own)
            columns = itertools.cycle(range(16))

            def carrier():
                at = next(columns)
                own.did(pool.tensor_tensor(carried[:, at:at + 1], half[:, 0:1], half[:, 1:2], ALU.add))

            pool.memset(ident[:, :], 0.0).then_inc(zeros_for_ident, 1)
            own.did(pool.memset(half[:, :], -0.5))
            pool.wait_ge(zeros_for_ident, 1)
            pool.affine_select(out=ident[:, :], in_=ident[:, :], compare_op=ALU.not_equal, fill=1.0,
                               base=0, pattern=[[-1, P]], channel_multiplier=1).then_inc(ident_ready, 1)
            pool.dma_start(cossin, rope).then_inc(constants_in, 16)
            pool.dma_start(gqk[:, 0:HD], c_q_g.rearrange("(a n) -> a n", a=1).to_broadcast([P, HD])).then_inc(constants_in, 16)
            pool.dma_start(gqk[:, 512:512 + HD], c_k_g.rearrange("(a n) -> a n", a=1).to_broadcast([P, HD])).then_inc(constants_in, 16)
            pool.dma_start(lng_b, a_ln_g.rearrange("(a n) -> a n", a=1).to_broadcast([P, W_BR])).then_inc(constants_in, 16)
            pool.dma_start(lnb_b, a_ln_b.rearrange("(a n) -> a n", a=1).to_broadcast([P, W_BR])).then_inc(constants_in, 16)
            pool.dma_start(bs_b, a_bs.rearrange("g p -> (g p)").rearrange("(a n) -> a n", a=1).to_broadcast([P, W_BR])).then_inc(constants_in, 16)
            pool.dma_start(rb_b[:, :], r_b.rearrange("(a n) -> a n", a=1).to_broadcast([P, NE])).then_inc(constants_in, 16)
            pool.dma_start(edge, inv_count.rearrange("g e n -> (g e n)").rearrange("(a n) -> a n", a=1).to_broadcast([P, 128])).then_inc(constants_in, 16)
            def power(cols, n, t_sem, count):
                pool.wait_ge(t_sem, count)
                pool.tensor_tensor(cols, cols, half[:, 0:n], ALU.pow).then_inc(rstd_ready, 1)

            def turn(i, ahead, front=False):
                for s in range(2):
                    t = 2 * i + s
                    n0 = 3 * t + 2
                    power(small[:, 32 + 16 * s:42 + 16 * s], N_QK, var_ready, n0 + 1 if ahead else 3 * t + 3 - s)
                    if ahead:
                        power(ln_cols(0, s)[:, 7:8], 1, var_ready, n0 + 2)
                    pool.wait_ge(h_tile_ready, t + 1)
                    pool.tensor_copy(hT[:, :, ds(i * 256 + s * P, P)], h_tile[s]).then_inc(h_joined, 1)
                    power(ln_cols(1, s)[:, 7:8], 1, var_ready, n0 + 3 if ahead else 3 * t + 4 - s)
                    pool.wait_ge(v_normed, t + 1)
                    carrier()
                    v = vln[:, ds(t, 1), :].rearrange("p a n -> p (a n)")
                    own.did(pool.tensor_tensor(v, v, lng_b, ALU.mult))
                    own.settle()
                    carrier()
                    pool.tensor_tensor(v, v, lnb_b, ALU.add).then_inc(v_ready, 1)

            own.settle()
            power(ln_cols(0, 0)[:, 7:8], 1, var_ready, 1)
            power(ln_cols(0, 1)[:, 7:8], 1, var_ready, 2)
            pool.wait_ge(constants_in, 8 * 16)
            for h in range(1, N_Q):
                own.did(pool.tensor_copy(gqk[:, h * HD:(h + 1) * HD], gqk[:, 0:HD]))
            pool.tensor_copy(gqk[:, 576:640], gqk[:, 512:576]).then_inc(gains_spread, 1)
            own.settle()

            with pool.Fori(0, PAIRS - 1) as i:
                own.enter(i, 6)
                turn(i, True)
                own.leave(PAIRS - 1)
            turn(PAIRS - 1, False)
            pool.wait_ge(qk_copied, TILES)
            for s in range(2):
                pool.wait_ge(result_used[s], R_MB // 2)
            for j in range(4):
                pool.tensor_copy(q_tile[:, j, :], qT[:, j, 0:P]).then_inc(q_tile_copied, 1)
            with pool.Fori(1, TILES) as t:
                for j in range(4):
                    pool.wait_ge(merge_added, 16)
                    pool.wait_ge(scores_done, N_Q * t + 2 * j - 6)
                    pool.tensor_copy(q_tile[:, j:j + 1, :], qT[:, j:j + 1, ds(t * P, P)]).then_inc(q_tile_copied, 1)

            def power2(var_sem, rstd_sem, cols, count):
                pool.wait_ge(var_sem, count)
                pool.tensor_tensor(cols[:, 7:8], cols[:, 7:8], half[:, 0:1], ALU.pow).then_inc(rstd_sem, 1)

            def take(i, s):
                carrier()
                pool.tensor_copy(m_tile[s], merged[:, :, ds(256 * i + P * s, P)]).then_inc(merged_tile_taken, 1)

            pool.wait_ge(weighted_done, N_Q * TILES)
            pool.memset(rw_sb, 0.0).then_inc(router_zeroed, 1)
            own.did(pool.memset(flip, 0.0))
            own.settle()
            pool.affine_select(out=flip, in_=flip, compare_op=ALU.not_equal, fill=1.0,
                               base=1 - P, pattern=[[1, P]], channel_multiplier=1).then_inc(ident_ready, 1)
            pool.wait_ge(merge_added, 24)
            take(0, 1)

            def rows_turn(i, more):
                for s in range(2):
                    t = 2 * i + s
                    power2(var2_ready, rstd2_ready, ln_cols(1, s), 2 * t + 1)
                    power2(var2_ready, rstd2_ready, ln_cols(2, s), 2 * t + 2)
                    if more:
                        pool.wait_ge(w_o_product_done, t + 1)
                        take(i + 1, s)

            with pool.Fori(0, PAIRS - 1) as i:
                own.enter(i, 2)
                rows_turn(i, True)
                own.leave(PAIRS - 1)
            rows_turn(PAIRS - 1, False)

            def indexed(e, pairs, wait, count):
                pool.wait_ge(wait, count)
                carrier()
                for dst, src in pairs:
                    own.did(pool.tensor_copy(dst, src[:, ds(e, 1)]))
                own.settle()
                carrier()

            def gather(e, wait, count):
                indexed(e, ((get_idx_p[:, :], idx_p), (get_idx_s[:, :], idx_s)), wait, count)
                for dst, idx in ((xg_p, get_idx_p), (xg_s, get_idx_s)):
                    pool.indirect_dma_start(out=dst, out_offset=None, in_=h2_rows,
                                            in_offset=bass.IndirectOffsetOnAxis(ap=idx[:, 0:1], axis=0)).then_inc(rows_gathered, 16)

            def scatter(e, first=False):
                if not first:
                    pool.wait_ge(out_added, 32 * e)
                    carrier()
                pool.wait_ge(out_p_ready, e + 1)
                carrier()
                indexed(e, ((add_idx_p[:, :], idx_p), (add_idx_s[:, :], idx_s)), out_s_ready, e + 1)
                for src, idx in ((out_p, add_idx_p), (out_s, add_idx_s)):
                    pool.indirect_dma_start(out=y_rows, out_offset=bass.IndirectOffsetOnAxis(ap=idx[:, 0:1], axis=0),
                                            in_=src, in_offset=None, compute_op=ALU.add).then_inc(out_added, 16)

            for s in range(2):
                pool.wait_ge(h2_row_stored[s], 16 * PAIRS)
                pool.wait_ge(y_row_stored[s], 16 * PAIRS)
            pool.wait_ge(top_turned, 1)
            gather(0, choice_ready, 4)
            gather(1, xg_s_turned, 1)
            scatter(0, True)
            n = own.n
            gather(2, xg_s_turned, 2)
            scatter(1)
            per = own.n - n
            with pool.Fori(2, NE - 1) as e:
                own.enter(e - 2, per)
                gather(e + 1, xg_s_turned, e + 1)
                scatter(e)
                own.leave(NE - 3)
            scatter(NE - 1)

            pool.wait_ge(ln2_in, 32)
            power2(var3_ready, rstd3_ready, ln_cols(1, 0), 1)
            for t in range(TILES):
                if t + 1 < TILES:
                    power2(var3_ready, rstd3_ready, ln_cols(1, (t + 1) % 2), t + 2)
                pool.wait_ge(y_spread, t + 1)
                pool.tensor_tensor(y_out[t % LAST], y_out[t % LAST], ln2b_b, ALU.add).then_inc(last_ready, 1)

        @block.scalar
        def _(act):
            act.wait_ge(setup_rows_in, 64)
            act.activation(rows_in[0:16, :], rows_in[0:16, :], ACT.Silu).then_inc(silu_c_done, 1)

            for m in range(4):
                act.wait_ge(mod_parts_done, m + 1)
                if m >= 2:
                    act.wait_ge(mod_summed, m - 1)
                act.activation(part_sb[m % 2], part_ps[m % 2], ACT.Copy).then_inc(mod_parts_copied, 1)

            def modulate(i, s, group):
                t = 2 * i + s
                act.wait_ge(xh_turned, t + 1)
                if not (isinstance(i, int) and i == 0):
                    act.wait_ge(z3_done, t - 1)
                    act.wait_ge(h_joined, t - 1)
                for k in range(KD):
                    last = act.activation(h_tile[s][:, k, :], tp[s][:, k, :], ACT.Identity,
                                          bias=modT[:, k, group:group + 1],
                                          scale=modT[:, 8 + k, group:group + 1])
                last.then_inc(h_tile_ready, 1)

            def keep_qk(i, s):
                act.wait_ge(qk_turned, 2 * i + s + 1)
                act.activation(qT[:, :, ds(i * 256 + s * P, P)], tp[s][:, 0:4, :], ACT.Copy)
                act.activation(kT[:, :, ds(i * 256 + s * P, P)], tp[s][:, 4:6, :], ACT.Copy).then_inc(qk_copied, 1)

            def turn(i, group):
                first = isinstance(i, int) and i == 0
                for s in range(2):
                    t = 2 * i + s
                    act.wait_ge(z1_done, t + 1)
                    if not first:
                        act.wait_ge(qk_rotated, t - 1)
                    act.activation(z_qkv[s][:, 0:512], z1, ACT.Copy).then_inc(z_copied, 1)
                    if s == 0 and not first:
                        keep_qk(i - 1, 0)
                    act.wait_ge(z2_done, t + 1)
                    act.activation(z_qkv[s][:, 512:768], z2, ACT.Copy).then_inc(z_copied, 1)
                    if s == 1 and group is not None:
                        modulate(i + 1, 0, group)
                    act.wait_ge(z3_done, t + 1)
                    if not first:
                        act.wait_ge(v_normed, t - 1)
                    act.activation(v_gelu[s], z3, ACT.Gelu_apprx_tanh).then_inc(v_gelu_ready, 1)
                    if s == 0 and not first:
                        keep_qk(i - 1, 1)
                    if s == 1 and group is not None:
                        modulate(i + 1, 1, group)

            act.wait_ge(mod_ready, 1)
            for s in range(2):
                modulate(0, s, 0)
            turn(0, 0)
            with act.Fori(1, PROMPT_PAIRS - 1) as i:
                turn(i, 0)
            turn(PROMPT_PAIRS - 1, 1)
            turn(PROMPT_PAIRS, None)
            for s in range(2):
                keep_qk(PAIRS - 1, s)

            act.wait_ge(xh_turned, TILES)
            act.wait_ge(xh_ready, TILES)
            for j in range(4):
                act.wait_ge(result_done[j % 2], j // 2 + 1)
                act.activation(y0[:, j, :], res[j % 2], ACT.Gelu_apprx_tanh).then_inc(result_used[j % 2], 1)
            act.wait_ge(pads_ready, 1)
            for g in range(4):
                r = R_B + g
                act.wait_ge(result_done[r % 2], r // 2 + 1)
                if g >= 2:
                    act.wait_ge(pooled_ready, g - 1)
                for at, lo, n in SEGS:
                    last = act.activation(z_pad[g % 2][:, at:at + n], res[r % 2][:, lo:lo + n], ACT.Copy)
                last.then_inc(result_used[r % 2], 1)

            def gates(name):
                _, r0, _, m0, _ = MERGES[name]

                def turn(i, first):
                    for s in range(2):
                        act.wait_ge(result_done[0], r0 // 2 + 2 * i + s + 1)
                        act.wait_ge(result_used[1], r0 // 2 + 2 * i + s)
                        act.activation(gate_sb, res[0], ACT.Sigmoid).then_inc(result_used[0], 1)

                turn(0, True)
                with act.Fori(1, 4) as i:
                    turn(i, False)

            gates("A")
            for g in range(4):
                r = R_MIX + g
                act.wait_ge(result_done[r % 2], r // 2 + 1)
                act.activation(y1[:, g, :], res[r % 2], ACT.Copy, scale=colT[:, 76 + g:77 + g]).then_inc(result_used[r % 2], 1)
            for j in range(4):
                r = R_D + 3 * j
                act.wait_ge(result_done[r % 2], r // 2 + 1)
                if j == 0:
                    act.wait_ge(pooled_ready, 4)
                else:
                    act.wait_ge(result_used[(r - 2) % 2], (r - 2) // 2 + 1)
                act.activation(cg_sb, res[r % 2], ACT.Copy).then_inc(result_used[r % 2], 1)
            gates("B")
            gates("D")

            def attend(t, keys, first=False, last=False):
                n = N_Q * t

                def exp(h):
                    u = h % 2
                    act.wait_ge(score_max_ready, n + h + 1)
                    if not (isinstance(t, int) and t == 0 and h < 2):
                        act.wait_ge(prob_turned, n + h - 1)
                    act.activation(prob[u][:, 0:keys], score_ps[u][:, 0:keys], ACT.Exp,
                                   bias=small[:, u:u + 1], scale=HD ** -0.5,
                                   accum_out=sums[:, h % 4:h % 4 + 1]).then_inc(exp_done, 1)

                if first:
                    exp(0)
                for h in range(N_Q):
                    if h + 1 < N_Q or not last:
                        exp(h + 1)
                    act.wait_ge(prob_turned, n + h + 1)
                    if not (isinstance(t, int) and t == 0 and h < 2):
                        act.wait_ge(weighted_done, n + h - 1)
                    act.activation(probT[h % 2][:, 0:keys // P, :], pt_ps[:, 0:keys // P, :], ACT.Copy).then_inc(probT_copied, 1)

            all_tiles(act, attend)
            act.wait_ge(mod2_rows_turned, 1)
            act.activation(rows_in[0:64, :], modr_ps, ACT.Copy).then_inc(mod2_rows_copied, 1)
            gates("C")

            def route(part, t):
                s = t % 2
                if part == "x1":
                    act.wait_ge(x1_ready, t + 1)
                    if t >= 2:
                        act.wait_ge(y_row_stored[s], 8 * (t - s))
                    act.activation(xa_row[s], x1_row[s], ACT.Copy, scale=ALPHA).then_inc(x1_scaled, 1)
                elif part == "h":
                    act.wait_ge(h2_turned, t + 1)
                    act.activation(h2T[s], h2t_ps, ACT.Copy).then_inc(h2T_copied, 1)
                elif part == "part":
                    act.wait_ge(logit_parts_done, t + 1)
                    act.activation(lpart_sb, lpart_ps, ACT.Copy).then_inc(logit_parts_copied, 1)
                elif part == "aff":
                    act.wait_ge(affinity_turned, t + 1)
                    row, col = t * P // HALF * 32, t * P % HALF
                    act.activation(affT[row:row + NE, col:col + P], affT_ps[row:row + NE, :], ACT.Copy).then_inc(affinity_copied, 1)
                else:
                    act.wait_ge(logit_max_ready, t + 1)
                    act.activation(aff_t[:, s, 1, :], aff_t[:, s, 0, :], ACT.Exp, bias=small[:, 2 * s:2 * s + 1],
                                   accum_out=small[:, 2 * s + 1:2 * s + 2]).then_inc(route_exp_done, 1)

            act.wait_ge(result_done[1], R_END // 2)
            act.wait_ge(merge_added, 24)
            act.activation(m_tile[0], merged[:, :, 0:P], ACT.Copy).then_inc(first_merged_tile_taken, 1)
            act.wait_ge(affT_filled, 1)
            route("x1", 0)
            for t in range(TILES):
                route("h", t)
                if t:
                    route("exp", t - 1)
                if t + 1 < TILES:
                    route("x1", t + 1)
                route("part", t)
                if t:
                    route("aff", t - 1)
            route("exp", TILES - 1)
            route("aff", TILES - 1)

            def expert(e, more):
                for j in range(KD):
                    act.wait_ge(ab_done, 8 * e + j + 1)
                    if not (isinstance(e, int) and e == 0 and j < 2):
                        act.wait_ge(gT_ready, 8 * e + j - 1)
                    act.activation(silu[j % 2], ab_ps[j % 2][:, 0, :], ACT.Silu).then_inc(silu_done, 1)
                if more:
                    act.wait_ge(xg_p_turned, e + 2)
                    act.activation(xgT[:, :, 0:CAP_P], xt_p, ACT.Copy).then_inc(xgT_p_copied, 1)
                act.wait_ge(out_turned, e + 1)
                if not (isinstance(e, int) and e == 0):
                    act.wait_ge(out_added, 32 * e)
                act.activation(out_p, op_ps, ACT.Copy, scale=gate_p[:, ds(e, 1)]).then_inc(out_p_ready, 1)

            act.wait_ge(xg_p_turned, 1)
            act.activation(xgT[:, :, 0:CAP_P], xt_p, ACT.Copy).then_inc(xgT_p_copied, 1)
            act.wait_ge(choice_ready, 4)
            expert(0, True)
            with act.Fori(1, NE - 1) as e:
                expert(e, True)
            expert(NE - 1, False)

            for t in range(TILES):
                act.wait_ge(rstd3_ready, t + 1)
                act.wait_ge(y_centred, t + 1)
                act.activation(y_out[t % LAST], y_out[t % LAST], ACT.Copy, scale=ln_cols(1, t % 2)[:, 7:8]).then_inc(y_spread, 1)

        @block.vector
        def _(dve):
            own = Chain(dve, vector_own)

            def norm_stats(src, cols, bn, n):
                for j in range(n // 512):
                    own.did(dve.bn_stats(bn[:, 6 * j:6 * j + 6], src[:, 512 * j:512 * j + 512]))
                own.settle()
                own.did(dve.tensor_copy(carry[:, 0:1], half[:, 0:1]))
                own.did(dve.bn_aggr(cols[:, 0:2], bn[:, 0:6 * (n // 512)]))
                own.settle()
                dve.tensor_scalar(cols[:, 7:8], cols[:, 1:2], LN_EPS, None, ALU.add).then_inc(var_ready, 1)

            bn = aff_t[:, 0, 0, 0:12]

            def ln_x_stats(i, s, n_loads):
                dve.wait_ge(x_tile_in[s], n_loads)
                norm_stats(x_in[s], ln_cols(0, s), bn, D)

            def ln_x_apply(s, tile_before, rs_count, first):
                dve.wait_ge(rstd_ready, rs_count)
                if not first:
                    dve.wait_ge(xh_turned, tile_before)
                cols = ln_cols(0, s)
                dve.tensor_scalar(xh[s], x_in[s], cols[:, 0:1], cols[:, 7:8], ALU.subtract, ALU.mult).then_inc(xh_ready, 1)

            dve.wait_ge(setup_rows_turned, 1)
            dve.wait_ge(pool_own, 1)
            dve.tensor_copy(colT[:, :], rows_ps).then_inc(columns_ready, 1)
            own.did(dve.memset(c_pad[:, :, :], 0.0))
            own.settle()
            dve.wait_ge(columns_ready, 1)
            own.did(dve.tensor_copy(c_pad[:, :, 0:2], colT[:, 0:16].rearrange("p (g k) -> p k g", g=2)))
            dve.wait_ge(ident_ready, 1)
            own.settle()
            dve.tensor_reduce(every32[:, :], ident[:, :].rearrange("p (a n) -> p n a", n=32)[:, 0:NE, :], AX.X, ALU.add).then_inc(mod_ready_to_multiply, 1)
            for s in range(2):
                ln_x_stats(0, s, 16)
                ln_x_apply(s, 0, s + 1, True)
            dve.wait_ge(mod_summed, 4)
            dve.wait_ge(columns_ready, 1)
            own.did(dve.tensor_tensor(modT[:, :, :], mod_ps, colT[:, 16:32].unsqueeze(2).to_broadcast([P, 16, 2]), ALU.add))
            own.settle()
            dve.tensor_scalar(modT[:, 8:16, :], modT[:, 8:16, :], 1.0, None, ALU.add).then_inc(mod_ready, 1)
            dve.wait_ge(ws_turned, 1)
            dve.tensor_copy(wsT, ws_ps).then_inc(ws_turned, 1)

            def turn(i, ahead):
                for s in range(2):
                    t = 2 * i + s
                    n0 = 3 * t + 2
                    z = z_qkv[s]
                    dve.wait_ge(z_copied, 2 * t + 2)
                    own.did(dve.tensor_tensor(r_sq, z[:, 0:640], z[:, 0:640], ALU.mult))
                    own.did(dve.tensor_copy(va[:, ds(t, 1), :].rearrange("p a n -> p (a n)"), z[:, 640:768]))
                    own.settle()
                    rs = small[:, 32 + 16 * s:42 + 16 * s]
                    own.did(dve.tensor_reduce(rs, r_sq.rearrange("p (h n) -> p h n", n=HD), AX.X, ALU.add))
                    own.settle()
                    dve.tensor_scalar(rs, rs, 1.0 / HD, RMS_EPS, ALU.mult, ALU.add).then_inc(var_ready, 1)
                    if ahead:
                        ln_x_stats(i, s, 16 * (i + 2))
                    if ahead:
                        ln_x_apply(s, t + 1, n0 + 2, False)
                    dve.wait_ge(rstd_ready, n0 + 1 if ahead else 3 * t + 3 - s)
                    v3 = lambda a: a.rearrange("p (h n) -> p h n", n=HD)
                    own.did(dve.tensor_tensor(v3(r_n), v3(z[:, 0:640]), rs.unsqueeze(2).to_broadcast([P, N_QK, HD]), ALU.mult))
                    own.settle()
                    own.did(dve.tensor_tensor(r_sq, r_n, gqk, ALU.mult))
                    own.settle()
                    pair = r_sq.rearrange("p (h n two) -> p h n two", n=32, two=2)
                    cs = cossin[:, ds(t, 1), :, :].rearrange("p t a n -> p (t a) n")
                    cos = cs[:, 0:1, :].to_broadcast([P, N_QK, 32])
                    sin = cs[:, 1:2, :].to_broadcast([P, N_QK, 32])
                    h3 = lambda a: a.rearrange("p (h n) -> p h n", n=32)
                    if not (isinstance(i, int) and i == 0):
                        dve.wait_ge(qk_turned, t - 1)
                    for part, (ca, cb, op) in enumerate(((cos, sin, ALU.subtract), (sin, cos, ALU.add))):
                        if part:
                            own.settle()
                        own.did(dve.tensor_tensor(h3(r_a), pair[:, :, :, 0], ca, ALU.mult))
                        own.did(dve.tensor_tensor(h3(r_b2), pair[:, :, :, 1], cb, ALU.mult))
                        own.settle()
                        oq = qk_out[s][:, 0:512].rearrange("p (h n two) -> p h n two", n=32, two=2)[:, :, :, part]
                        own.did(dve.tensor_tensor(oq, h3(r_a)[:, 0:N_Q, :], h3(r_b2)[:, 0:N_Q, :], op))
                        for copy in range(2):
                            ok = qk_out[s][:, 512:768].rearrange("p (g c n two) -> p g c n two", g=2, c=2, two=2)[:, :, copy, :, part]
                            last = dve.tensor_tensor(ok, h3(r_a)[:, N_Q:N_QK, :], h3(r_b2)[:, N_Q:N_QK, :], op)
                            if part == 0 or copy == 0:
                                own.did(last)
                            else:
                                last.then_inc(qk_rotated, 1)
                    dve.wait_ge(v_gelu_ready, t + 1)
                    norm_stats(v_gelu[s], ln_cols(1, s), bn, W_BR)
                    dve.wait_ge(rstd_ready, n0 + 3 if ahead else 3 * t + 4 - s)
                    cols = ln_cols(1, s)
                    dve.tensor_scalar(vln[:, ds(t, 1), :].rearrange("p a n -> p (a n)"), v_gelu[s],
                                      cols[:, 0:1], cols[:, 7:8], ALU.subtract, ALU.mult).then_inc(v_normed, 1)

            dve.wait_ge(gains_spread, 1)
            turn_first = own.n
            turn(0, True)
            per = own.n - turn_first
            with dve.Fori(1, PAIRS - 1) as i:
                own.enter(i - 1, per)
                turn(i, True)
                own.leave(PAIRS - 2)
            turn(PAIRS - 1, False)

            own.settle()
            dve.wait_ge(qk_turned, TILES)
            dve.wait_ge(qk_rotated, TILES)
            for s in range(2):
                own.did(dve.memset(z_pad[s], 0.0))
            own.settle()
            dve.tensor_copy(pads_set[:, :], z_pad[0][:, 0:1]).then_inc(pads_ready, 1)
            dve.wait_ge(result_used[0], 2)
            dve.wait_ge(result_used[1], 2)
            gate3 = gate_sb[:, 0:512].rearrange("p (g n) -> p g n", g=4)
            b3 = bs_b.rearrange("p (g n) -> p g n", g=4)
            for t in range(TILES):
                dve.wait_ge(spatial_done, t + 1)
                u = y0[:, :, t * P:(t + 1) * P]
                dve.tensor_tensor(gate3, sv_ps[t % 2], b3, ALU.add).then_inc(spatial_used, 1)
                dve.wait_ge(spatial_used, t + 1)
                dve.tensor_tensor(u, u, gate3, ALU.mult).then_inc(ya_ready, 1)
                dve.wait_ge(ya_ready, t + 1)
            for g, w in enumerate(WINDOWS):
                z = z_pad[g % 2]
                dve.wait_ge(result_used[g % 2], (R_B + g) // 2 + 1)
                n = PADDED
                own.settle()
                own.did(dve.tensor_tensor(sum_a[:, 1:n], z[:, 0:n - 1], z[:, 1:n], ALU.add))
                src, dst, a = sum_a, sum_b, 1
                while 2 * a < w:
                    own.settle()
                    own.did(dve.tensor_tensor(dst[:, 2 * a:n - 2 * a], src[:, a:n - 3 * a], src[:, 3 * a:n - a], ALU.add))
                    src, dst, a = dst, src, 2 * a
                own.settle()
                for at, lo, m in SEGS:
                    own.did(dve.scalar_tensor_tensor(out=y1[:, g, lo:lo + m], in0=src[:, at:at + m], scalar=1.0 / w,
                                                     in1=z[:, at:at + m], op0=ALU.mult, op1=ALU.subtract))
                for e, (at, lo, m) in enumerate(SEGS):
                    for side, (sl, o) in enumerate(((slice(at, at + 8), lo), (slice(at + m - 8, at + m), lo + m - 8))):
                        own.settle()
                        own.did(dve.tensor_tensor(dst[:, 0:8], src[:, sl], edge[:, g, 2 * e + side, :], ALU.mult))
                        own.settle()
                        last = dve.tensor_tensor(y1[:, g, o:o + 8], dst[:, 0:8], z[:, sl], ALU.subtract)
                        if e and side:
                            last.then_inc(pooled_ready, 1)
                            dve.wait_ge(pooled_ready, g + 1)
                        else:
                            own.did(last)

            def merge(name):
                _, r0, _, m0, _ = MERGES[name]

                def turn(i, first):
                    for s in range(2):
                        dm = merged[:, ds(2 * i + s, 1), :].rearrange("p a n -> p (a n)")
                        done = r0 // 2 + 2 * i + s + 1
                        dve.wait_ge(result_used[0], done)
                        dve.wait_ge(result_done[1], done)
                        if name == "A":
                            dve.tensor_tensor(dm, gate_sb, res[1], ALU.mult).then_inc(result_used[1], 1)
                            continue
                        if not (first and s == 0 and m0 == 8):
                            dve.wait_ge(merge_added, m0 - 8 + 2 * i + s)
                        dve.tensor_tensor(prod, gate_sb, res[1], ALU.mult).then_inc(result_used[1], 1)
                        dve.wait_ge(result_used[1], done)
                        dve.tensor_tensor(dm, dm, prod, ALU.add).then_inc(merge_added, 1)

                turn(0, True)
                with dve.Fori(1, 4) as i:
                    turn(i, False)

            merge("A")
            own.did(dve.memset(z_conv, 0.0))
            for j in range(4):
                rc, rx, rb = (R_D + 3 * j + m for m in range(3))
                dve.wait_ge(result_used[rc % 2], rc // 2 + 1)
                dve.wait_ge(result_done[rx % 2], rx // 2 + 1)
                own.settle()
                for e, (at, lo, m) in enumerate(CSEGS):
                    last = dve.tensor_tensor(z_conv[:, at:at + m], cg_sb[:, lo:lo + m], res[rx % 2][:, lo:lo + m], ALU.mult)
                    if e:
                        last.then_inc(result_used[rx % 2], 1)
                    else:
                        own.did(last)
                dve.wait_ge(result_used[rx % 2], rx // 2 + 1)
                own.settle()
                n = T + 4
                tap = [colT[:, 64 + 4 * q + j:65 + 4 * q + j] for q in range(3)]
                own.did(dve.tensor_scalar(taps[:, 1:n - 1], z_conv[:, 0:n - 2], tap[0], None, ALU.mult))
                for q in (1, 2):
                    own.settle()
                    own.did(dve.scalar_tensor_tensor(out=taps[:, 1:n - 1], in0=z_conv[:, q:n - 2 + q], scalar=tap[q],
                                                     in1=taps[:, 1:n - 1], op0=ALU.mult, op1=ALU.add))
                dve.wait_ge(result_done[rb % 2], rb // 2 + 1)
                own.settle()
                for e, (at, lo, m) in enumerate(CSEGS):
                    last = dve.tensor_tensor(y0[:, j, lo:lo + m], taps[:, at:at + m], res[rb % 2][:, lo:lo + m], ALU.mult)
                    if e:
                        last.then_inc(result_used[rb % 2], 1)
                    else:
                        own.did(last)
                dve.wait_ge(result_used[rb % 2], rb // 2 + 1)
            merge("B")
            merge("D")

            def attend(t, keys, first=False, last=False):
                n = N_Q * t

                def row_max(h):
                    u = h % 2
                    dve.wait_ge(scores_done, n + h + 1)
                    own.did(dve.tensor_reduce(small[:, 4 + u:5 + u], score_ps[u][:, 0:keys], AX.X, ALU.max))
                    own.settle()
                    dve.tensor_scalar(small[:, u:u + 1], small[:, 4 + u:5 + u], -HD ** -0.5, None, ALU.mult).then_inc(score_max_ready, 1)

                def head_out(h):
                    u, k = h % 4, h % N_Q
                    own.did(dve.reciprocal(small[:, 36 + u:37 + u], sums[:, u:u + 1]))
                    own.settle()
                    dve.wait_ge(weighted_done, n + h + 1)
                    if h in (2, 4) and keys == T_PROMPT:
                        dve.wait_ge(mod2_parts_done, 2 * t + h // 2)
                        dve.tensor_copy(part2_sb, part2_ps).then_inc(mod2_parts_copied, 1)
                    if h == 0 and not (isinstance(t, int) and t == 0):
                        dve.wait_ge(heads_turned, t)
                    dve.tensor_scalar(o_row[:, HD * k:HD * k + HD], o_ps[h % 2], small[:, 36 + u:37 + u], None, ALU.mult).then_inc(head_out_ready, 1)

                def tile_out(i):
                    dve.wait_ge(heads_turned, i + 1)
                    dve.tensor_copy(y1[:, :, ds(i * P, P)], oT_ps).then_inc(heads_copied, 1)

                if first:
                    row_max(0)
                for h in range(N_Q):
                    if h + 1 < N_Q or not last:
                        row_max(h + 1)
                    if h == 1 and not first:
                        tile_out(t - 1)
                    if h or not first:
                        head_out(h - 1)
                if last:
                    head_out(N_Q - 1)
                    tile_out(t)

            dve.wait_ge(merge_added, 16)
            own.per_tile = 2 * N_Q
            all_tiles(dve, attend, own)
            dve.wait_ge(mod2_summed, 16)
            own.did(dve.tensor_tensor(mod2T[:, :, :], mod2_ps, colT[:, 32:64].unsqueeze(1).to_broadcast([P, 2, 32]), ALU.add))
            own.settle()
            dve.tensor_scalar(mod2T[:, :, 16:24], mod2T[:, :, 16:24], 1.0, None, ALU.add).then_inc(mod2_by_feature, 1)
            merge("C")

            bn2 = aff_t2[:, 0:12]

            def stats(src, cols, done):
                for j in range(2):
                    own.did(dve.bn_stats(bn2[:, 6 * j:6 * j + 6], src[:, 512 * j:512 * j + 512]))
                own.settle()
                own.did(dve.tensor_copy(carry[:, 0:1], half[:, 0:1]))
                own.did(dve.bn_aggr(cols[:, 0:2], bn2))
                own.settle()
                dve.tensor_scalar(cols[:, 7:8], cols[:, 1:2], LN_EPS, None, ALU.add).then_inc(done, 1)

            def centre(dst, src, cols, gain):
                own.did(dve.scalar_tensor_tensor(out=dst, in0=src, scalar=cols[:, 0:1], in1=gain,
                                                 op0=ALU.subtract, op1=ALU.mult))
                own.settle()

            def spread(dst, cols, offset, done):
                dve.scalar_tensor_tensor(out=dst, in0=dst, scalar=cols[:, 7:8], in1=offset,
                                         op0=ALU.mult, op1=ALU.add).then_inc(done, 1)

            def soft1(s, t):
                lg = aff_t[:, s, 0, :]
                dve.wait_ge(logits_done, t + 1)
                own.did(dve.tensor_tensor(lg, logit_ps, rb_b[:, :], ALU.add))
                own.settle()
                own.did(dve.tensor_reduce(small[:, 4 + s:5 + s], lg, AX.X, ALU.max))
                own.settle()
                dve.tensor_scalar(small[:, 2 * s:2 * s + 1], small[:, 4 + s:5 + s], -1.0, None, ALU.mult).then_inc(logit_max_ready, 1)

            def soft2(s, t):
                dve.wait_ge(route_exp_done, t + 1)
                own.did(dve.reciprocal(small[:, 6 + s:7 + s], small[:, 2 * s + 1:2 * s + 2]))
                own.settle()
                if not (isinstance(t, int) and t < 2):
                    dve.wait_ge(affinity_turned, t - 1)
                dve.tensor_scalar(aff3[:, s, :].rearrange("p (a n) -> p a n", n=32)[:, :, 0:NE],
                                  aff_t[:, s, 1:2, :].to_broadcast([P, 3, NE]), small[:, 6 + s:7 + s], None, ALU.mult).then_inc(affinity_ready, 1)

            def rows_turn(i, grp, first=False):
                for s in range(2):
                    t = 2 * i + s
                    c1, c2 = ln_cols(1, s), ln_cols(2, s)
                    dve.wait_ge(w_o_product_done, t + 1)
                    if not first:
                        dve.wait_ge(x1_scaled, t - 1)
                    dve.tensor_tensor(x1_row[s], y_ps[s], g1_b[grp], ALU.mult).then_inc(y_gated, 1)
                    dve.wait_ge(y_gated, t + 1)
                    dve.wait_ge(x_row_in[s], 16 * i + 16)
                    dve.scalar_tensor_tensor(out=x1_row[s], in0=x_row[s], scalar=ALPHA, in1=x1_row[s],
                                             op0=ALU.mult, op1=ALU.add).then_inc(x_added, 1)
                    dve.wait_ge(x_added, t + 1)
                    stats(x1_row[s], c1, var2_ready)
                    centre(x1_row[s], x1_row[s], c1, ln1g_b)
                    if not first:
                        soft1(s, t - 2)
                    dve.wait_ge(rstd2_ready, 2 * t + 1)
                    spread(x1_row[s], c1, ln1b_b, x1_ready)
                    dve.wait_ge(x1_ready, t + 1)
                    stats(x1_row[s], c2, var2_ready)
                    if not first:
                        soft2(s, t - 2)
                        dve.wait_ge(h2_row_stored[s], 16 * i)
                        dve.wait_ge(h2_turned, t - 1)
                    centre(h2_row[s], x1_row[s], c2, sc2_b[grp])
                    dve.wait_ge(rstd2_ready, 2 * t + 2)
                    spread(h2_row[s], c2, sh2_b[grp], h2_ready)

            own.did(dve.memset(aff3[:, :, :], 0.0))
            dve.wait_ge(merge_added, 24)
            dve.memset(affT, -1.0).then_inc(affT_filled, 1)
            own.settle()
            dve.wait_ge(row_constants_in, 16 * 8)
            rows_turn(0, 0, True)
            n = own.n
            rows_turn(1, 0)
            per = own.n - n
            with dve.Fori(2, PROMPT_PAIRS) as i:
                own.enter(i - 2, per)
                rows_turn(i, 0)
                own.leave(PROMPT_PAIRS - 2)
            rows_turn(PROMPT_PAIRS, 1)
            for s in range(2):
                soft1(s, TILES - 2 + s)
                soft2(s, TILES - 2 + s)

            dve.wait_ge(affinity_copied, TILES)
            for r in range(0, CAP_P, 8):
                own.settle()
                own.did(dve.max(out=top_v[:, r:r + 8], in_=affT))
                own.settle()
                own.did(dve.max_index(out=top_i[:, r:r + 8], in_max=top_v[:, r:r + 8], in_values=affT))
                own.settle()
                if r + 8 < CAP_P:
                    own.did(dve.match_replace(out=affT, in_to_replace=top_v[:, r:r + 8], in_values=affT, imm_value=-1.0))
            own.did(dve.tensor_copy(top_f, top_i[:, :]))
            own.settle()
            for g in range(1, 3):
                last = dve.tensor_scalar(top_f[32 * g:32 * g + NE, :], top_f[32 * g:32 * g + NE, :], float(g * HALF), None, ALU.add)
                if g == 1:
                    own.did(last)
            last.then_inc(top_found, 1)
            dve.wait_ge(top_turned, 1)
            dve.tensor_copy(top_ranks, top_ps).then_inc(top_copied, 1)
            dve.wait_ge(half2_reversed, 1)
            dve.wait_ge(top_copied, 1)
            own.did(dve.tensor_tensor(first_wins, top_ranks[:, 0, 0:NE], flip_ps[:, 0, :], ALU.is_ge))
            own.did(dve.tensor_tensor(index_gap, top_ranks[:, 1, 0:NE], flip_ps[:, 1, :], ALU.subtract))
            dve.tensor_tensor(gate_p[:, :], top_ranks[:, 0, 0:NE], flip_ps[:, 0, :], ALU.max).then_inc(choice_ready, 1)
            dve.tensor_copy(gate_s[:, :], top_ranks[0:CAP_S, 0, 64:64 + NE]).then_inc(choice_ready, 1)
            dve.tensor_copy(idx_s[:, :], top_ranks[0:CAP_S, 1, 64:64 + NE]).then_inc(choice_ready, 1)
            own.settle()
            own.did(dve.tensor_tensor(index_gap, index_gap, first_wins, ALU.mult))
            own.settle()
            dve.tensor_tensor(idx_p[:, :], index_gap, flip_ps[:, 1, :], ALU.add).then_inc(choice_ready, 1)

            def expert(e, more):
                for j in range(KD):
                    dve.wait_ge(silu_done, 8 * e + j + 1)
                    dve.tensor_tensor(gT[:, j, :], silu[j % 2], ab_ps[j % 2][:, 1, :], ALU.mult).then_inc(gT_ready, 1)
                for j in range(KD):
                    dve.wait_ge(w2_product_done, 8 * e + j + 1)
                    own.did(dve.tensor_scalar(outT[:, j, 0:CAP_P], ab_ps[j % 2][:, 0, 0:CAP_P], mod2T[:, 0, 24 + j:25 + j], None, ALU.mult))
                    own.settle()
                    dve.tensor_scalar(outT[:, j, CAP_P:CAP], ab_ps[j % 2][:, 0, CAP_P:CAP], mod2T[:, 1, 24 + j:25 + j], None, ALU.mult).then_inc(outT_copied, 1)
                if more:
                    dve.wait_ge(xg_s_turned, e + 2)
                    dve.tensor_copy(xgT[:, :, CAP_P:CAP], xt_s).then_inc(xgT_s_copied, 1)
                dve.wait_ge(out_turned, e + 1)
                if not (isinstance(e, int) and e == 0):
                    dve.wait_ge(out_added, 32 * e)
                for h in range(2):
                    last = dve.tensor_scalar(out_s[:, 512 * h:512 * h + 512], os_ps[h], gate_s[:, ds(e, 1)], None, ALU.mult)
                last.then_inc(out_s_ready, 1)

            dve.wait_ge(choice_ready, 4)
            dve.wait_ge(xg_s_turned, 1)
            dve.tensor_copy(xgT[:, :, CAP_P:CAP], xt_s).then_inc(xgT_s_copied, 1)
            expert(0, True)
            with dve.Fori(1, NE - 1) as e:
                own.enter(e - 1, KD)
                expert(e, True)
                own.leave(NE - 2)
            expert(NE - 1, False)

            dve.wait_ge(ln2_in, 32)
            for t in range(TILES):
                c1 = ln_cols(1, t % 2)
                dve.wait_ge(y_tile_in[t % LAST], 16 * (t // LAST) + 16)
                if t >= 2:
                    dve.wait_ge(y_spread, t - 1)
                stats(y_in[t % LAST], c1, var3_ready)
                if t >= LAST:
                    dve.wait_ge(out_stored[t % LAST], 16)
                dve.scalar_tensor_tensor(out=y_out[t % LAST], in0=y_in[t % LAST], scalar=c1[:, 0:1], in1=ln2g_b,
                                         op0=ALU.subtract, op1=ALU.mult).then_inc(y_centred, 1)

        @block.tensor
        def _(pe):
            pe.wait_ge(ident_ready, 1)
            pe.wait_ge(silu_c_done, 1)
            pe.wait_ge(setup_rows_in, 64)
            pe.transpose(rows_ps, rows_in[0:80, :], ident[0:80, 0:80]).then_inc(setup_rows_turned, 1)
            pe.wait_ge(columns_ready, 1)
            def partial(dst, w):
                for k in range(KD):
                    g = 32 * (k % 4)
                    last = pe.matmul(dst[g:g + 32, :], c_pad[:, k, :], w[:, k, :], start=k < 4, stop=k >= 4)
                return last

            def summed(dst, part):
                for j in range(part.shape[1] // P):
                    last = pe.matmul(dst(j), part[:, j * P:(j + 1) * P], every32[:, 0:2], start=True, stop=True)
                return last

            pe.wait_ge(mod_ready_to_multiply, 1)
            for m in range(5):
                if m < 4:
                    pe.wait_ge(w_ada_in[m], 16)
                    if m >= 2:
                        pe.wait_ge(mod_parts_copied, m - 1)
                    partial(part_ps[m % 2], w_ada_buf[m]).then_inc(mod_parts_done, 1)
                if m:
                    pe.wait_ge(mod_parts_copied, m)
                    summed(lambda j: mod_ps[:, 4 * (m - 1) + j, :], part_sb[(m - 1) % 2]).then_inc(mod_summed, 1)
            pe.wait_ge(ws_in_sem, 16)
            for g in range(4):
                last = pe.transpose(ws_ps[:, g, :], ws_in[:, g, :], ident[:, :])
            last.then_inc(ws_turned, 1)

            def turn_x_rows(i, s):
                t = 2 * i + s
                pe.wait_ge(xh_ready, t + 1)
                if not (isinstance(i, int) and i < 2):
                    pe.wait_ge(qk_copied, t - 3)
                for k in range(KD):
                    last = pe.transpose(tp[s][:, k, :], xh[s][:, k * P:(k + 1) * P], ident[:, :])
                last.then_inc(xh_turned, 1)

            def turn_qk(i, s, more=True):
                t = 2 * i + s
                pe.wait_ge(qk_rotated, t + 1)
                if more:
                    pe.wait_ge(h_tile_ready, t + 3)
                for k in range(6):
                    last = pe.transpose(tp[s][:, k, :], qk_out[s][:, k * P:(k + 1) * P], ident[:, :])
                last.then_inc(qk_turned, 1)

            def turn(i, more=True):
                first = isinstance(i, int) and i == 0
                for s in range(2):
                    t = 2 * i + s
                    zero = first and s == 0
                    pe.wait_ge(h_tile_ready, t + 1)
                    for dst, lo, n, done, freed, cnt in ((z1, 0, 512, z1_done, z_copied, 2 * t - 1), (z2, 512, 256, z2_done, z_copied, 2 * t),
                                                         (z3, 768, 512, z3_done, v_gelu_ready, t)):
                        if not zero:
                            pe.wait_ge(freed, cnt)
                        elif dst is z3:
                            pe.wait_ge(wz_in[1], 16)
                        for k in range(KD):
                            last = pe.matmul(dst, h_tile[s][:, k, :], wz[:, k, lo:lo + n], start=k == 0, stop=k == KD - 1)
                        last.then_inc(done, 1)
                        if s == 0 and not first and dst is not z2:
                            turn_qk(i - 1, 0 if dst is z1 else 1)
                        if s == 1 and more and dst is not z1:
                            turn_x_rows(i + 1, 0 if dst is z2 else 1)

            for s in range(2):
                turn_x_rows(0, s)
            pe.wait_ge(wz_in[0], 16)
            pe.wait_ge(mod_ready, 1)
            pe.wait_ge(ws_turned, 2)
            turn(0)
            with pe.Fori(1, PAIRS - 1) as i:
                turn(i)
            turn(PAIRS - 1, False)
            for s in range(2):
                turn_qk(PAIRS - 1, s, False)

            def product(par, freed, w, count, k_tiles, rhs):
                if freed is not None:
                    pe.wait_ge(result_used[par], freed)
                pe.wait_ge(w[1], count)
                for lo, n in BLOCKS:
                    for k in range(k_tiles):
                        last = pe.matmul(res[par][:, lo:lo + n], w[0][:, k, :], rhs[:, k, lo:lo + n],
                                         start=k == 0, stop=k == k_tiles - 1)
                last.then_inc(result_done[par], 1)

            def wt(s):
                return w_tile[s], w_tile_in[s]

            pe.wait_ge(qk_copied, TILES)
            pe.wait_ge(z_copied, 2 * TILES)
            pe.wait_ge(v_gelu_ready, TILES)
            pe.wait_ge(h_joined, TILES)
            for s in range(2):
                product(s, None, wt(s), 16, KD, hT)
            with pe.Fori(1, 2) as i:
                for s in range(2):
                    product(s, i, wt(s), 16 * i + 16, KD, hT)
            pe.wait_ge(v_ready, TILES)
            for t in range(TILES):
                if t >= 2:
                    pe.wait_ge(spatial_used, t - 1)
                for g in range(4):
                    last = pe.matmul(sv_ps[t % 2][:, g, :], vln[:, t, g * P:(g + 1) * P], wsT[:, g, :], start=True, stop=True)
                last.then_inc(spatial_done, 1)
            with pe.Fori(2, 4) as i:
                for s in range(2):
                    product(s, i, wt(s), 16 * i + 16, KD, hT)

            def merge(name):
                n0, r0, _, m0, y = MERGES[name]
                with pe.Fori(0, 4) as i:
                    for s in range(2):
                        product(0, r0 // 2 + 2 * i + s, wt(s), 8 * n0 + 16 * i + 16, KD, hT)
                        product(1, r0 // 2 + 2 * i + s, (p_tile[s], p_tile_in[s]), 8 * m0 + 16 * i + 16, KB, y)

            pe.wait_ge(ya_ready, TILES)
            merge("A")
            pe.wait_ge(wg_in, 16)
            pe.wait_ge(pooled_ready, 4)
            for g in range(4):
                r = R_MIX + g
                pe.wait_ge(result_used[r % 2], r // 2)
                for lo, n in BLOCKS:
                    last = pe.matmul(res[r % 2][:, lo:lo + n], wg_sb[:, g, :], y1[:, g, lo:lo + n], start=True, stop=True)
                last.then_inc(result_done[r % 2], 1)
            with pe.Fori(0, 2) as i:
                for m in range(6):
                    product(m % 2, R_D // 2 + 3 * i + m // 2, wt(m % 2), 8 * N_D + 48 * i + 16 * (m // 2) + 16, KD, hT)
            pe.wait_ge(result_used[0], R_D // 2)
            pe.wait_ge(result_used[1], R_D // 2)
            merge("B")
            pe.wait_ge(result_used[1], R_MB // 2)
            merge("D")

            def modulation(i, h):
                if h >= 4:
                    pe.wait_ge(mod2_parts_copied, 2 * i + h // 2 - 1)
                    a = h // 2 - 2
                    summed(lambda j: mod2_ps[:, :, ds(4 * i + 2 * a + j, 1)].rearrange("p g a -> p (g a)"), part2_sb) \
                        .then_inc(mod2_summed, 1)
                if h <= 4:
                    a = h // 2 - 1
                    pe.wait_ge(mod2_weights_in[a], 16 * i + 16)
                    partial(part2_ps, w_mod[a]).then_inc(mod2_parts_done, 1)

            def attend(t, keys, first=False, last=False):
                n = N_Q * t

                def scores(h):
                    k = h % N_Q
                    lo = HD * (k % 2)
                    if k % 2 == 0:
                        pe.wait_ge(q_tile_copied, 4 * t + h // 2 + 1)
                    if not (isinstance(t, int) and t == 0 and h < 2):
                        pe.wait_ge(exp_done, n + h - 1)
                    for at in range(0, keys, 512):
                        m = min(512, keys)
                        k0 = 0 if keys == T_PROMPT else T_PROMPT
                        end = pe.matmul(score_ps[k % 2][:, at:at + m], q_tile[lo:lo + HD, k // 2, :],
                                        kT[lo:lo + HD, k // 4, k0 + at:k0 + at + m], start=True, stop=True)
                    end.then_inc(scores_done, 1)

                def weighted(h):
                    k = h % N_Q
                    pe.wait_ge(probT_copied, n + h + 1)
                    if not (isinstance(t, int) and t == 0 and h < 2):
                        pe.wait_ge(head_out_ready, n + h - 1)
                    if h == 1 and not (isinstance(t, int) and t == 0):
                        pe.wait_ge(heads_copied, t)
                    if h in (2, 4, 6) and keys == T_PROMPT:
                        modulation(t, h)
                    t0 = 0 if keys == T_PROMPT else T_PROMPT // P
                    for b in range(keys // P):
                        end = pe.matmul(o_ps[k % 2], probT[k % 2][:, b, :], va[:, t0 + b, (k // 4) * HD:(k // 4 + 1) * HD],
                                        start=b == 0, stop=b == keys // P - 1)
                    end.then_inc(weighted_done, 1)

                def turn_out(i):
                    pe.wait_ge(head_out_ready, N_Q * i + N_Q)
                    if not (isinstance(i, int) and i == 0):
                        pe.wait_ge(heads_copied, i)
                    for j in range(4):
                        end = pe.transpose(oT_ps[:, j, :], o_row[:, j * P:(j + 1) * P], ident[:, :])
                    end.then_inc(heads_turned, 1)

                if first:
                    scores(0)
                for h in range(N_Q):
                    if h + 1 < N_Q or not last:
                        scores(h + 1)
                    if h == 1 and not first:
                        turn_out(t - 1)
                    pe.wait_ge(exp_done, n + h + 1)
                    if not (isinstance(t, int) and t == 0 and h == 0):
                        pe.wait_ge(probT_copied, n + h)
                    for b in range(keys // P):
                        end = pe.transpose(pt_ps[:, b, :], prob[h % 2][:, b * P:(b + 1) * P], ident[:, :])
                    end.then_inc(prob_turned, 1)
                    if h or not first:
                        weighted(h - 1)
                if last:
                    weighted(N_Q - 1)
                    turn_out(t)

            for s in range(2):
                pe.wait_ge(result_used[s], R_MC // 2)
            pe.wait_ge(spatial_used, TILES)
            all_tiles(pe, attend)
            pe.wait_ge(mod2_by_feature, 1)
            pe.transpose(modr_ps, mod2T[:, :, :].rearrange("p g c -> p (g c)"), ident[:, :]).then_inc(mod2_rows_turned, 1)
            pe.wait_ge(exp_done, N_Q * TILES)
            pe.wait_ge(probT_copied, N_Q * TILES)
            pe.wait_ge(heads_copied, TILES)
            merge("C")

            for s in range(2):
                pe.wait_ge(result_used[s], R_END // 2)
            pe.wait_ge(mod2_rows_copied, 1)

            def rows_out(i, s, between=None):
                t = 2 * i + s
                if isinstance(i, int) and t == 0:
                    pe.wait_ge(first_merged_tile_taken, 1)
                else:
                    pe.wait_ge(merged_tile_taken, t)
                if not (isinstance(i, int) and i == 0):
                    pe.wait_ge(y_gated, t - 1)
                for h in range(2):
                    for k in range(KD):
                        last = pe.matmul(y_ps[s][:, 512 * h:512 * h + 512], m_tile[s][:, k, :], wo_sb[:, k, 512 * h:512 * h + 512],
                                         start=k == 0, stop=k == KD - 1)
                    if h == 0 and between:
                        between()
                last.then_inc(w_o_product_done, 1)

            def turn_h(s, t):
                pe.wait_ge(h2_ready, t + 1)
                if not (isinstance(t, int) and t == 0):
                    pe.wait_ge(h2T_copied, t)
                for k in range(KD):
                    last = pe.transpose(h2t_ps[:, k, :], h2_row[s][:, k * P:(k + 1) * P], ident[:, :])
                last.then_inc(h2_turned, 1)

            def logits_part(s, t):
                pe.wait_ge(h2T_copied, t + 1)
                if not (isinstance(t, int) and t == 0):
                    pe.wait_ge(logit_max_ready, t)
                for k in range(KD):
                    g = 32 * (k % 4)
                    last = pe.matmul(lpart_ps[g:g + 32, :], rw_sb[:, k, :], h2T[s][:, k, :], start=k < 4, stop=k >= 4)
                last.then_inc(logit_parts_done, 1)

            def logits(t):
                pe.wait_ge(logit_parts_copied, t + 1)
                pe.matmul(logit_ps, lpart_sb, every32[:, :], start=True, stop=True).then_inc(logits_done, 1)

            def turn_aff(s, t):
                pe.wait_ge(affinity_ready, t + 1)
                if not (isinstance(t, int) and t == 0):
                    pe.wait_ge(affinity_copied, t)
                pe.transpose(affT_ps, aff3[:, s, :], ident[:, :]).then_inc(affinity_turned, 1)

            pe.wait_ge(w_o_in, 32)
            for s in range(2):
                rows_out(0, s)
            for s in range(2):
                turn_h(s, s)
                rows_out(1, s, lambda: logits_part(s, s))
                if s:
                    turn_aff(0, 0)
                logits(s)
            with pe.Fori(2, PAIRS) as i:
                for s in range(2):
                    turn_h(s, 2 * i + s - 2)
                    rows_out(i, s, lambda: logits_part(s, 2 * i + s - 2))
                    turn_aff(1 - s, 2 * i + s - 3)
                    logits(2 * i + s - 2)
            for s in range(2):
                turn_h(s, TILES - 2 + s)
                logits_part(s, TILES - 2 + s)
                turn_aff(1 - s, TILES - 3 + s)
                logits(TILES - 2 + s)
            turn_aff(1, TILES - 1)

            pe.wait_ge(top_found, 1)
            pe.wait_ge(affinity_copied, TILES)
            pe.transpose(top_ps[:, 0, :], top_v, ident[0:TK, 0:TK])
            pe.transpose(top_ps[:, 1, :], top_f, ident[0:TK, 0:TK]).then_inc(top_turned, 1)
            pe.wait_ge(ident_ready, 2)
            pe.wait_ge(top_copied, 1)
            pe.matmul(flip_ps, flip, top_ranks[:, :, 32:32 + NE], start=True, stop=True).then_inc(half2_reversed, 1)

            def turn_xp(e):
                pe.wait_ge(rows_gathered, 32 * e + 32)
                for k in range(KD):
                    last = pe.transpose(xt_p[:, k, :], xg_p[:, k * P:(k + 1) * P], ident[:, :])
                last.then_inc(xg_p_turned, 1)

            def turn_xs(e, first=False):
                if not first:
                    pe.wait_ge(choice_ready, 4)
                    pe.wait_ge(out_s_ready, e - 1)
                for k in range(KD):
                    last = pe.transpose(xt_s[:, k, :], xg_s[:, k * P:(k + 1) * P], ident[0:CAP_S, 0:CAP_S])
                last.then_inc(xg_s_turned, 1)

            def expert(e, more, first=False):
                pe.wait_ge(xgT_p_copied, e + 1)
                pe.wait_ge(xgT_s_copied, e + 1)
                for j in range(KD):
                    if not (first and j < 2):
                        if j < 2:
                            pe.wait_ge(outT_copied, 8 * e - 1 + j)
                        else:
                            pe.wait_ge(gT_ready, 8 * e + j - 1)
                    for m in range(2):
                        c = 2 * (j // 4) + m
                        if j % 4 == 0:
                            pe.wait_ge(expert_half_in[c], 16 * e + 16)
                        for k in range(KD):
                            last = pe.matmul(ab_ps[j % 2][:, m, :], w_half[c][:, k, (j % 4) * P:(j % 4 + 1) * P], xgT[:, k, :],
                                             start=k == 0, stop=k == KD - 1)
                    last.then_inc(ab_done, 1)
                if more:
                    turn_xp(e + 1)
                for j in range(KD):
                    if j < 2:
                        pe.wait_ge(gT_ready, 8 * e + 7 + j)
                        if j == 0:
                            pe.wait_ge(gT_ready, 8 * e + 8)
                    else:
                        pe.wait_ge(outT_copied, 8 * e + j - 1)
                    if j % 4 == 0:
                        pe.wait_ge(expert_half_in[4 + j // 4], 16 * e + 16)
                    for k in range(KD):
                        last = pe.matmul(ab_ps[j % 2][:, 0, :], w_half[4 + j // 4][:, k, (j % 4) * P:(j % 4 + 1) * P], gT[:, k, :],
                                         start=k == 0, stop=k == KD - 1)
                    last.then_inc(w2_product_done, 1)
                if more:
                    turn_xs(e + 1, first)
                pe.wait_ge(outT_copied, 8 * e + 8)
                if not first:
                    pe.wait_ge(out_p_ready, e)
                    pe.wait_ge(out_s_ready, e)
                for j in range(KD):
                    pe.transpose(op_ps[:, j * P:(j + 1) * P], outT[:, j, 0:CAP_P], ident[:, :])
                if more:
                    pe.wait_ge(xgT_s_copied, e + 2)
                for j in range(KD):
                    last = pe.transpose(os_ps[j // 4][:, (j % 4) * P:(j % 4 + 1) * P], outT[:, j, CAP_P:CAP], ident[:, :])
                last.then_inc(out_turned, 1)

            pe.wait_ge(choice_ready, 4)
            turn_xp(0)
            turn_xs(0, True)
            expert(0, True, True)
            with pe.Fori(1, NE - 1) as e:
                expert(e, True)
            expert(NE - 1, False)


_NAMES = ("w_ada", "b_ada", "w_in", "a_ln_g", "a_ln_b", "a_ws", "a_bs", "b_wg", "b_scale", "c_q_g", "c_k_g", "d_conv")
_NAMES_2 = ("w_o", "ln1_g", "ln1_b", "r_w", "r_b", "e_w1", "e_w3", "e_w2", "ln2_g", "ln2_b")


def rope_table():
    inv = (np.float32(10000.0) ** (-np.arange(16, dtype=np.float32) / np.float32(16))).astype(np.float32)
    tables = []
    for n in (T_PROMPT, T_SAMPLE):
        row = np.repeat(np.arange(n // 64, dtype=np.float32), 64)
        col = np.tile(np.arange(64, dtype=np.float32), n // 64)
        angle = np.concatenate([row[:, None] * inv, col[:, None] * inv], axis=-1)
        tables.append(np.stack([np.cos(angle), np.sin(angle)], axis=1))
    table = np.concatenate(tables).astype(np.float32).reshape(TILES, P, 2, 32)
    return np.ascontiguousarray(table.transpose(1, 0, 2, 3))


def edge_counts():
    rows = []
    for w in WINDOWS:
        for n in (T_PROMPT, T_SAMPLE):
            t = np.arange(n)
            count = np.clip(t + w // 2, 0, n) - np.clip(t - w // 2, 0, n)
            rows += [count[:8], count[-8:]]
    return (np.float32(1) / np.stack(rows).astype(np.float32)).reshape(len(WINDOWS), 4, 8)


def kernel(**inputs):
    import concourse.bacc as _bacc
    from concourse.bass_utils import run_bass_kernel_spmd as _run

    given = {k: np.asarray(v) for k, v in inputs.items()}
    arrays = {
        "x": np.concatenate([given["x_prompt"][0], given["x_sample"][0]]),
        "c": np.concatenate([given["c_prompt"], given["c_sample"]]),
    }
    for name in _NAMES:
        arrays[name] = given[name][0]
    arrays["p_all"] = np.stack([given[f"p_{b}"][0] for b in "abcd"])
    for name in _NAMES_2:
        arrays[name] = given[name][0]
    arrays["rope"] = rope_table()
    arrays["inv_count"] = edge_counts()
    arrays = {f"in_{k}_dram": np.ascontiguousarray(v) for k, v in arrays.items()}

    nc = _bacc.Bacc("TRN2", target_bir_lowering=False, num_devices=1)
    args = [nc.dram_tensor(k, a.shape, mybir.dt.from_np(a.dtype), kind="ExternalInput").ap() for k, a in arrays.items()]
    out = nc.dram_tensor("out_0_dram", (T, D), F32, kind="ExternalOutput").ap()
    build(nc, *args, out)
    rows = _run(nc, [arrays], core_ids=[0]).results[0]["out_0_dram"]
    return rows[:T_PROMPT].reshape(1, T_PROMPT, D), rows[T_PROMPT:].reshape(1, T_SAMPLE, D)
```
